# Optimizing a Trainium2 kernel written in Bass

```python
import math
import jax, jax.numpy as jnp
from jax import lax
import numpy as np

D_MODEL = 1024
BATCH = 1
SEQ = 512
DEPTH = 1

HEAD_DIM = 64
N_DIFF_HEADS = 4
DIFF_V_DIM = 2 * HEAD_DIM
DIFF_QK_WIDTH = N_DIFF_HEADS * 2 * HEAD_DIM
DIFF_WIDTH = N_DIFF_HEADS * DIFF_V_DIM
N_FOX_HEADS = 8
FOX_WIDTH = N_FOX_HEADS * HEAD_DIM
MIX_WIDTH = DIFF_WIDTH + FOX_WIDTH
IN_PROJ_WIDTH = 2 * DIFF_QK_WIDTH + DIFF_WIDTH + 3 * FOX_WIDTH + N_FOX_HEADS
SPLIT_POINTS = (DIFF_QK_WIDTH, 2 * DIFF_QK_WIDTH, 2 * DIFF_QK_WIDTH + DIFF_WIDTH,
                2 * DIFF_QK_WIDTH + DIFF_WIDTH + FOX_WIDTH,
                2 * DIFF_QK_WIDTH + DIFF_WIDTH + 2 * FOX_WIDTH,
                2 * DIFF_QK_WIDTH + DIFF_WIDTH + 3 * FOX_WIDTH)
Q_BLOCK = 128
N_BUCKETS = 32
MAX_DISTANCE = 128
PEER_HEADS = 8
PEER_QUERY_DIM = 256
PEER_HALF_DIM = PEER_QUERY_DIM // 2
PEER_N_KEYS = 128
PEER_N_EXPERTS = PEER_N_KEYS * PEER_N_KEYS
PEER_TOPK = 16
PEER_CHUNK = 128
EPS = 1e-6
NEG_INF = -1e30

kernel_name = "hymba_diff_fox_peer_block"

def rmsnorm(x, g):
    xf = x.astype(jnp.float32)
    xf = xf * lax.rsqrt(jnp.mean(xf * xf, axis=-1, keepdims=True) + EPS)
    return (xf * g.astype(jnp.float32)).astype(x.dtype)

def t5_bucket(dist):
    max_exact = N_BUCKETS // 2
    nf = jnp.maximum(dist, 1).astype(jnp.float32)
    large = max_exact + (jnp.log(nf / max_exact) / math.log(MAX_DISTANCE / max_exact)
                         * (N_BUCKETS - max_exact)).astype(jnp.int32)
    large = jnp.minimum(large, N_BUCKETS - 1)
    return jnp.where(dist < max_exact, dist, large)

def hybrid_mixer(h, w_in, b_f, lam_q1, lam_k1, lam_q2, lam_k2, g_subln, w_o, rel_bias, lambda_init):
    B, S, _ = h.shape
    proj = h @ w_in
    qd, kd, vd, qf, kf, vf, fl = jnp.split(proj, SPLIT_POINTS, axis=-1)
    qd = qd.reshape(B, S, N_DIFF_HEADS, 2, HEAD_DIM).transpose(0, 2, 3, 1, 4)
    kd = kd.reshape(B, S, N_DIFF_HEADS, 2, HEAD_DIM).transpose(0, 2, 3, 1, 4)
    vd = vd.reshape(B, S, N_DIFF_HEADS, DIFF_V_DIM).transpose(0, 2, 1, 3)
    qf = qf.reshape(B, S, N_FOX_HEADS, HEAD_DIM).transpose(0, 2, 1, 3)
    kf = kf.reshape(B, S, N_FOX_HEADS, HEAD_DIM).transpose(0, 2, 1, 3)
    vf = vf.reshape(B, S, N_FOX_HEADS, HEAD_DIM).transpose(0, 2, 1, 3)
    log_f = jax.nn.log_sigmoid((fl + b_f).astype(jnp.float32))
    cum = jnp.cumsum(log_f, axis=1).transpose(0, 2, 1)
    lam = (jnp.exp(jnp.sum(lam_q1.astype(jnp.float32) * lam_k1.astype(jnp.float32)))
           - jnp.exp(jnp.sum(lam_q2.astype(jnp.float32) * lam_k2.astype(jnp.float32)))
           + lambda_init)
    scale = HEAD_DIM ** -0.5
    k_pos = jnp.arange(S, dtype=jnp.int32)
    n_blocks = S // Q_BLOCK

    def block(i):
        t0 = i * Q_BLOCK
        q_pos = t0 + jnp.arange(Q_BLOCK, dtype=jnp.int32)
        dist = q_pos[:, None] - k_pos[None, :]
        causal = dist >= 0
        bias = jnp.moveaxis(rel_bias[t5_bucket(jnp.maximum(dist, 0))], -1, 0)
        q_blk = lax.dynamic_slice_in_dim(qd, t0, Q_BLOCK, axis=3)
        s_d = (jnp.einsum('bhmqd,bhmkd->bhmqk', q_blk, kd).astype(jnp.float32) * scale
               + bias.astype(jnp.float32)[None, :, None])
        p = jax.nn.softmax(jnp.where(causal, s_d, NEG_INF), axis=-1)
        p_diff = p[:, :, 0] - lam * p[:, :, 1]
        o_d = jnp.einsum('bhqk,bhkd->bhqd', p_diff.astype(vd.dtype), vd)
        o_d = rmsnorm(o_d, g_subln) * (1.0 - lambda_init)
        qf_blk = lax.dynamic_slice_in_dim(qf, t0, Q_BLOCK, axis=2)
        cum_q = lax.dynamic_slice_in_dim(cum, t0, Q_BLOCK, axis=2)
        s_f = (jnp.einsum('bhqd,bhkd->bhqk', qf_blk, kf).astype(jnp.float32) * scale
               + cum_q[..., :, None] - cum[..., None, :])
        p_f = jax.nn.softmax(jnp.where(causal, s_f, NEG_INF), axis=-1)
        o_f = jnp.einsum('bhqk,bhkd->bhqd', p_f.astype(vf.dtype), vf)
        return o_d, o_f

    o_d, o_f = lax.map(block, jnp.arange(n_blocks, dtype=jnp.int32))
    o_d = o_d.transpose(1, 0, 3, 2, 4).reshape(B, S, DIFF_WIDTH)
    o_f = o_f.transpose(1, 0, 3, 2, 4).reshape(B, S, FOX_WIDTH)
    return jnp.concatenate([o_d, o_f], axis=-1) @ w_o

def peer_ffn(h, w_pq, sub_keys, peer_u, peer_v):
    B, S, D = h.shape
    T = B * S
    ht = h.reshape(T, D)
    q = (ht @ w_pq).reshape(T, PEER_HEADS, 2, PEER_HALF_DIM).astype(jnp.float32)
    s = jnp.einsum('thpd,pnd->thpn', q, sub_keys.astype(jnp.float32))
    sv, si = lax.top_k(s, PEER_TOPK)
    cand = sv[..., 0, :, None] + sv[..., 1, None, :]
    cand_id = si[..., 0, :, None] * PEER_N_KEYS + si[..., 1, None, :]
    cand = cand.reshape(T, PEER_HEADS, PEER_TOPK * PEER_TOPK)
    cand_id = cand_id.reshape(T, PEER_HEADS, PEER_TOPK * PEER_TOPK)
    top_s, top_pos = lax.top_k(cand, PEER_TOPK)
    ids = jnp.take_along_axis(cand_id, top_pos, axis=-1)
    g = jax.nn.softmax(top_s, axis=-1)
    nc = T // PEER_CHUNK

    def chunk(args):
        h_c, ids_c, g_c = args
        u = peer_u[ids_c]
        a = jax.nn.gelu(jnp.einsum('chkd,cd->chk', u, h_c).astype(jnp.float32))
        w = (g_c * a).astype(h_c.dtype)
        return jnp.einsum('chk,chkd->cd', w, peer_v[ids_c])

    out = lax.map(chunk, (ht.reshape(nc, PEER_CHUNK, D),
                          ids.reshape(nc, PEER_CHUNK, PEER_HEADS, PEER_TOPK),
                          g.reshape(nc, PEER_CHUNK, PEER_HEADS, PEER_TOPK)))
    return out.reshape(B, S, D)

def setup_inputs(seed: int = 0) -> dict:
    key = jax.random.key(seed)
    ks = jax.random.split(key, 24)
    D = D_MODEL
    nrm = lambda k, shape, s: jax.random.normal(k, shape, jnp.float32) * s
    gain = lambda k, shape: 1.0 + nrm(k, shape, 0.02)
    return {
        "x": nrm(ks[0], (BATCH, SEQ, D), 1.0),
        "c": nrm(ks[1], (BATCH, D), 1.0),
        "rel_bias": nrm(ks[2], (N_BUCKETS, N_DIFF_HEADS), 0.5),
        "w_ada": nrm(ks[3], (DEPTH, D, 6 * D), 0.5 * D ** -0.5),
        "b_ada": nrm(ks[4], (DEPTH, 6 * D), 0.02),
        "g_pre_mix": gain(ks[5], (DEPTH, D)),
        "g_post_mix": gain(ks[6], (DEPTH, D)),
        "w_in": nrm(ks[7], (DEPTH, D, IN_PROJ_WIDTH), D ** -0.5),
        "b_f": 1.0 + nrm(ks[8], (DEPTH, N_FOX_HEADS), 0.5),
        "lam_q1": nrm(ks[9], (DEPTH, HEAD_DIM), 0.1),
        "lam_k1": nrm(ks[10], (DEPTH, HEAD_DIM), 0.1),
        "lam_q2": nrm(ks[11], (DEPTH, HEAD_DIM), 0.1),
        "lam_k2": nrm(ks[12], (DEPTH, HEAD_DIM), 0.1),
        "g_subln": gain(ks[13], (DEPTH, DIFF_V_DIM)),
        "w_o": nrm(ks[14], (DEPTH, MIX_WIDTH, D), MIX_WIDTH ** -0.5),
        "g_pre_ffn": gain(ks[15], (DEPTH, D)),
        "g_post_ffn": gain(ks[16], (DEPTH, D)),
        "w_pq": nrm(ks[17], (DEPTH, D, PEER_HEADS * PEER_QUERY_DIM), D ** -0.5),
        "sub_keys": nrm(ks[18], (DEPTH, 2, PEER_N_KEYS, PEER_HALF_DIM), PEER_HALF_DIM ** -0.5),
        "peer_u": nrm(ks[19], (DEPTH, PEER_N_EXPERTS, D), D ** -0.5),
        "peer_v": nrm(ks[20], (DEPTH, PEER_N_EXPERTS, D), D ** -0.5),
    }

def reference(x, c, rel_bias, w_ada, b_ada, g_pre_mix, g_post_mix, w_in, b_f,
              lam_q1, lam_k1, lam_q2, lam_k2, g_subln, w_o, g_pre_ffn, g_post_ffn,
              w_pq, sub_keys, peer_u, peer_v):
    for l in range(DEPTH):
        lambda_init = 0.8 - 0.6 * math.exp(-0.3 * l)
        mod = jax.nn.silu(c) @ w_ada[l] + b_ada[l]
        sh1, sc1, gt1, sh2, sc2, gt2 = jnp.split(mod[:, None, :], 6, axis=-1)
        h = rmsnorm(x, g_pre_mix[l]) * (1.0 + sc1) + sh1
        y = hybrid_mixer(h, w_in[l], b_f[l], lam_q1[l], lam_k1[l], lam_q2[l], lam_k2[l],
                         g_subln[l], w_o[l], rel_bias, lambda_init)
        x = x + gt1 * rmsnorm(y, g_post_mix[l])
        h = rmsnorm(x, g_pre_ffn[l]) * (1.0 + sc2) + sh2
        y = peer_ffn(h, w_pq[l], sub_keys[l], peer_u[l], peer_v[l])
        x = x + gt2 * rmsnorm(y, g_post_ffn[l])
    return x


_drawn_inputs = setup_inputs


def setup_inputs(seed=0):
    import zlib

    import numpy as np

    out = dict(_drawn_inputs(seed))
    spreads = {}
    factors = {'lam_q1': 3.218, 'lam_k1': 5.74, 'g_post_ffn': 8.0}
    for name, (base, spread) in spreads.items():
        noise = np.random.default_rng([zlib.crc32(name.encode()), seed]).standard_normal(out[name].shape)
        drawn = base * np.exp(spread * noise) if base else spread * noise
        out[name] = __import__('jax').numpy.asarray(drawn.astype(out[name].dtype))
    for name, factor in factors.items():
        out[name] = (out[name] * factor).astype(out[name].dtype)
    return out
```

```python
import math
from contextlib import ExitStack

import numpy as np

import concourse.bass as bass
from concourse import mybir

P = 128
T = 512
D = 1024
TT = T // P
KD = D // P
SLOTS = 4
LEAD = 3
HEAD_UNITS = 8
N_DIFF = 4
N_BUCKETS = 32
MAX_DISTANCE = 128
BIAS_LEN = 640
PEER_HEADS = 8
TOPK = 16
CHUNKS = 128
EPS = 1e-6
LAMBDA_INIT = 0.8 - 0.6 * math.exp(0.0)
MASKED = -1e30
REMOVED = -3e38

A1_PER_HEAD = 6
A1 = PEER_HEADS * A1_PER_HEAD
A2 = 64
A3 = CHUNKS - A1 - A2
M_A2 = PEER_HEADS * 8
M_A3 = M_A2 + A2
M_V = M_A3 + A3
GROUP = 8
GROUPS = CHUNKS // GROUP
TOK = 8
TB = 64

RAW_V = [4, 4, 4, 4]
RAW_QK = [6, 6]
RAW_ADA2 = [14, 14, 6, 6]
RAW_WO = [22, 22, 14, 14]
RAW_MAIN = [24, 24, 16, 16]
SPLIT_V = [0, 0, 0, 0]
SPLIT_QK = [2, 2]
SPLIT_WO = [10, 10, 2, 2]
SPLIT_MAIN = [12, 12, 4, 4]
ADA1_TURNS = 4
ADA2_TURNS = 8

SCORE_BANKS = [[(3, 0)], [(3, 1)], [(2, 0), (0, 0)], [(2, 1), (0, 1)], [(1, 0), (1, 1)]]
SCORE_AT = {(3, 0): 0, (3, 1): 512, (2, 0): 1024, (0, 0): 1408, (2, 1): 1536, (0, 1): 1920, (1, 0): 2048, (1, 1): 2304}
BLOCKS = [(3, 2), (2, 4), (0, 4), (1, 5)]
NB = len(SCORE_BANKS)


class Steps:

    def __init__(self, engine, sem):
        self.engine, self.sem, self.turns, self.n = engine, sem, 0, 0

    def after(self, ins):
        self.count(ins)
        self.wait()

    def count(self, ins):
        self.n += 1
        ins.then_inc(self.sem, 1)

    def wait(self):
        self.engine.wait_ge(self.sem, self.turns + self.n)

    def enter(self, turn, steps_per_turn):
        self.first, self.per_turn = self.n, steps_per_turn
        self.turns = turn * steps_per_turn

    def leave(self, turns):
        assert self.n - self.first == self.per_turn, (self.n - self.first, self.per_turn)
        self.turns, self.n = 0, self.first + turns * self.per_turn


def bucket_table():
    table = np.zeros((N_BUCKETS + 1, BIAS_LEN), np.float32)
    exact = N_BUCKETS // 2
    for m in range(BIAS_LEN):
        dist = T - 1 - m
        if dist < 0:
            table[N_BUCKETS, m] = MASKED
        elif dist < exact:
            table[dist, m] = 1.0
        else:
            large = exact + int(math.log(dist / exact) / math.log(MAX_DISTANCE / exact) * (N_BUCKETS - exact))
            table[min(large, N_BUCKETS - 1), m] = 1.0
    return table


def build_layer(nc, x, vecs, rows, b_f, rel_bias, table, w_fl, keys, w_ada, w_v, w_qk, w_o, w_pq, peer_u, peer_v, out):
    F32, F32R, BF16, U32 = mybir.dt.float32, mybir.dt.float32r, mybir.dt.bfloat16, mybir.dt.uint32
    ACT = mybir.ActivationFunctionType
    ALU = mybir.AluOpType
    X_AXIS = mybir.AxisListType.X

    bias_dram = nc.dram_tensor("bias_by_distance", (N_DIFF, BIAS_LEN), F32, kind="Internal").ap()
    cum_dram = nc.dram_tensor("cumulative_forget", (8, T), F32, kind="Internal").ap()
    ncum_dram = nc.dram_tensor("negated_cumulative_forget", (8, T), F32, kind="Internal").ap()
    act_dram = nc.dram_tensor("expert_activations", (CHUNKS, P, T), F32, kind="Internal").ap()
    gate_dram = nc.dram_tensor("expert_gates", (CHUNKS, P, T), F32, kind="Internal").ap()

    with ExitStack() as ctx:
        def sb(name, shape, dt, scope=ctx):
            return scope.enter_context(nc.sbuf_tensor(name, shape, dt))

        raw = sb("raw", [P, SLOTS, D], F32)
        hi = sb("hi", [P, SLOTS, D], F32R)
        lo = sb("lo", [P, SLOTS, D], F32R)
        xres = sb("xres", [P, TT, D], F32)
        ident = sb("ident", [P, P], F32)
        flip = sb("flip", [P, P], F32)
        ones = sb("ones", [P, P], F32)
        ident_bf = sb("ident_bf", [P, P], BF16)
        causal = sb("causal", [P, P], BF16)
        iota = sb("iota", [P, P], BF16)
        iota16 = sb("iota16", [P, TOPK], F32)
        keys_sb = sb("keys_sb", [P, 2, P], F32)
        vec = sb("vec", [P, 88], F32)
        row = sb("row", [P, 384], F32)
        gsub = sb("gsub", [P, P], F32)
        silu_c = sb("silu_c", [P, 3, KD], F32)
        modc = sb("modc", [P, 48], F32)
        scale1 = sb("scale1", [P, 2, KD], F32)
        gate_cols = sb("gate_cols", [P, 2, KD], F32)
        forget_b = sb("forget_b", [8, 1], F32)
        relb = sb("relb", [N_BUCKETS + 1, N_DIFF], F32)
        lam = sb("lam", [P, 8], F32)
        spare = sb("spare", [1, 1], F32)
        lam_prod = sb("lam_prod", [P, 2, 64], F32)
        sumsq = sb("sumsq", [P, 5, TT], F32)
        meansq = sb("meansq", [P, 5, TT], F32)
        rstd = sb("rstd", [P, 5, TT], F32)
        minus_half = sb("minus_half", [P, TT], F32)
        negmax = sb("negmax", [P, 8], F32)
        psums = sb("psums", [P, 8], F32)
        rsums = sb("rsums", [P, 8], F32)
        lrsums = sb("lrsums", [P, 4], F32)
        gg2 = sb("gg2", [P, D], F32)
        aout = sb("aout", [P, 2, T], F32)
        id_i = sb("id_i", [P, T], BF16)
        id_j = sb("id_j", [P, T], BF16)
        gate_part = sb("gate_part", [P, 3, T], BF16)

        with ExitStack() as s:
            ht_hi = sb("ht_hi", [P, KD, T], F32R, s)
            ht_lo = sb("ht_lo", [P, KD, T], F32R, s)
        w_odd_hi = sb("w_odd_hi", [P, GROUP, T], F32R)
        w_odd_lo = sb("w_odd_lo", [P, GROUP, T], F32R)
        with ExitStack() as s:
            work = sb("work", [P, TT, D], F32, s)
        with ExitStack() as s:
            onehot_i = sb("onehot_i", [P, 2, TOK, P], BF16, s)
            gated_j = sb("gated_j", [P, 2, TOK, 3, P], BF16, s)
        acc = sb("acc", [P, KD, T], F32)
        with ExitStack() as s:
            v_sb = sb("v_sb", [P, TT, D], F32, s)
            probs = sb("probs", [P, 5 * T], F32, s)
            hankel = sb("hankel", [P, N_DIFF, T], F32, s)
            probs_t = sb("probs_t", [P, 2, T], F32, s)
            q_t = sb("q_t", [P, T], F32, s)
            k_t = sb("k_t", [P, T], F32, s)
            aug_q = sb("aug_q", [2, 2, T], F32, s)
            aug_k = sb("aug_k", [2, 2, T], F32, s)
            gg1 = sb("gg1", [P, D], F32, s)
            diag = sb("diag", [P, KD, P], F32, s)
            forget = sb("forget", [8, 3, T], F32, s)
            wfl = sb("wfl", [P, KD, 8], F32, s)
            wfl_hi = sb("wfl_hi", [P, KD, 8], F32R, s)
            wfl_lo = sb("wfl_lo", [P, KD, 8], F32R, s)
            table_sb = v_sb[0:N_BUCKETS + 1, 0, 0:BIAS_LEN]
            bias_row = v_sb[0:N_DIFF, 1, 0:BIAS_LEN]
        with ExitStack() as s:
            query = sb("query", [P, 2, T], F32, s)
            top_v = sb("top_v", [P, 2, TT, TOPK], F32, s)
            top_i = sb("top_i", [P, 2, TT, TOPK], U32, s)
            top_f = sb("top_f", [P, 2, TT, TOPK], F32, s)
            left = sb("left", [P, TT, P], F32, s)
            cand = sb("cand", [P, TT, TOPK, TOPK], F32, s)
            cand_left = sb("cand_left", [P, TT, TOPK, TOPK], F32, s)
            best = sb("best", [P, TT, TOPK], F32, s)
            pos = sb("pos", [P, 3, TT, TOPK], U32, s)
            pos_f = sb("pos_f", [P, 2, TT, TOPK], F32, s)
            match = sb("match", [P, 2, TT, TOPK, TOPK], F32, s)
            picked = sb("picked", [P, 3, TT, PEER_HEADS, TOPK], F32, s)
            gate_sum = sb("gate_sum", [P, 2, TT, PEER_HEADS], F32, s)
            gate_rest = sb("gate_rest", [P, 2, T], F32, s)
        with ExitStack() as s:
            gates = sb("gates", [P, 2, P, TB], F32, s)
        w_even_hi = sb("w_even_hi", [P, GROUP, T], F32R)
        w_even_lo = sb("w_even_lo", [P, GROUP, T], F32R)
        a_in = sb("a_in", [P, SLOTS, T], F32)
        g_in = sb("g_in", [P, SLOTS, T], F32)
        w_tmp = sb("w_tmp", [P, 2, T], F32)
        w_hi, w_lo = [w_even_hi, w_odd_hi], [w_even_lo, w_odd_lo]

        ps = ctx.enter_context(nc.psum_tensor("ps", [P, 8, 512], F32))

        def sem(name):
            return ctx.enter_context(nc.semaphore(name))

        vec_loaded = sem("vec_loaded")
        smalls_loaded = sem("smalls_loaded")
        relb_loaded = sem("relb_loaded")
        x_loaded = [sem(f"x_loaded{t}") for t in range(TT)]
        raw_full = [sem(f"raw_full{s}") for s in range(SLOTS)]
        ada_read = [sem(f"ada_read{s}") for s in range(SLOTS)]
        hi_done = [sem(f"hi_done{s}") for s in range(SLOTS)]
        lo_done = [sem(f"lo_done{s}") for s in range(SLOTS)]
        unit_done = [sem(f"unit_done{s}") for s in range(SLOTS)]
        consts_ready = sem("consts_ready")
        pool_steps = sem("pool_steps")
        act_steps = sem("act_steps")
        dve_steps = sem("dve_steps")
        silu_exp = sem("silu_exp")
        silu_ready = sem("silu_ready")
        lam_dots = sem("lam_dots")
        lam_exps = sem("lam_exps")
        bias_mm = sem("bias_mm")
        bias_row_ready = sem("bias_row_ready")
        bias_stored = sem("bias_stored")
        hankel_loaded = sem("hankel_loaded")
        mod_ready = sem("mod_ready")
        sumsq_done = sem("sumsq_done")
        meansq_ready = sem("meansq_ready")
        rstd_ready = sem("rstd_ready")
        xn_ready = sem("xn_ready")
        turned = sem("turned")
        ht_f32 = sem("ht_f32")
        ht_hi_done = sem("ht_hi_done")
        ht_lo_done = sem("ht_lo_done")
        wfl_hi_done = sem("wfl_hi_done")
        wfl_lo_done = sem("wfl_lo_done")
        forget_mm = sem("forget_mm")
        forget_abs = sem("forget_abs")
        forget_ln = sem("forget_ln")
        cum_ready = sem("cum_ready")
        cum_stored = sem("cum_stored")
        aug_loaded = sem("aug_loaded")
        v_ready = sem("v_ready")
        qk_ready = sem("qk_ready")
        scores_done = sem("scores_done")
        other_rows = sem("other_rows")
        max_done = sem("max_done")
        exp_done = sem("exp_done")
        probs_ready = sem("probs_ready")
        probs_turned = sem("probs_turned")
        probs_t_ready = sem("probs_t_ready")
        pv_done = sem("pv_done")
        heads_out = sem("heads_out")
        diag_ready = sem("diag_ready")
        spread = sem("spread")
        gg_ready = sem("gg_ready")
        y_ready = sem("y_ready")
        x1_ready = sem("x1_ready")
        query_ready = sem("query_ready")
        key_scores = sem("key_scores")
        level1_done = [sem(f"level1_done{p}") for p in range(2)]
        gate_shifted = sem("gate_shifted")
        gate_exp = sem("gate_exp")
        picks_ready = sem("picks_ready")
        picks_turned = sem("picks_turned")
        ids_ready = sem("ids_ready")
        gelu_done = [sem(f"gelu_done{b}") for b in range(2)]
        act_stored = [sem(f"act_stored{b}") for b in range(2)]
        onehots_ready = [sem(f"onehots_ready{b}") for b in range(2)]
        gate_mm = [sem(f"gate_mm{b}") for b in range(2)]
        gates_staged = [sem(f"gates_staged{b}") for b in range(2)]
        gates_stored = [sem(f"gates_stored{b}") for b in range(2)]
        ag_loaded = [sem(f"ag_loaded{s}") for s in range(SLOTS)]
        w_f32 = sem("w_f32")
        w_hi_done = sem("w_hi_done")
        w_ready = sem("w_ready")
        acc_added = [sem(f"acc_added{s}") for s in range(SLOTS)]
        out_stored = sem("out_stored")

        block = ctx.enter_context(nc.Block())

        @block.sync
        def _(sp):
            def load(slot, tile, ada_uses, split_uses):
                sp.wait_ge(ada_read[slot], ada_uses)
                sp.wait_ge(hi_done[slot], split_uses)
                sp.wait_ge(lo_done[slot], split_uses)
                sp.dma_start(raw[:, slot, :], tile).then_inc(raw_full[slot], 16)

            def tile_of(dram, n):
                return dram[n] if isinstance(n, int) else dram[bass.ds(n, 1), :, :].rearrange("o p n -> (o p) n")

            sp.dma_start(vec[:, :], vecs).then_inc(vec_loaded, 16)
            for t in range(TT):
                sp.dma_start(xres[:, t, :], x[t * P:(t + 1) * P, :]).then_inc(x_loaded[t], 16)
            for s in range(SLOTS):
                load(s, w_ada[s], 0, 0)
            with sp.Fori(0, ADA1_TURNS - 1) as j:
                for s in range(SLOTS):
                    load(s, tile_of(w_ada, (j + 1) * SLOTS + s), j + 1, 0)
            for n in range(2 * SLOTS):
                load(n % SLOTS, w_v[n], ADA1_TURNS, n // SLOTS)
            with sp.Fori(0, HEAD_UNITS) as u:
                for s in range(2):
                    load(s, tile_of(w_qk, u * 2 + s), ADA1_TURNS, SPLIT_QK[s] + u)
            for s in range(SLOTS):
                load(s, w_ada[16 + s], ADA1_TURNS, SPLIT_WO[s])
            with sp.Fori(0, ADA2_TURNS - 1) as j:
                for s in range(SLOTS):
                    load(s, tile_of(w_ada, (j + 1) * SLOTS + (16 + s)), j + (ADA1_TURNS + 1), SPLIT_WO[s])
            ada = ADA1_TURNS + ADA2_TURNS
            for n in range(2 * SLOTS):
                s = n % SLOTS
                load(s, w_o[n], ada, SPLIT_WO[s] + n // SLOTS)
            with sp.Fori(0, PEER_HEADS) as h:
                for t in range(8):
                    s = t % SLOTS
                    tile = tile_of(w_pq, h * 2 + t) if t < 2 else tile_of(peer_u, h * A1_PER_HEAD + (t - 2))
                    load(s, tile, ada, h * 2 + (SPLIT_MAIN[s] + t // SLOTS))
            with sp.Fori(0, (A2 + A3) // SLOTS) as j:
                for s in range(SLOTS):
                    load(s, tile_of(peer_u, j * SLOTS + (A1 + s)), ada, j + (SPLIT_MAIN[s] + M_A2 // SLOTS))
            with sp.Fori(0, CHUNKS // SLOTS) as j:
                for s in range(SLOTS):
                    load(s, tile_of(peer_v, j * SLOTS + s), ada, j + (SPLIT_MAIN[s] + M_V // SLOTS))

        @block.gpsimd
        def _(pool):
            steps = Steps(pool, pool_steps)
            nc.gpsimd.memset(ident[:, :], 0.0).then_inc(pool_steps, 1)
            nc.gpsimd.memset(flip[:, :], 0.0).then_inc(pool_steps, 1)
            nc.gpsimd.memset(causal[:, :], 0.0).then_inc(pool_steps, 1)
            nc.gpsimd.memset(ident_bf[:, :], 0.0).then_inc(pool_steps, 1)
            nc.gpsimd.memset(ones[:, :], 1.0).then_inc(consts_ready, 1)
            nc.gpsimd.memset(aug_q[:, :, :], 1.0).then_inc(pool_steps, 1)
            nc.gpsimd.memset(aug_k[:, :, :], 1.0).then_inc(pool_steps, 1)
            nc.gpsimd.memset(relb[:, :], 1.0).then_inc(pool_steps, 1)
            nc.gpsimd.memset(minus_half[:, :], -0.5).then_inc(pool_steps, 1)
            steps.n = 8
            steps.wait()
            pool.dma_start(relb[0:N_BUCKETS, :], rel_bias).then_inc(relb_loaded, 16)
            for m in (ident, ident_bf):
                nc.gpsimd.affine_select(out=m[:, :], in_=m[:, :], compare_op=ALU.not_equal, fill=1.0, base=0,
                                        pattern=[[-1, P]], channel_multiplier=1).then_inc(consts_ready, 1)
            nc.gpsimd.affine_select(out=flip[:, :], in_=flip[:, :], compare_op=ALU.not_equal, fill=1.0,
                                    base=-(P - 1), pattern=[[1, P]], channel_multiplier=1).then_inc(consts_ready, 1)
            nc.gpsimd.affine_select(out=causal[:, :], in_=causal[:, :], compare_op=ALU.is_ge, fill=MASKED, base=0,
                                    pattern=[[-1, P]], channel_multiplier=1).then_inc(consts_ready, 1)
            nc.gpsimd.iota(iota[:, :], pattern=[[1, P]], base=0, channel_multiplier=0,
                           allow_small_or_imprecise_dtypes=True).then_inc(consts_ready, 1)
            nc.gpsimd.iota(iota16[:, :], pattern=[[1, TOPK]], base=0, channel_multiplier=0,
                           allow_small_or_imprecise_dtypes=True).then_inc(consts_ready, 1)

            def root(n, norm):
                pool.wait_ge(meansq_ready, n)
                nc.gpsimd.tensor_tensor(rstd[:, norm, :], meansq[:, norm, :], minus_half[:, :],
                                        ALU.pow).then_inc(rstd_ready, 1)

            pool.wait_ge(bias_row_ready, 1)
            pool.dma_start(bias_dram, bias_row).then_inc(bias_stored, 16)
            pool.wait_ge(bias_stored, 16)
            pool.dma_start(hankel[:, :, :],
                           bass.AP(bias_dram.tensor, 0, [[1, P], [BIAS_LEN, N_DIFF], [1, T]])).then_inc(hankel_loaded, 16)
            root(1, 0)
            pool.wait_ge(cum_ready, 1)
            pool.dma_start(cum_dram, forget[:, 1, :]).then_inc(cum_stored, 16)
            pool.dma_start(ncum_dram, forget[:, 2, :]).then_inc(cum_stored, 16)
            pool.wait_ge(cum_stored, 32)

            def load_aug(pair, scores_before):
                if scores_before is not None:
                    pool.wait_ge(scores_done, scores_before)
                    pool.wait_ge(aug_loaded, pair * 32)
                first = pair * 2
                at = slice(0, 2) if isinstance(pair, int) else bass.ds(first, 2)
                pool.dma_start(aug_q[0:1, :, :], cum_dram[at, :].rearrange("(o h) t -> o h t", o=1)).then_inc(aug_loaded, 16)
                pool.dma_start(aug_k[1:2, :, :], ncum_dram[at, :].rearrange("(o h) t -> o h t", o=1)).then_inc(aug_loaded, 16)

            load_aug(0, None)
            with pool.Fori(0, N_DIFF) as u:
                root(u + 2, 1)
            with pool.Fori(0, 3) as p:
                load_aug(p + 1, p * NB + (N_DIFF + 1) * NB)
            root(6, 2)
            root(7, 3)

            def load_ag(n, slot, n_before):
                if n_before is not None:
                    pool.wait_ge(w_f32, n_before)
                chunk = slice(n, n + 1) if isinstance(n, int) else bass.ds(n, 1)
                pool.dma_start(a_in[:, slot, :], act_dram[chunk, :, :].rearrange("o p t -> (o p) t")).then_inc(ag_loaded[slot], 16)
                pool.dma_start(g_in[:, slot, :], gate_dram[chunk, :, :].rearrange("o p t -> (o p) t")).then_inc(ag_loaded[slot], 16)

            for b in range(2):
                pool.wait_ge(gates_stored[b], 16 * 4 * (T // TB // 2))
                pool.wait_ge(act_stored[b], 16 * (A1 + A2) // 2)
            for n in range(SLOTS):
                load_ag(n, n, None)
            for n in range(SLOTS, GROUP):
                load_ag(n, n % SLOTS, n - (SLOTS - 1))
            for b in range(2):
                pool.wait_ge(act_stored[b], 16 * CHUNKS // 2)
            with pool.Fori(GROUP // SLOTS, CHUNKS // SLOTS) as j:
                for s in range(SLOTS):
                    load_ag(j * SLOTS + s, s, j * SLOTS + s - (SLOTS - 1))
            root(8, 4)

        @block.scalar
        def _(act):
            steps = Steps(act, act_steps)

            def split_hi(slot, raw_use, split_use):
                act.wait_ge(raw_full[slot], raw_use * 16 + 16)
                act.wait_ge(unit_done[slot], split_use)
                nc.scalar.activation(hi[:, slot, :], raw[:, slot, :], ACT.Copy).then_inc(hi_done[slot], 1)

            def split_hi_main(t, turn):
                s, k = t % SLOTS, t // SLOTS
                split_hi(s, turn + (RAW_MAIN[s] + k), turn + (SPLIT_MAIN[s] + k))

            act.dma_start(table_sb, table).then_inc(smalls_loaded, 16)
            act.dma_start(keys_sb[:, :, :], keys).then_inc(smalls_loaded, 16)
            act.dma_start(row[:, :], bass.AP(rows.tensor, 0, [[0, P], [1, 384]])).then_inc(smalls_loaded, 16)
            act.dma_start(forget_b[:, :], b_f).then_inc(smalls_loaded, 16)
            act.dma_start(wfl[:, :, :], w_fl).then_inc(smalls_loaded, 16)
            act.wait_ge(vec_loaded, 16)
            nc.scalar.activation(silu_c[:, 0, :], vec[:, 80:88], ACT.Exp, scale=-1.0).then_inc(silu_exp, 1)
            act.wait_ge(lam_dots, 1)
            nc.scalar.activation(lam[:, 2:4], lam[:, 0:2], ACT.Exp).then_inc(lam_exps, 1)
            for t in range(TT):
                act.wait_ge(x_loaded[t], 16)
                nc.scalar.activation(work[:, t, :], xres[:, t, :], ACT.Square,
                                     accum_out=sumsq[:, 0, t:t + 1]).then_inc(sumsq_done, 1)
            act.wait_ge(smalls_loaded, 5 * 16)
            nc.scalar.activation(wfl_hi[:, :, :], wfl[:, :, :], ACT.Copy).then_inc(wfl_hi_done, 1)

            def affine_ht(base, which):
                for k in range(KD):
                    act.wait_ge(turned, base + k + 1)
                    if k >= 2 or base:
                        act.wait_ge(ht_lo_done, base + k - 1 if k >= 2 else base)
                    shift = modc[:, 24 * which + k:24 * which + k + 1]
                    act.activation(probs[:, (k % 2) * T:(k % 2 + 1) * T], ps[:, k % 2, :], ACT.Identity, bias=shift,
                                   scale=scale1[:, which, k:k + 1]).then_inc(ht_f32, 1)
                    act.wait_ge(ht_f32, which * KD + k + 1)
                    act.activation(ht_hi[:, k, :], probs[:, (k % 2) * T:(k % 2 + 1) * T], ACT.Copy).then_inc(ht_hi_done, 1)

            act.wait_ge(mod_ready, 1)
            affine_ht(0, 0)
            for n in range(SLOTS):
                split_hi(n, RAW_V[n], 0)
            act.wait_ge(forget_abs, 1)
            nc.scalar.activation(forget[:, 2, :], forget[:, 1, :], ACT.Exp).then_inc(forget_ln, 1)
            act.wait_ge(forget_ln, 1)
            nc.scalar.activation(forget[:, 1, :], forget[:, 2, :], ACT.Ln, bias=1.0).then_inc(forget_ln, 1)
            for n in range(SLOTS):
                split_hi(n, RAW_V[n] + 1, 1)
            act.wait_ge(unit_done[3], 1)
            for t in range(2):
                act.activation(v_sb[:, t, 0:512], ps[:, t, :], ACT.Copy).then_inc(v_ready, 1)
            for s in range(2):
                split_hi(s, RAW_QK[s], SPLIT_QK[s])
            act.wait_ge(unit_done[3], 2)
            for t in range(2):
                act.activation(v_sb[:, t, 512:1024], ps[:, 4 + t, :], ACT.Copy).then_inc(v_ready, 1)

            def evacuate_qk(u):
                act.wait_ge(unit_done[0], u + (SPLIT_QK[0] + 1))
                act.activation(q_t[:, :], ps[:, 5, :], ACT.Copy, scale=0.125).then_inc(qk_ready, 1)
                act.wait_ge(unit_done[1], u + (SPLIT_QK[1] + 1))
                act.activation(k_t[:, :], ps[:, 6, :], ACT.Copy).then_inc(qk_ready, 1)

            evacuate_qk(0)

            def attention(u, fox, last, jobs_before):
                if not last:
                    for s in range(2):
                        split_hi(s, u + (RAW_QK[s] + 1), u + (SPLIT_QK[s] + 1))
                for b, held in enumerate(SCORE_BANKS):
                    act.wait_ge(max_done, u * NB + (b + 1))
                    for i, m in held:
                        at, w, c = SCORE_AT[i, m], (i + 1) * P, 2 * i + m
                        last_exp = act.activation(probs[:, at:at + w], ps[:, b, at % 512:at % 512 + w], ACT.Exp,
                                                  bias=negmax[:, c:c + 1], accum_out=psums[:, c:c + 1])
                    last_exp.then_inc(exp_done, 1)
                if not last:
                    evacuate_qk(u + 1)
                jobs = [(i, m) for i, _ in BLOCKS for m in range(1 + fox)]
                for n, (i, m) in enumerate(jobs):
                    act.wait_ge(probs_turned, jobs_before + (n + 1))
                    if n >= 2:
                        act.wait_ge(pv_done, jobs_before + (n - 1))
                    w = (i + 1) * P
                    act.activation(probs_t[:, n % 2, 0:w], ps[:, 5 + n % 2, 0:w], ACT.Copy).then_inc(probs_t_ready, 1)
                if not fox:
                    act.wait_ge(pv_done, jobs_before + 4)
                    act.wait_ge(heads_out, u * 4)
                    for i in range(TT):
                        act.activation(lrs_junk[:, i, :], ps[:, 7, i * P:(i + 1) * P], ACT.Square,
                                       accum_out=sumsq[:, 1, i:i + 1]).then_inc(sumsq_done, 1)

            lrs_junk = diag
            with act.Fori(0, N_DIFF) as u:
                attention(u, False, False, u * 4)
            with act.Fori(0, 3) as p:
                attention(p + N_DIFF, True, False, p * 8 + 16)
            attention(7, True, True, 16 + 24)

            for k in range(KD):
                act.wait_ge(turned, KD + k + 1)
                act.activation(ht_hi[:, k, :], ps[:, k % 2, :], ACT.Copy).then_inc(ht_hi_done, 1)
            for s in range(SLOTS):
                split_hi(s, RAW_WO[s], SPLIT_WO[s])
            for n, gg in enumerate((gg1, gg2)):
                act.wait_ge(spread, n + 1)
                act.activation(gg[:, :], ps[:, 5:7, :].rearrange("p a n -> p (a n)"), ACT.Copy).then_inc(gg_ready, 1)
            for s in range(SLOTS):
                split_hi(s, RAW_WO[s] + 1, SPLIT_WO[s] + 1)
            for half in range(2):
                act.wait_ge(unit_done[3], SPLIT_WO[3] + 1 + half)
                for t in range(2):
                    act.activation(work[:, t, half * 512:half * 512 + 512], ps[:, 4 * half + t, :], ACT.Copy).then_inc(y_ready, 1)
            for t in range(LEAD):
                split_hi_main(t, 0)
            act.wait_ge(y_ready, 8)
            for t in range(TT):
                act.activation(v_sb[:, t, :], work[:, t, :], ACT.Square,
                               accum_out=sumsq[:, 2, t:t + 1]).then_inc(sumsq_done, 1)
            for t in range(TT):
                act.wait_ge(x1_ready, t + 1)
                act.activation(v_sb[:, t, :], xres[:, t, :], ACT.Square,
                               accum_out=sumsq[:, 3, t:t + 1]).then_inc(sumsq_done, 1)
            affine_ht(2 * KD, 1)

            def gelu(parity, uses, chunk):
                act.wait_ge(act_stored[parity], uses * 16)
                act.activation(aout[:, parity, :], ps[:, parity, :], ACT.Gelu_apprx_tanh).then_inc(gelu_done[parity], 1)
                act.wait_ge(gelu_done[parity], uses + 1)
                act.dma_start(act_dram[bass.ds(chunk, 1), :, :].rearrange("o p t -> (o p) t") if not isinstance(chunk, int)
                              else act_dram[chunk], aout[:, parity, :]).then_inc(act_stored[parity], 16)

            def unit_end(t, turn):
                s = t % SLOTS
                act.wait_ge(unit_done[s], turn + (SPLIT_MAIN[s] + t // SLOTS + 1))

            with act.Fori(0, PEER_HEADS) as h:
                for t in range(8):
                    split_hi_main(t + LEAD, h * 2)
                    unit_end(t, h * 2)
                    if t < 2:
                        act.wait_ge(key_scores, h * 2)
                        act.activation(query[:, t, :], ps[:, 4 + t, :], ACT.Copy).then_inc(query_ready, 1)
                    else:
                        gelu(t % 2, h * 3 + (t - 2) // 2, h * A1_PER_HEAD + (t - 2))
            act.wait_ge(gate_shifted, 1)
            act.activation(picked[:, 2], picked[:, 2], ACT.Exp).then_inc(gate_exp, 1)

            with act.Fori(0, A2 // 16) as r:
                for t in range(16):
                    split_hi_main(t + LEAD + M_A2, r * 4)
                    unit_end(t + M_A2, r * 4)
                    gelu(t % 2, r * 8 + (A1 + t) // 2, r * 16 + (A1 + t))
                    half, par = t // 8, t % 2
                    act.wait_ge(gate_mm[par], r * 8 + (t // 2 + 1))
                    if t % 8 == 0:
                        act.wait_ge(gates_stored[half], r * 64)
                    at = (t % 8) * TOK
                    act.activation(gates[:, half, :, at:at + TOK],
                                   ps[:, 2 + 2 * par:4 + 2 * par, :].rearrange("p a (q j) -> p j (a q)", j=P),
                                   ACT.Copy).then_inc(gates_staged[par], 1)
                    if t % 8 == 7:
                        for b in range(2):
                            act.wait_ge(gates_staged[b], r * 8 + 4 * (half + 1))
                        for j0 in range(0, P, 32):
                            act.dma_start(gate_dram[j0:j0 + 32, :, bass.ds(r * (2 * TB) + half * TB, TB)].rearrange("j i t -> i j t"),
                                          gates[:, half, j0:j0 + 32, :]).then_inc(gates_stored[half], 16)

            def split_w_hi(n, buffer, e, turn, tile):
                act.wait_ge(w_f32, n + 1)
                if e == 0:
                    unit_end(tile, turn)
                act.activation(w_hi[buffer][:, e, :], w_tmp[:, e % 2, :], ACT.Copy).then_inc(w_hi_done, 1)

            for t in range(A3):
                split_hi_main(t + LEAD + M_A3, 0)
                unit_end(t + M_A3, 0)
                gelu(t % 2, (A1 + A2 + t) // 2, A1 + A2 + t)
                if t >= A3 - GROUP:
                    e = t - (A3 - GROUP)
                    split_w_hi(e, 0, e, 0, M_A2 - 1)

            def second_sweep(g2, last):
                for half in range(2):
                    for dc in range(KD):
                        t = half * 8 + dc
                        final_half = last and half == 1
                        if not (final_half and dc + LEAD >= KD):
                            split_hi_main(t + LEAD + M_V, g2 * 4)
                        if not final_half:
                            split_w_hi(g2 * 16 + (GROUP + t), 1 - half, dc, g2 * 4, M_V + half * 8 - 1)

            with act.Fori(0, GROUPS // 2 - 1) as g2:
                second_sweep(g2, False)
            second_sweep(GROUPS // 2 - 1, True)

            for t in range(TT):
                act.wait_ge(turned, 3 * KD + t + 1)
                act.activation(raw[:, t, :], ps[:, 2 * t:2 * t + 2, :].rearrange("p a n -> p (a n)"), ACT.Square,
                               accum_out=sumsq[:, 4, t:t + 1]).then_inc(sumsq_done, 1)
            for t in range(TT):
                act.wait_ge(x1_ready, TT + t + 1)
                act.dma_start(out[t * P:(t + 1) * P, :], xres[:, t, :]).then_inc(out_stored, 16)
            act.wait_ge(out_stored, 16 * TT)

        @block.vector
        def _(dve):
            steps = Steps(dve, dve_steps)
            V = nc.vector

            def split_lo(slot, split_use):
                dve.wait_ge(hi_done[slot], split_use + 1)
                V.tensor_tensor(lo[:, slot, :], raw[:, slot, :], hi[:, slot, :].bitcast(F32),
                                ALU.subtract).then_inc(lo_done[slot], 1)

            def split_lo_main(t, turn):
                s = t % SLOTS
                split_lo(s, turn + (SPLIT_MAIN[s] + t // SLOTS))

            def mean_square(norm, n, width):
                dve.wait_ge(sumsq_done, n)
                V.tensor_scalar(meansq[:, norm, :], sumsq[:, norm, :], 1.0 / width, EPS, ALU.mult, ALU.add).then_inc(meansq_ready, 1)

            dve.wait_ge(silu_exp, 1)
            steps.after(V.tensor_scalar(silu_c[:, 1, :], silu_c[:, 0, :], 1.0, None, ALU.add))
            steps.after(V.reciprocal(silu_c[:, 2, :], silu_c[:, 1, :]))
            V.tensor_tensor(silu_c[:, 0, :], silu_c[:, 2, :], vec[:, 80:88], ALU.mult).then_inc(silu_ready, 1)
            dve.wait_ge(smalls_loaded, 5 * 16)
            for m in range(2):
                steps.count(V.tensor_tensor(lam_prod[:, m, :], row[:, 128 + 128 * m:192 + 128 * m],
                                            row[:, 192 + 128 * m:256 + 128 * m], ALU.mult))
            steps.wait()
            V.tensor_reduce(lam[:, 0:2], lam_prod[:, :, :], X_AXIS, ALU.add).then_inc(lam_dots, 1)
            dve.wait_ge(lam_exps, 1)
            steps.after(V.tensor_tensor(lam[:, 4:5], lam[:, 3:4], lam[:, 2:3], ALU.subtract))
            steps.after(V.tensor_scalar(lam[:, 5:6], lam[:, 4:5], -LAMBDA_INIT, None, ALU.add))
            steps.after(V.tensor_scalar(gsub[:, :], row[:, 0:P], 1.0 - LAMBDA_INIT, None, ALU.mult))
            dve.wait_ge(bias_mm, 2)
            steps.after(V.tensor_copy(bias_row[:, 0:512], ps[0:N_DIFF, 2, :]))
            V.tensor_copy(bias_row[:, 512:BIAS_LEN], ps[0:N_DIFF, 3, 0:BIAS_LEN - 512]).then_inc(bias_row_ready, 1)
            mean_square(0, 4, D)
            dve.wait_ge(wfl_hi_done, 1)
            V.tensor_tensor(wfl_lo[:, :, :], wfl[:, :, :], wfl_hi[:, :, :].bitcast(F32), ALU.subtract).then_inc(wfl_lo_done, 1)

            def normalise(n, norm):
                dve.wait_ge(rstd_ready, n)
                for t in range(TT):
                    V.tensor_scalar(work[:, t, :], xres[:, t, :], rstd[:, norm, t:t + 1], None, ALU.mult).then_inc(xn_ready, 1)

            normalise(1, 0)
            for s in range(SLOTS):
                dve.wait_ge(ada_read[s], ADA1_TURNS)
            steps.after(V.tensor_tensor(modc[:, 0:16], ps[:, 7, 0:16], vec[:, 0:16], ALU.add))
            V.scalar_tensor_tensor(scale1[:, 0, :], modc[:, 8:16], 1.0, vec[:, 48:56], ALU.add, ALU.mult).then_inc(mod_ready, 1)

            def ht_remainder(base, source):
                for k in range(KD):
                    dve.wait_ge(ht_hi_done, base + k + 1)
                    V.tensor_tensor(ht_lo[:, k, :], source(k), ht_hi[:, k, :].bitcast(F32), ALU.subtract).then_inc(ht_lo_done, 1)

            ht_remainder(0, lambda k: probs[:, (k % 2) * T:(k % 2 + 1) * T])
            for n in range(SLOTS):
                split_lo(n, 0)
            dve.wait_ge(forget_mm, 1)
            steps.after(V.tensor_scalar(forget[:, 0, :], ps[0:8, 6, :], forget_b[:, 0:1], None, ALU.add))
            steps.after(V.tensor_scalar(forget[:, 2, :], forget[:, 0, :], -1.0, None, ALU.mult))
            V.tensor_tensor(forget[:, 1, :], forget[:, 0, :], forget[:, 2, :], ALU.min).then_inc(forget_abs, 1)
            dve.wait_ge(forget_ln, 2)
            steps.after(V.scalar_tensor_tensor(forget[:, 2, :], forget[:, 0, :], 0.0, forget[:, 1, :], ALU.min, ALU.subtract))
            steps.after(V.memset(forget[:, 0, :], 1.0))
            steps.after(V.tensor_tensor_scan(forget[:, 1, :], forget[:, 0, :], forget[:, 2, :], 0.0, ALU.mult, ALU.add))
            V.tensor_scalar(forget[:, 2, :], forget[:, 1, :], -1.0, None, ALU.mult).then_inc(cum_ready, 1)
            for n in range(SLOTS):
                split_lo(n, 1)
            dve.wait_ge(unit_done[3], 1)
            for t in range(2, TT):
                V.tensor_copy(v_sb[:, t, 0:512], ps[:, t, :]).then_inc(v_ready, 1)
            for s in range(2):
                split_lo(s, SPLIT_QK[s])
            dve.wait_ge(unit_done[3], 2)
            for t in range(2, TT):
                V.tensor_copy(v_sb[:, t, 512:1024], ps[:, 4 + t, :]).then_inc(v_ready, 1)

            def attention(u, fox, last):
                if not last:
                    for s in range(2):
                        split_lo(s, u + (SPLIT_QK[s] + 1))
                for b, held in enumerate(SCORE_BANKS):
                    dve.wait_ge(scores_done, u * NB + (b + 1))
                    if b == NB - 1:
                        V.tensor_reduce(negmax[:, 2:4], ps[:, b, :].rearrange("p (m k) -> p m k", m=2), X_AXIS, ALU.max,
                                        negate=True).then_inc(max_done, 1)
                        continue
                    for i, m in held:
                        at, w, c = SCORE_AT[i, m] % 512, (i + 1) * P, 2 * i + m
                        last_max = V.tensor_reduce(negmax[:, c:c + 1], ps[:, b, at:at + w], X_AXIS, ALU.max, negate=True)
                    last_max.then_inc(max_done, 1)
                for i, banks in BLOCKS:
                    w, c = (i + 1) * P, 2 * i
                    p0 = probs[:, SCORE_AT[i, 0]:SCORE_AT[i, 0] + w]
                    p1 = probs[:, SCORE_AT[i, 1]:SCORE_AT[i, 1] + w]
                    dve.wait_ge(exp_done, u * NB + banks)
                    steps.after(V.reciprocal(rsums[:, c:c + 2], psums[:, c:c + 2]))
                    if fox:
                        V.tensor_scalar(p0, p0, rsums[:, c:c + 1], None, ALU.mult).then_inc(probs_ready, 1)
                        V.tensor_scalar(p1, p1, rsums[:, c + 1:c + 2], None, ALU.mult).then_inc(probs_ready, 1)
                    else:
                        steps.after(V.tensor_tensor(lrsums[:, i:i + 1], rsums[:, c + 1:c + 2], lam[:, 5:6], ALU.mult))
                        steps.after(V.tensor_scalar(p1, p1, lrsums[:, i:i + 1], None, ALU.mult))
                        V.scalar_tensor_tensor(p0, p0, rsums[:, c:c + 1], p1, ALU.mult, ALU.add).then_inc(probs_ready, 1)

            with dve.Fori(0, N_DIFF) as u:
                steps.enter(u, 4 * 3)
                attention(u, False, False)
                mean_square(1, u * 4 + 8, P)
                dve.wait_ge(rstd_ready, u + 2)
                for i in range(TT):
                    V.scalar_tensor_tensor(work[:, i, bass.ds(u * P, P)], ps[:, 7, i * P:(i + 1) * P], rstd[:, 1, i:i + 1],
                                           gsub[:, :], ALU.mult, ALU.mult).then_inc(heads_out, 1)
                steps.leave(N_DIFF)

            def fox_out(u, jobs):
                dve.wait_ge(pv_done, jobs)
                for i in range(TT):
                    V.tensor_copy(work[:, i, bass.ds(u * P, P)], ps[:, 7, i * P:(i + 1) * P]).then_inc(heads_out, 1)

            with dve.Fori(0, 3) as p:
                steps.enter(p, 4)
                attention(p + N_DIFF, True, False)
                fox_out(p + N_DIFF, p * 8 + 24)
                steps.leave(3)
            attention(7, True, True)
            fox_out(7, 48)

            for s in range(SLOTS):
                dve.wait_ge(ada_read[s], ADA1_TURNS + ADA2_TURNS)
            steps.after(V.tensor_tensor(modc[:, 16:48], ps[:, 4, 0:32], vec[:, 16:48], ALU.add))
            steps.count(V.scalar_tensor_tensor(scale1[:, 1, :], modc[:, 32:40], 1.0, vec[:, 64:72], ALU.add, ALU.mult))
            steps.count(V.tensor_tensor(gate_cols[:, 0, :], modc[:, 16:24], vec[:, 56:64], ALU.mult))
            steps.count(V.tensor_tensor(gate_cols[:, 1, :], modc[:, 40:48], vec[:, 72:80], ALU.mult))
            steps.wait()
            for k in range(KD):
                V.tensor_scalar(diag[:, k, :], ident[:, :], gate_cols[:, 0, k:k + 1], None, ALU.mult).then_inc(diag_ready, 1)
            ht_remainder(KD, lambda k: ps[:, k % 2, :])
            for s in range(SLOTS):
                split_lo(s, SPLIT_WO[s])
            dve.wait_ge(spread, 1)
            for k in range(KD):
                V.tensor_scalar(diag[:, k, :], ident[:, :], gate_cols[:, 1, k:k + 1], None, ALU.mult).then_inc(diag_ready, 1)
            for s in range(SLOTS):
                split_lo(s, SPLIT_WO[s] + 1)
            for half in range(2):
                dve.wait_ge(unit_done[3], SPLIT_WO[3] + 1 + half)
                for t in range(2, TT):
                    V.tensor_copy(work[:, t, half * 512:half * 512 + 512], ps[:, 4 * half + t, :]).then_inc(y_ready, 1)
            for t in range(LEAD):
                split_lo_main(t, 0)
            mean_square(2, 24, D)
            dve.wait_ge(rstd_ready, 6)
            dve.wait_ge(gg_ready, 2)
            for t in range(TT):
                steps.count(V.scalar_tensor_tensor(work[:, t, :], work[:, t, :], rstd[:, 2, t:t + 1], gg1[:, :], ALU.mult, ALU.mult))
            for t in range(TT):
                steps.wait()
                V.tensor_tensor(xres[:, t, :], xres[:, t, :], work[:, t, :], ALU.add).then_inc(x1_ready, 1)
            mean_square(3, 28, D)
            normalise(7, 3)
            ht_remainder(2 * KD, lambda k: probs[:, (k % 2) * T:(k % 2 + 1) * T])

            def apart():
                steps.count(V.memset(spare[0:1, 0:1], 0.0))

            def level1(p, h):
                s = lambda t: ps[:, 6 + p, t * P:(t + 1) * P]
                dve.wait_ge(key_scores, h * 2 + (p + 1))
                apart()
                for t in range(TT):
                    steps.count(V.max(top_v[:, p, t, 0:8], s(t)))
                steps.wait()
                apart()
                for t in range(TT):
                    steps.count(V.match_replace(left[:, t, :], top_v[:, p, t, 0:8], s(t), REMOVED))
                for t in range(TT):
                    steps.count(V.max_index(top_i[:, p, t, 0:8], top_v[:, p, t, 0:8], s(t)))
                steps.wait()
                apart()
                for t in range(TT):
                    steps.count(V.max(top_v[:, p, t, 8:16], left[:, t, :]))
                steps.wait()
                apart()
                for t in range(TT):
                    steps.count(V.max_index(top_i[:, p, t, 8:16], top_v[:, p, t, 8:16], left[:, t, :]))
                steps.wait()
                V.tensor_copy(top_f[:, p], top_i[:, p]).then_inc(level1_done[p], 1)

            def level2_first():
                b = top_v[:, 1].unsqueeze(2).to_broadcast([P, TT, TOPK, TOPK])
                steps.count(V.tensor_tensor(cand[:, :, :, :], top_v[:, 0].unsqueeze(3).to_broadcast([P, TT, TOPK, TOPK]), b, ALU.add))
                steps.wait()
                apart()
                for t in range(TT):
                    steps.count(V.max(best[:, t, 0:8], cand[:, t].rearrange("p a b -> p (a b)")))
                steps.wait()
                apart()
                for t in range(TT):
                    steps.count(V.match_replace(cand_left[:, t].rearrange("p a b -> p (a b)"), best[:, t, 0:8],
                                                cand[:, t].rearrange("p a b -> p (a b)"), REMOVED))
                steps.wait()

            def level2_second():
                steps.wait()
                apart()
                for t in range(TT):
                    steps.count(V.max(best[:, t, 8:16], cand_left[:, t].rearrange("p a b -> p (a b)")))
                for t in range(TT):
                    steps.count(V.max_index(pos[:, 0, t, 0:8], best[:, t, 0:8], cand[:, t].rearrange("p a b -> p (a b)")))
                steps.wait()
                apart()
                for t in range(TT):
                    steps.count(V.max_index(pos[:, 0, t, 8:16], best[:, t, 8:16], cand_left[:, t].rearrange("p a b -> p (a b)")))
                steps.wait()

            def decode(p, h):
                if p == 0:
                    steps.count(V.tensor_scalar(pos[:, 1], pos[:, 0], 4, None, ALU.logical_shift_right))
                    steps.count(V.tensor_scalar(pos[:, 2], pos[:, 0], 15, None, ALU.bitwise_and))
                    steps.wait()
                    steps.count(V.tensor_copy(pos_f[:, :], pos[:, 1:3]))
                    steps.count(V.tensor_copy(picked[:, 2, :, bass.ds(h, 1), :].rearrange("p t o k -> p t (o k)"), best[:, :, :]))
                    steps.wait()
                four = [P, TT, TOPK, TOPK]
                steps.after(V.tensor_tensor(match[:, 0].rearrange("p t k a -> p (t k) a"),
                                            pos_f[:, p].rearrange("p t k -> p (t k)").unsqueeze(2).to_broadcast([P, TT * TOPK, TOPK]),
                                            iota16[:, :].unsqueeze(1).to_broadcast([P, TT * TOPK, TOPK]), ALU.is_equal))
                steps.after(V.tensor_tensor(match[:, 1], match[:, 0], top_f[:, p].unsqueeze(2).to_broadcast(four), ALU.mult))
                steps.after(V.tensor_reduce(picked[:, p, :, bass.ds(h, 1), :].rearrange("p t o k -> p t (o k)"), match[:, 1],
                                            X_AXIS, ALU.add))

            with dve.Fori(0, PEER_HEADS) as h:
                steps.enter(h, 2 * 24 + 11 + 14 + 4 + 6)
                for t in range(8):
                    split_lo_main(t + LEAD, h * 2)
                    if t in (2, 3):
                        level1(t - 2, h)
                    elif t == 4:
                        level2_first()
                    elif t == 5:
                        level2_second()
                    elif t >= 6:
                        decode(t - 6, h)
                steps.leave(PEER_HEADS)
            flat = [P, TT * PEER_HEADS, TOPK]
            gate = picked[:, 2].rearrange("p t h k -> p (t h) k")
            total = gate_sum[:, 0].rearrange("p t h -> p (t h)")
            inverse = gate_sum[:, 1].rearrange("p t h -> p (t h)")
            steps.after(V.tensor_copy(total, gate[:, :, 0:1].rearrange("p a o -> p (a o)")))
            V.tensor_tensor(gate, gate, total.unsqueeze(2).to_broadcast(flat), ALU.subtract).then_inc(gate_shifted, 1)
            dve.wait_ge(gate_exp, 1)
            steps.after(V.tensor_reduce(total, gate, X_AXIS, ALU.add))
            steps.after(V.reciprocal(inverse, total))
            V.tensor_tensor(gate, gate, inverse.unsqueeze(2).to_broadcast(flat), ALU.mult).then_inc(picks_ready, 1)
            dve.wait_ge(picks_turned, 3)
            steps.count(V.tensor_copy(id_i[:, :], ps[:, 4, :]))
            steps.count(V.tensor_copy(id_j[:, :], ps[:, 5, :]))
            steps.after(V.tensor_copy(gate_part[:, 0, :], ps[:, 6, :]))
            steps.after(V.tensor_tensor(gate_rest[:, 0, :], ps[:, 6, :], gate_part[:, 0, :], ALU.subtract))
            steps.after(V.tensor_copy(gate_part[:, 1, :], gate_rest[:, 0, :]))
            steps.after(V.tensor_tensor(gate_rest[:, 1, :], gate_rest[:, 0, :], gate_part[:, 1, :], ALU.subtract))
            steps.after(V.tensor_copy(gate_part[:, 2, :], gate_rest[:, 1, :]))
            V.memset(lam[:, 6:7], 0.0).then_inc(ids_ready, 1)

            with dve.Fori(0, A2 // 16) as r:
                for t in range(16):
                    split_lo_main(t + LEAD + M_A2, r * 4)
                    par = t % 2
                    dve.wait_ge(gate_mm[par], r * 8 + t // 2)
                    for q in range(TOK):
                        col = bass.ds(r * (16 * TOK) + (t * TOK + q), 1)
                        V.tensor_scalar(onehot_i[:, par, q, :], iota[:, :], id_i[:, col], None, ALU.is_equal)
                        for part in range(3):
                            last = V.tensor_scalar(gated_j[:, par, q, part, :], iota[:, :], id_j[:, col],
                                                   gate_part[:, part, col], ALU.is_equal, ALU.mult)
                    last.then_inc(onehots_ready[par], 1)

            def w_chunk(n, buffer, e, slot, uses):
                dve.wait_ge(ag_loaded[slot], uses * 32 + 32)
                V.tensor_tensor(w_tmp[:, e % 2, :], a_in[:, slot, :], g_in[:, slot, :], ALU.mult).then_inc(w_f32, 1)

            def w_rest(n, buffer, e):
                dve.wait_ge(w_hi_done, n + 1)
                V.tensor_tensor(w_lo[buffer][:, e, :], w_tmp[:, e % 2, :], w_hi[buffer][:, e, :].bitcast(F32),
                                ALU.subtract).then_inc(w_ready, 1)

            for t in range(A3):
                split_lo_main(t + LEAD + M_A3, 0)
                if t >= A3 - GROUP:
                    e = t - (A3 - GROUP)
                    if e >= 2:
                        dve.wait_ge(w_ready, e - 1)
                    w_chunk(e, 0, e, e % SLOTS, e // SLOTS)
                    w_rest(e, 0, e)

            for b in range(2):
                dve.wait_ge(act_stored[b], 16 * CHUNKS // 2)
            steps.after(V.memset(acc[:, :, :], 0.0))

            def second_sweep(g2, last):
                for half in range(2):
                    final_half = last and half == 1
                    for dc in range(KD):
                        t = half * 8 + dc
                        if not (final_half and dc + LEAD >= KD):
                            split_lo_main(t + LEAD + M_V, g2 * 4)
                        n = g2 * 16 + (GROUP + t)
                        if not final_half:
                            dve.wait_ge(w_ready, n - 1)
                            w_chunk(n, 1 - half, dc, dc % SLOTS, g2 * 4 + (GROUP + t) // SLOTS)
                        s = dc % SLOTS
                        dve.wait_ge(unit_done[s], g2 * 4 + (SPLIT_MAIN[s] + (M_V + t) // SLOTS + 1))
                        dve.wait_ge(acc_added[s], g2 * 4 + t // SLOTS)
                        V.tensor_tensor(acc[:, dc, :], acc[:, dc, :], ps[:, s, :], ALU.add).then_inc(acc_added[s], 1)
                        if not final_half:
                            w_rest(n, 1 - half, dc)

            with dve.Fori(0, GROUPS // 2 - 1) as g2:
                second_sweep(g2, False)
            second_sweep(GROUPS // 2 - 1, True)

            mean_square(4, 32, D)
            dve.wait_ge(rstd_ready, 8)
            for t in range(TT):
                steps.count(V.scalar_tensor_tensor(raw[:, t, :], ps[:, 2 * t:2 * t + 2, :].rearrange("p a n -> p (a n)"),
                                                   rstd[:, 4, t:t + 1], gg2[:, :], ALU.mult, ALU.mult))
                steps.wait()
                V.tensor_tensor(xres[:, t, :], xres[:, t, :], raw[:, t, :], ALU.add).then_inc(x1_ready, 1)

        @block.tensor
        def _(pe):
            mm = nc.tensor.matmul

            def three(dst, w_hi_ap, w_lo_ap, r_hi, r_lo, start, stop):
                mm(dst, w_hi_ap, r_hi, start=start, stop=False)
                mm(dst, w_hi_ap, r_lo, start=False, stop=False)
                return mm(dst, w_lo_ap, r_hi, start=False, stop=stop)

            def unit(slot, split_use, bank, r_hi, r_lo):
                pe.wait_ge(lo_done[slot], split_use + 1)
                for k in range(KD):
                    at = slice(k * P, (k + 1) * P)
                    last = three(ps[:, bank, :], hi[:, slot, at], lo[:, slot, at], r_hi[:, k, :], r_lo[:, k, :],
                                 k == 0, k == KD - 1)
                last.then_inc(unit_done[slot], 1)

            def row_unit(slot, split_use, first_bank, quarter):
                pe.wait_ge(lo_done[slot], split_use + 1)
                for k2 in range(2):
                    k, at = 2 * quarter + k2, slice(k2 * 512, k2 * 512 + 512)
                    for t in range(TT):
                        cols = slice(t * P, (t + 1) * P)
                        last = three(ps[:, first_bank + t, :], ht_hi[:, k, cols], ht_lo[:, k, cols],
                                     hi[:, slot, at], lo[:, slot, at], k == 0, k == KD - 1)
                last.then_inc(unit_done[slot], 1)

            def turn_work(base, source):
                for k in range(KD):
                    if k >= 2:
                        pe.wait_ge(ht_lo_done, base + k - 1)
                    for t in range(TT):
                        last = nc.tensor.transpose(ps[:, k % 2, t * P:(t + 1) * P], work[:, t, k * P:(k + 1) * P], ident[:, :])
                    last.then_inc(turned, 1)

            def ada(slot, raw_use, bank, col):
                pe.wait_ge(raw_full[slot], raw_use * 16 + 16)
                for k in range(KD):
                    last = mm(ps[:, bank, bass.ds(col, 1)], raw[:, slot, k * P:(k + 1) * P], silu_c[:, 0, k:k + 1],
                              start=(k == 0), stop=(k == KD - 1))
                last.then_inc(ada_read[slot], 1)

            pe.wait_ge(smalls_loaded, 5 * 16)
            pe.wait_ge(relb_loaded, 16)
            mm(ps[0:N_DIFF, 2, :], relb[:, :], table_sb[:, 0:512], start=True, stop=True).then_inc(bias_mm, 1)
            mm(ps[0:N_DIFF, 3, 0:BIAS_LEN - 512], relb[:, :], table_sb[:, 512:BIAS_LEN], start=True, stop=True).then_inc(bias_mm, 1)
            pe.wait_ge(silu_ready, 1)
            with pe.Fori(0, ADA1_TURNS) as j:
                for s in range(SLOTS):
                    ada(s, j, 7, j * SLOTS + s)
            pe.wait_ge(consts_ready, 7)
            pe.wait_ge(xn_ready, TT)
            turn_work(0, work)
            pe.wait_ge(ht_lo_done, KD)
            pe.wait_ge(wfl_lo_done, 1)
            for k in range(KD):
                last = three(ps[0:8, 6, :], wfl_hi[:, k, :], wfl_lo[:, k, :], ht_hi[:, k, :], ht_lo[:, k, :], k == 0, k == KD - 1)
            last.then_inc(forget_mm, 1)
            pe.wait_ge(hankel_loaded, 16)
            for n in range(2 * SLOTS):
                if n == SLOTS:
                    pe.wait_ge(forget_abs, 1)
                    pe.wait_ge(mod_ready, 1)
                row_unit(n % SLOTS, n // SLOTS, 4 * (n // SLOTS), n % SLOTS)

            def project(u):
                for s in range(2):
                    unit(s, u + SPLIT_QK[s], 5 + s, ht_hi, ht_lo)

            pe.wait_ge(v_ready, 2 * TT)
            project(0)

            def attention(u, fox, last, jobs_before):
                pe.wait_ge(qk_ready, u * 2 + 2)
                pe.wait_ge(exp_done, u * NB)
                if fox:
                    pe.wait_ge(aug_loaded, (u - (N_DIFF - 1)) * 32)
                for b, held in enumerate(SCORE_BANKS):
                    for i, m in held:
                        at, w = SCORE_AT[i, m] % 512, (i + 1) * P
                        dst = ps[:, b, at:at + w]
                        half = slice(64 * m, 64 * m + 64)
                        if (i, m) == (1, 1):
                            pe.wait_ge(other_rows, u + 1)
                        mm(dst, q_t[half, i * P:(i + 1) * P], k_t[half, 0:w], start=True, stop=False)
                        if fox:
                            mm(dst, aug_q[:, m, i * P:(i + 1) * P], aug_k[:, m, 0:w], start=False, stop=False)
                            done = mm(dst[:, i * P:w], ident_bf[:, :], causal[:, :], start=False, stop=True)
                        else:
                            done = mm(dst, flip[:, :], hankel[:, bass.ds(u, 1), (3 - i) * P:T].rearrange("p o k -> p (o k)"),
                                      start=False, stop=True)
                        if (i, m) == (1, 0):
                            done.then_inc(other_rows, 1)
                    done.then_inc(scores_done, 1)
                pe.wait_ge(probs_t_ready, jobs_before)
                if not last:
                    project(u + 1)
                    pe.wait_ge(qk_ready, u * 2 + 4)
                pe.wait_ge(heads_out, u * 4)
                jobs = [(i, m) for i, _ in BLOCKS for m in range(1 + fox)]

                def turn_probs(n):
                    pe.wait_ge(probs_ready, jobs_before + (n + 1))
                    if n >= 2:
                        pe.wait_ge(probs_t_ready, jobs_before + (n - 1))
                    i, m = jobs[n]
                    at = SCORE_AT[i, m]
                    for kb in range(i + 1):
                        done = nc.tensor.transpose(ps[:, 5 + n % 2, kb * P:(kb + 1) * P],
                                                   probs[:, at + kb * P:at + (kb + 1) * P], ident[:, :])
                    done.then_inc(probs_turned, 1)

                def times_v(n):
                    pe.wait_ge(probs_t_ready, jobs_before + (n + 1))
                    i, m = jobs[n]
                    width = 64 if fox else P
                    for kb in range(i + 1):
                        cols = bass.ds(u * P + m * 64, width) if not isinstance(u, int) else slice(u * P + m * 64, u * P + m * 64 + width)
                        done = mm(ps[:, 7, i * P + m * 64:i * P + m * 64 + width], probs_t[:, n % 2, kb * P:(kb + 1) * P],
                                  v_sb[:, kb, cols], start=(kb == 0), stop=(kb == i))
                    done.then_inc(pv_done, 1)

                turn_probs(0)
                for n in range(1, len(jobs)):
                    turn_probs(n)
                    times_v(n - 1)
                times_v(len(jobs) - 1)

            with pe.Fori(0, N_DIFF) as u:
                attention(u, False, False, u * 4)
            with pe.Fori(0, 3) as p:
                attention(p + N_DIFF, True, False, p * 8 + 16)
            attention(7, True, True, 40)

            pe.wait_ge(exp_done, HEAD_UNITS * NB)
            with pe.Fori(0, ADA2_TURNS) as j:
                for s in range(SLOTS):
                    ada(s, j + RAW_ADA2[s], 4, j * SLOTS + s)

            def spread_gate(n):
                pe.wait_ge(diag_ready, (n + 1) * KD)
                for k in range(KD):
                    last = mm(ps[:, 5 + k // 4, (k % 4) * P:(k % 4 + 1) * P], ones[:, :], diag[:, k, :], start=True, stop=True)
                last.then_inc(spread, 1)

            pe.wait_ge(heads_out, HEAD_UNITS * TT)
            turn_work(KD, work)
            spread_gate(0)
            pe.wait_ge(ht_lo_done, 2 * KD)
            for n in range(SLOTS):
                row_unit(n, SPLIT_WO[n], 0, n)
            pe.wait_ge(gg_ready, 1)
            spread_gate(1)
            pe.wait_ge(gg_ready, 2)
            for n in range(SLOTS):
                row_unit(n, SPLIT_WO[n] + 1, 4, n)
            pe.wait_ge(xn_ready, 2 * TT)
            turn_work(2 * KD, work)
            pe.wait_ge(ht_lo_done, 3 * KD)

            def main_unit(t, turn, bank, r_hi, r_lo):
                s = t % SLOTS
                unit(s, turn + (SPLIT_MAIN[s] + t // SLOTS), bank, r_hi, r_lo)

            def key_products(p, h):
                pe.wait_ge(query_ready, h * 2 + (p + 1))
                pe.wait_ge(level1_done[p], h)
                for t in range(TT):
                    last = mm(ps[:, 6 + p, t * P:(t + 1) * P], query[:, p, t * P:(t + 1) * P], keys_sb[:, p, :],
                              start=True, stop=True)
                last.then_inc(key_scores, 1)

            with pe.Fori(0, PEER_HEADS) as h:
                for t in range(8):
                    if t < 2:
                        pe.wait_ge(query_ready, h * 2 + t)
                        main_unit(t, h * 2, 4 + t, ht_hi, ht_lo)
                        if t == 1:
                            key_products(0, h)
                    else:
                        pe.wait_ge(gelu_done[t % 2], h * 3 + (t - 2) // 2)
                        main_unit(t, h * 2, t % 2, ht_hi, ht_lo)
                        if t == 2:
                            key_products(1, h)
            pe.wait_ge(picks_ready, 1)
            for n in range(3):
                for t in range(TT):
                    last = nc.tensor.transpose(ps[:, 4 + n, t * P:(t + 1) * P], picked[:, n, t].rearrange("p h k -> p (h k)"), ident[:, :])
                last.then_inc(picks_turned, 1)
            pe.wait_ge(ids_ready, 1)
            with pe.Fori(0, A2 // 16) as r:
                for t in range(16):
                    par = t % 2
                    pe.wait_ge(gelu_done[par], r * 8 + (A1 + t) // 2)
                    main_unit(t + M_A2, r * 4, par, ht_hi, ht_lo)
                    pe.wait_ge(onehots_ready[par], r * 8 + (t // 2 + 1))
                    pe.wait_ge(gates_staged[par], r * 8 + t // 2)
                    for q in range(TOK):
                        for part in range(3):
                            last = mm(ps[:, 2 + 2 * par + q // 4, (q % 4) * P:(q % 4 + 1) * P], onehot_i[:, par, q, :],
                                      gated_j[:, par, q, part, :], start=(part == 0), stop=(part == 2))
                    last.then_inc(gate_mm[par], 1)
            for t in range(A3):
                pe.wait_ge(gelu_done[t % 2], (A1 + A2 + t) // 2)
                main_unit(t + M_A3, 0, t % 2, ht_hi, ht_lo)

            def second_sweep(g2):
                for half in range(2):
                    for dc in range(KD):
                        t, s = half * 8 + dc, dc % SLOTS
                        if dc >= SLOTS or half:
                            pe.wait_ge(acc_added[s], g2 * 4 + t // SLOTS)
                        else:
                            pe.wait_ge(acc_added[s], g2 * 4)
                        pe.wait_ge(lo_done[s], g2 * 4 + (SPLIT_MAIN[s] + (M_V + t) // SLOTS + 1))
                        for e in range(GROUP):
                            if dc == 0:
                                pe.wait_ge(w_ready, g2 * 16 + (half * 8 + e + 1))
                            at = slice(e * P, (e + 1) * P)
                            last = three(ps[:, s, :], hi[:, s, at], lo[:, s, at], w_hi[half][:, e, :], w_lo[half][:, e, :],
                                         e == 0, e == GROUP - 1)
                        last.then_inc(unit_done[s], 1)

            for b in range(2):
                pe.wait_ge(gelu_done[b], CHUNKS // 2)
            with pe.Fori(0, GROUPS // 2 - 1) as g2:
                second_sweep(g2)
            second_sweep(GROUPS // 2 - 1)
            for s in range(SLOTS):
                pe.wait_ge(acc_added[s], CHUNKS // SLOTS)
            for t in range(TT):
                for k in range(KD):
                    last = nc.tensor.transpose(ps[:, 2 * t + k // 4, (k % 4) * P:(k % 4 + 1) * P], acc[:, k, t * P:(t + 1) * P], ident[:, :])
                last.then_inc(turned, 1)


def kernel(**inputs):
    import numpy as _np
    import concourse.bacc as _bacc
    from concourse import mybir as _mybir
    from concourse.bass_utils import run_bass_kernel_spmd as _run

    a = {k: _np.asarray(v) for k, v in inputs.items()}

    def tiles(w):
        return w.reshape(KD, P, -1, P).transpose(2, 1, 0, 3).reshape(-1, P, D)

    def row_tiles(w):
        return w.reshape(4, 2, P, -1, 512).transpose(3, 0, 2, 1, 4).reshape(-1, P, D)

    def columns(v):
        return v.reshape(-1, P).T

    w_in = a["w_in"][0]
    qk = _np.concatenate([w_in[:, at + (u % 4) * P:at + (u % 4) * P + P] for u in range(HEAD_UNITS)
                          for at in ((0, 512) if u < 4 else (1536, 2048))], axis=1)
    sent = {
        "x": a["x"][0],
        "vecs": _np.concatenate([columns(a["b_ada"][0]), columns(a["g_pre_mix"][0]), columns(a["g_post_mix"][0]),
                                 columns(a["g_pre_ffn"][0]), columns(a["g_post_ffn"][0]), columns(a["c"][0])], axis=1),
        "rows": _np.concatenate([a["g_subln"][0], a["lam_q1"][0], a["lam_k1"][0], a["lam_q2"][0], a["lam_k2"][0]])[None],
        "b_f": a["b_f"].reshape(8, 1),
        "rel_bias": a["rel_bias"],
        "table": bucket_table(),
        "w_fl": w_in[:, 3072:].reshape(KD, P, 8).transpose(1, 0, 2),
        "keys": a["sub_keys"][0].transpose(2, 0, 1),
        "w_ada": tiles(a["w_ada"][0]),
        "w_v": _np.concatenate([row_tiles(w_in[:, 1024:1536]), row_tiles(w_in[:, 2560:3072])]),
        "w_qk": tiles(qk),
        "w_o": row_tiles(a["w_o"][0]),
        "w_pq": tiles(a["w_pq"][0]),
        "peer_u": a["peer_u"][0].reshape(P, CHUNKS, KD, P).transpose(1, 3, 2, 0).reshape(CHUNKS, P, D),
        "peer_v": a["peer_v"][0].reshape(P, GROUPS, GROUP, KD, P).transpose(1, 3, 0, 2, 4).reshape(CHUNKS, P, D),
    }
    nc = _bacc.Bacc("TRN2", target_bir_lowering=False, num_devices=1)
    arrays, args = {}, {}
    for name, array in sent.items():
        arrays[f"in_{name}"] = array = _np.ascontiguousarray(array)
        args[name] = nc.dram_tensor(f"in_{name}", array.shape, _mybir.dt.from_np(array.dtype), kind="ExternalInput").ap()
    args["out"] = nc.dram_tensor("out_0", (T, D), _mybir.dt.float32, kind="ExternalOutput").ap()
    build_layer(nc, **args)
    r = _run(nc, [arrays], core_ids=[0])
    return _np.asarray(r.results[0]["out_0"]).reshape(1, T, D)
```

```python
import math
from contextlib import ExitStack

import numpy as np

import concourse.bass as bass
from concourse import mybir

P = 128
T = 512
D = 1024
TT = T // P
KD = D // P
SLOTS = 4
LEAD = 3
HEAD_UNITS = 8
N_DIFF = 4
N_BUCKETS = 32
MAX_DISTANCE = 128
BIAS_LEN = 640
PEER_HEADS = 8
TOPK = 16
CHUNKS = 128
EPS = 1e-6
LAMBDA_INIT = 0.8 - 0.6 * math.exp(0.0)
MASKED = -1e30
REMOVED = -3e38

A1_PER_HEAD = 6
A1 = PEER_HEADS * A1_PER_HEAD
A2 = 64
A3 = CHUNKS - A1 - A2
M_A2 = PEER_HEADS * 8
M_A3 = M_A2 + A2
M_V = M_A3 + A3
GROUP = 8
GROUPS = CHUNKS // GROUP
TOK = 8
TB = 64

ADA1_TILES = 16
ADA2_PER_UNIT = 4
RAW_V = [4, 4, 4, 4]
RAW_QK = [6, 6]
RAW_ADA2 = 6
RAW_WO = [14, 14, 22, 22]
RAW_MAIN = [16, 16, 24, 24]
SPLIT_V = [0, 0, 0, 0]
SPLIT_QK = [2, 2]
SPLIT_WO = [10, 10, 2, 2]
SPLIT_MAIN = [12, 12, 4, 4]
ADA_V = 4
ADA_END = [4, 4, 20, 20]

CREDIT = 1

SCORE_BANKS = [[(3, 0)], [(3, 1)], [(2, 0), (0, 0)], [(2, 1), (0, 1)], [(1, 0), (1, 1)]]
SCORE_AT = {(3, 0): 0, (3, 1): 512, (2, 0): 1024, (0, 0): 1408, (2, 1): 1536, (0, 1): 1920, (1, 0): 2048, (1, 1): 2304}
BLOCKS = [(3, 2), (2, 4), (0, 4), (1, 5)]
NB = len(SCORE_BANKS)


class Steps:

    def __init__(self, engine, sem):
        self.engine, self.sem, self.turns, self.n = engine, sem, 0, 0

    def after(self, ins):
        self.count(ins)
        self.wait()

    def count(self, ins):
        self.n += 1
        ins.then_inc(self.sem, 1)

    def wait(self):
        self.engine.wait_ge(self.sem, self.turns + self.n)

    def enter(self, turn, steps_per_turn):
        self.first, self.per_turn = self.n, steps_per_turn
        self.turns = turn * steps_per_turn

    def leave(self, turns):
        assert self.n - self.first == self.per_turn, (self.n - self.first, self.per_turn)
        self.turns, self.n = 0, self.first + turns * self.per_turn


def bucket_table():
    table = np.zeros((N_BUCKETS + 1, BIAS_LEN), np.float32)
    exact = N_BUCKETS // 2
    for m in range(BIAS_LEN):
        dist = T - 1 - m
        if dist < 0:
            table[N_BUCKETS, m] = MASKED
        elif dist < exact:
            table[dist, m] = 1.0
        else:
            large = exact + int(math.log(dist / exact) / math.log(MAX_DISTANCE / exact) * (N_BUCKETS - exact))
            table[min(large, N_BUCKETS - 1), m] = 1.0
    return table


def build_layer(nc, x, vecs, rows, g_post, b_ada, b_f, rel_bias, table, w_fl, keys, w_ada, w_v, w_qk, w_o, w_pq, peer_u, peer_v, out):
    F32, F32R, BF16, U32 = mybir.dt.float32, mybir.dt.float32r, mybir.dt.bfloat16, mybir.dt.uint32
    ACT = mybir.ActivationFunctionType
    ALU = mybir.AluOpType
    X_AXIS = mybir.AxisListType.X

    bias_dram = nc.dram_tensor("bias_by_distance", (N_DIFF, BIAS_LEN), F32, kind="Internal").ap()
    cum_dram = nc.dram_tensor("cumulative_forget", (8, T), F32, kind="Internal").ap()
    ncum_dram = nc.dram_tensor("negated_cumulative_forget", (8, T), F32, kind="Internal").ap()
    act_dram = nc.dram_tensor("expert_activations", (CHUNKS, P, T), F32, kind="Internal").ap()
    gate_dram = nc.dram_tensor("expert_gates", (T // TB, P, P, TB), F32, kind="Internal").ap()

    with ExitStack() as ctx:
        def sb(name, shape, dt, scope=ctx):
            return scope.enter_context(nc.sbuf_tensor(name, shape, dt))

        raw = sb("raw", [P, SLOTS, D], F32)
        hi = sb("hi", [P, SLOTS, D], F32R)
        lo = sb("lo", [P, SLOTS, D], F32R)
        xres = sb("xres", [P, TT, D], F32)
        ident = sb("ident", [P, P], F32)
        flip = sb("flip", [P, P], F32)
        ones = sb("ones", [P, P], F32)
        ident_bf = sb("ident_bf", [P, P], BF16)
        causal = sb("causal", [P, P], BF16)
        iota = sb("iota", [P, P], F32)
        keys_sb = sb("keys_sb", [P, 2, P], F32)
        vec = sb("vec", [P, 40], F32)
        row = sb("row", [P, 384], F32)
        gsub = sb("gsub", [P, P], F32)
        silu_c = sb("silu_c", [P, 3, KD], F32)
        shift_cols = sb("shift_cols", [P, 2, KD], F32)
        scale1 = sb("scale1", [P, 2, KD], F32)
        forget_b = sb("forget_b", [8, 1], F32)
        relb = sb("relb", [N_BUCKETS + 1, N_DIFF], F32)
        lam = sb("lam", [P, 8], F32)
        spare = sb("spare", [1, 1], F32)
        lam_prod = sb("lam_prod", [P, 2, 64], F32)
        sumsq = sb("sumsq", [P, 6, TT], F32)
        meansq = sb("meansq", [P, 5, TT], F32)
        rstd = sb("rstd", [P, 5, TT], F32)
        minus_half = sb("minus_half", [P, TT], F32)
        negmax = sb("negmax", [P, 8], F32)
        psums = sb("psums", [P, 8], F32)
        rsums = sb("rsums", [P, 8], F32)
        lrsums = sb("lrsums", [P, 4], F32)
        gg2 = sb("gg2", [P, D], F32)
        with ExitStack() as s:
            aout = sb("aout", [P, 2, T], F32, s)
            pick_t = sb("pick_t", [P, 3, T], F32, s)
        ada_acc = sb("ada_acc", [P, ADA2_PER_UNIT, D], F32)

        with ExitStack() as s:
            ht_hi = sb("ht_hi", [P, KD, T], F32R, s)
            ht_lo = sb("ht_lo", [P, KD, T], F32R, s)
        w_odd_hi = sb("w_odd_hi", [P, GROUP, T], F32R)
        w_odd_lo = sb("w_odd_lo", [P, GROUP, T], F32R)
        with ExitStack() as s:
            work = sb("work", [P, TT, D], F32, s)
        with ExitStack() as s:
            onehot_i = sb("onehot_i", [P, 2, TOK, P], F32, s)
            gated_j = sb("gated_j", [P, 2, TOK, P], F32, s)
        acc = sb("acc", [P, KD, T], F32)
        with ExitStack() as s:
            v_sb = sb("v_sb", [P, TT, D], F32, s)
            probs = sb("probs", [P, 5 * T], F32, s)
            hankel = sb("hankel", [P, N_DIFF, T], F32, s)
            probs_t = sb("probs_t", [P, 2, T], F32, s)
            q_t = sb("q_t", [P, T], F32, s)
            k_t = sb("k_t", [P, T], F32, s)
            aug_q = sb("aug_q", [2, 2, T], F32, s)
            aug_k = sb("aug_k", [2, 2, T], F32, s)
            gg1 = sb("gg1", [P, D], F32, s)
            squares = sb("squares", [P, TT, P], F32, s)
            forget = sb("forget", [8, 3, T], F32, s)
            wfl = sb("wfl", [P, KD, 8], F32, s)
            wfl_hi = sb("wfl_hi", [P, KD, 8], F32R, s)
            wfl_lo = sb("wfl_lo", [P, KD, 8], F32R, s)
            table_sb = v_sb[0:N_BUCKETS + 1, 0, 0:BIAS_LEN]
            bias_row = v_sb[0:N_DIFF, 1, 0:BIAS_LEN]
            ada1_acc = v_sb[:, 2:4, :]
        with ExitStack() as s:
            query = sb("query", [P, 2, T], F32, s)
            top_v = sb("top_v", [P, 2, TT, TOPK], F32, s)
            top_i = sb("top_i", [P, 2, TT, TOPK], U32, s)
            top_f = sb("top_f", [P, 2, TT, TOPK], F32, s)
            left = sb("left", [P, TT, P], F32, s)
            cand = sb("cand", [P, TT, TOPK, TOPK], F32, s)
            cand_left = sb("cand_left", [P, TT, TOPK, TOPK], F32, s)
            best = sb("best", [P, TT, TOPK], F32, s)
            pos = sb("pos", [P, 3, TT, TOPK], U32, s)
            pos_f = sb("pos_f", [P, 2, TT, TOPK], F32, s)
            match = sb("match", [P, 2, TT, TOPK, TOPK], F32, s)
            picked = sb("picked", [P, 3, TT, PEER_HEADS, TOPK], F32, s)
            gate_sum = sb("gate_sum", [P, 2, TT, PEER_HEADS], F32, s)
        with ExitStack() as s:
            gates = sb("gates", [P, 2, P, TB], F32, s)
        w_even_hi = sb("w_even_hi", [P, GROUP, T], F32R)
        w_even_lo = sb("w_even_lo", [P, GROUP, T], F32R)
        a_in = sb("a_in", [P, SLOTS, T], F32)
        g_in = sb("g_in", [P, 2, T // TB, SLOTS, TB], F32)
        w_tmp = sb("w_tmp", [P, 2, T], F32)
        w_hi, w_lo = [w_even_hi, w_odd_hi], [w_even_lo, w_odd_lo]

        ps = ctx.enter_context(nc.psum_tensor("ps", [P, 8, 512], F32))

        def sem(name):
            return ctx.enter_context(nc.semaphore(name))

        vec_loaded = sem("vec_loaded")
        smalls_loaded = sem("smalls_loaded")
        relb_loaded = sem("relb_loaded")
        x_loaded = [sem(f"x_loaded{t}") for t in range(TT)]
        raw_full = [sem(f"raw_full{s}") for s in range(SLOTS)]
        ada_read = [sem(f"ada_read{s}") for s in range(SLOTS)]
        hi_done = [sem(f"hi_done{s}") for s in range(SLOTS)]
        lo_done = [sem(f"lo_done{s}") for s in range(SLOTS)]
        unit_done = [sem(f"unit_done{s}") for s in range(SLOTS)]
        consts_ready = sem("consts_ready")
        pool_steps = sem("pool_steps")
        act_steps = sem("act_steps")
        dve_steps = sem("dve_steps")
        silu_exp = sem("silu_exp")
        lam_dots = sem("lam_dots")
        lam_exps = sem("lam_exps")
        ada_acc_clear = sem("ada_acc_clear")
        ada_bias_loaded = sem("ada_bias_loaded")
        mod_mm = sem("mod_mm")
        gains_loaded = sem("gains_loaded")
        bias_mm = sem("bias_mm")
        bias_row_ready = sem("bias_row_ready")
        bias_stored = sem("bias_stored")
        hankel_loaded = sem("hankel_loaded")
        mod_ready = sem("mod_ready")
        sumsq_done = sem("sumsq_done")
        meansq_ready = sem("meansq_ready")
        rstd_ready = sem("rstd_ready")
        xn_ready = sem("xn_ready")
        turned = sem("turned")
        ht_f32 = sem("ht_f32")
        ht_hi_done = sem("ht_hi_done")
        ht_lo_done = sem("ht_lo_done")
        wfl_hi_done = sem("wfl_hi_done")
        wfl_lo_done = sem("wfl_lo_done")
        forget_mm = sem("forget_mm")
        forget_abs = sem("forget_abs")
        forget_ln = sem("forget_ln")
        cum_ready = sem("cum_ready")
        cum_stored = sem("cum_stored")
        aug_loaded = sem("aug_loaded")
        v_ready = sem("v_ready")
        qk_ready = sem("qk_ready")
        scores_done = sem("scores_done")
        other_rows = sem("other_rows")
        max_done = sem("max_done")
        exp_done = sem("exp_done")
        probs_ready = sem("probs_ready")
        probs_turned = sem("probs_turned")
        probs_t_ready = sem("probs_t_ready")
        pv_done = sem("pv_done")
        heads_out = sem("heads_out")
        spread = sem("spread")
        gg_ready = sem("gg_ready")
        y_ready = sem("y_ready")
        x1_ready = sem("x1_ready")
        query_ready = sem("query_ready")
        key_scores = sem("key_scores")
        level1_done = [sem(f"level1_done{p}") for p in range(2)]
        gate_shifted = sem("gate_shifted")
        gate_exp = sem("gate_exp")
        picks_ready = sem("picks_ready")
        picks_turned = sem("picks_turned")
        ids_ready = sem("ids_ready")
        gelu_done = [sem(f"gelu_done{b}") for b in range(2)]
        act_stored = [sem(f"act_stored{b}") for b in range(2)]
        onehots_ready = [sem(f"onehots_ready{b}") for b in range(2)]
        gate_mm = [sem(f"gate_mm{b}") for b in range(2)]
        gates_staged = [sem(f"gates_staged{b}") for b in range(2)]
        gates_stored = [sem(f"gates_stored{b}") for b in range(2)]
        act_in = [sem(f"act_in{s}") for s in range(SLOTS)]
        gate_in = [sem(f"gate_in{b}") for b in range(2)]
        acc_clear = sem("acc_clear")
        w_f32 = sem("w_f32")
        w_hi_done = sem("w_hi_done")
        w_ready = sem("w_ready")
        acc_added = [sem(f"acc_added{s}") for s in range(SLOTS)]
        out_stored = sem("out_stored")

        block = ctx.enter_context(nc.Block())

        @block.sync
        def _(sp):
            def load(slot, tile, ada_uses, split_uses):
                if ada_uses is not None:
                    sp.wait_ge(ada_read[slot], CREDIT + ada_uses)
                if split_uses is not None:
                    sp.wait_ge(hi_done[slot], split_uses)
                    sp.wait_ge(lo_done[slot], split_uses)
                sp.dma_start(raw[:, slot, :], tile).then_inc(raw_full[slot], 16)

            def tile_of(dram, n):
                return dram[n] if isinstance(n, int) else dram[bass.ds(n, 1), :, :].rearrange("o p n -> (o p) n")

            sp.dma_start(vec[:, :], vecs).then_inc(vec_loaded, 16)
            for s in range(SLOTS):
                load(s, w_ada[s], None, None)
            with sp.Fori(0, ADA1_TILES // SLOTS - 1) as j:
                for s in range(SLOTS):
                    load(s, tile_of(w_ada, (j + 1) * SLOTS + s), j + 1, None)
            for n in range(2 * SLOTS):
                load(n % SLOTS, w_v[n], ADA_V, n // SLOTS if n >= SLOTS else None)

            def load_qk(u):
                for s in range(2):
                    load(s, tile_of(w_qk, u * 2 + s), None, u + SPLIT_QK[s])

            def load_ada2(u):
                for i in range(ADA2_PER_UNIT):
                    s = 2 + i % 2
                    load(s, tile_of(w_ada, u + (ADA1_TILES + i * KD)), u * 2 + (ADA_V + i // 2), SPLIT_QK[0])

            load_qk(0)
            load_qk(1)
            with sp.Fori(0, HEAD_UNITS - 2) as u:
                load_ada2(u)
                load_qk(u + 2)
            with sp.Fori(HEAD_UNITS - 2, HEAD_UNITS) as u:
                load_ada2(u)
            for n in range(2 * SLOTS):
                s = n % SLOTS
                load(s, w_o[n], ADA_END[s], SPLIT_WO[s] + n // SLOTS)
            with sp.Fori(0, PEER_HEADS) as h:
                for t in range(8):
                    s = t % SLOTS
                    tile = tile_of(w_pq, h * 2 + t) if t < 2 else tile_of(peer_u, h * A1_PER_HEAD + (t - 2))
                    load(s, tile, None, h * 2 + (SPLIT_MAIN[s] + t // SLOTS))

            def load_u(j):
                for s in range(SLOTS):
                    load(s, tile_of(peer_u, j * SLOTS + (A1 + s)), None, j + (SPLIT_MAIN[s] + M_A2 // SLOTS))

            with sp.Fori(0, (A2 + A3) // SLOTS - 1) as j:
                load_u(j)

            def load_act(n, slot, multiplied):
                if multiplied is not None:
                    sp.wait_ge(w_f32, multiplied)
                chunk = slice(n, n + 1) if isinstance(n, int) else bass.ds(n, 1)
                sp.dma_start(a_in[:, slot, :], act_dram[chunk, :, :].rearrange("o p t -> (o p) t")).then_inc(act_in[slot], 16)

            def load_gates(q, buffer, multiplied):
                if multiplied is not None:
                    sp.wait_ge(w_f32, multiplied)
                four = slice(q * SLOTS, q * SLOTS + SLOTS) if isinstance(q, int) else bass.ds(q * SLOTS, SLOTS)
                sp.dma_start(g_in[:, buffer, :, :, :].rearrange("i b j t -> i b (j t)"),
                             gate_dram[:, :, four, :].rearrange("b i j t -> i b (j t)")).then_inc(gate_in[buffer], 16)

            for b in range(2):
                sp.wait_ge(gates_stored[b], CREDIT + 16 * (T // TB // 2))
                sp.wait_ge(act_stored[b], CREDIT + 16 * (A1 + A2) // 2)
            load_gates(0, 0, None)
            for n in range(SLOTS):
                load_act(n, n, None)
            load_gates(1, 1, None)
            load_u((A2 + A3) // SLOTS - 1)

            def load_v(j, with_act, with_gates):
                for parity in range(2):
                    for s in range(SLOTS):
                        load(s, tile_of(peer_v, (j * 2 + parity) * SLOTS + s), None, (j * 2 + parity) + (SPLIT_MAIN[s] + M_V // SLOTS))
                        if with_act[parity]:
                            load_act((j * 2 + parity) * SLOTS + (SLOTS + s), s, (j * 2 + parity) * SLOTS + (s + 1))
                    if with_gates[parity]:
                        load_gates((j * 2 + parity) + 2, parity, (j * 2 + parity) * SLOTS + SLOTS)

            both, one, none = (True, True), (True, False), (False, False)
            last_chunks = (A1 + A2) // GROUP - 1
            with sp.Fori(0, last_chunks) as j:
                load_v(j, both, both)
            for b in range(2):
                sp.wait_ge(act_stored[b], CREDIT + 16 * CHUNKS // 2)
            with sp.Fori(last_chunks, GROUPS - 1) as j:
                load_v(j, both, both)
            load_v(GROUPS - 1, one, none)

        @block.gpsimd
        def _(pool):
            steps = Steps(pool, pool_steps)
            nc.gpsimd.memset(ident[:, :], 0.0).then_inc(pool_steps, 1)
            nc.gpsimd.memset(flip[:, :], 0.0).then_inc(pool_steps, 1)
            nc.gpsimd.memset(causal[:, :], 0.0).then_inc(pool_steps, 1)
            nc.gpsimd.memset(ident_bf[:, :], 0.0).then_inc(pool_steps, 1)
            nc.gpsimd.memset(ones[:, :], 1.0).then_inc(consts_ready, 1)
            nc.gpsimd.memset(aug_q[:, :, :], 1.0).then_inc(pool_steps, 1)
            nc.gpsimd.memset(aug_k[:, :, :], 1.0).then_inc(pool_steps, 1)
            nc.gpsimd.memset(relb[:, :], 1.0).then_inc(pool_steps, 1)
            nc.gpsimd.memset(minus_half[:, :], -0.5).then_inc(pool_steps, 1)
            steps.n = 8
            steps.wait()
            pool.dma_start(relb[0:N_BUCKETS, :], rel_bias).then_inc(relb_loaded, 16)
            for m in (ident, ident_bf):
                nc.gpsimd.affine_select(out=m[:, :], in_=m[:, :], compare_op=ALU.not_equal, fill=1.0, base=0,
                                        pattern=[[-1, P]], channel_multiplier=1).then_inc(consts_ready, 1)
            nc.gpsimd.affine_select(out=flip[:, :], in_=flip[:, :], compare_op=ALU.not_equal, fill=1.0,
                                    base=-(P - 1), pattern=[[1, P]], channel_multiplier=1).then_inc(consts_ready, 1)
            nc.gpsimd.affine_select(out=causal[:, :], in_=causal[:, :], compare_op=ALU.is_ge, fill=MASKED, base=0,
                                    pattern=[[-1, P]], channel_multiplier=1).then_inc(consts_ready, 1)
            nc.gpsimd.iota(iota[:, :], pattern=[[1, P]], base=0, channel_multiplier=0,
                           allow_small_or_imprecise_dtypes=True).then_inc(consts_ready, 1)
            nc.gpsimd.memset(ada_acc[:, :, :], 0.0).then_inc(ada_acc_clear, 1)
            pool.wait_ge(ada_acc_clear, 1)
            pool.dma_start(ada_acc[0:1, :, :], b_ada.rearrange("o (i n) -> o i n", n=D)).then_inc(ada_bias_loaded, 16)
            for n, gg in enumerate((gg1, gg2)):
                pool.dma_start(gg[:, :], bass.AP(g_post.tensor, n * D, [[0, P], [1, D]])).then_inc(gains_loaded, 16)

            def root(n, norm):
                pool.wait_ge(meansq_ready, n)
                nc.gpsimd.tensor_tensor(rstd[:, norm, :], meansq[:, norm, :], minus_half[:, :],
                                        ALU.pow).then_inc(rstd_ready, 1)

            pool.wait_ge(bias_row_ready, 1)
            pool.dma_start(bias_dram, bias_row).then_inc(bias_stored, 16)
            pool.wait_ge(bias_stored, 16)
            pool.dma_start(hankel[:, :, :],
                           bass.AP(bias_dram.tensor, 0, [[1, P], [BIAS_LEN, N_DIFF], [1, T]])).then_inc(hankel_loaded, 16)
            root(1, 0)
            pool.wait_ge(cum_ready, 1)
            pool.dma_start(cum_dram, forget[:, 1, :]).then_inc(cum_stored, 16)
            pool.dma_start(ncum_dram, forget[:, 2, :]).then_inc(cum_stored, 16)
            pool.wait_ge(cum_stored, 32)

            def load_aug(pair, scores_before):
                if scores_before is not None:
                    pool.wait_ge(scores_done, scores_before)
                    pool.wait_ge(aug_loaded, pair * 32)
                first = pair * 2
                at = slice(0, 2) if isinstance(pair, int) else bass.ds(first, 2)
                pool.dma_start(aug_q[0:1, :, :], cum_dram[at, :].rearrange("(o h) t -> o h t", o=1)).then_inc(aug_loaded, 16)
                pool.dma_start(aug_k[1:2, :, :], ncum_dram[at, :].rearrange("(o h) t -> o h t", o=1)).then_inc(aug_loaded, 16)

            load_aug(0, None)
            with pool.Fori(0, N_DIFF) as u:
                root(u + 2, 1)
            with pool.Fori(0, 3) as p:
                load_aug(p + 1, p * NB + (N_DIFF + 1) * NB)
            root(6, 2)
            root(7, 3)

            for b in range(2):
                pool.wait_ge(gate_mm[b], CREDIT + A2 // 2)
            nc.gpsimd.memset(acc[:, :, :], 0.0).then_inc(acc_clear, 1)
            root(8, 4)

        @block.scalar
        def _(act):
            steps = Steps(act, act_steps)

            def split_hi(slot, raw_use, split_use):
                act.wait_ge(raw_full[slot], raw_use * 16 + 16)
                act.wait_ge(unit_done[slot], split_use)
                nc.scalar.activation(hi[:, slot, :], raw[:, slot, :], ACT.Copy).then_inc(hi_done[slot], 1)

            def split_hi_main(t, turn):
                s, k = t % SLOTS, t // SLOTS
                split_hi(s, turn + (RAW_MAIN[s] + k), turn + (SPLIT_MAIN[s] + k))

            for s in (exp_done, probs_t_ready, query_ready, *gelu_done, *gates_staged, *act_stored, *gates_stored):
                act.sem_inc(s, CREDIT)
            act.dma_start(table_sb, table).then_inc(smalls_loaded, 16)
            act.dma_start(keys_sb[:, :, :], keys).then_inc(smalls_loaded, 16)
            act.dma_start(row[:, :], bass.AP(rows.tensor, 0, [[0, P], [1, 384]])).then_inc(smalls_loaded, 16)
            act.dma_start(forget_b[:, :], b_f).then_inc(smalls_loaded, 16)
            act.dma_start(wfl[:, :, :], w_fl).then_inc(smalls_loaded, 16)
            for t in range(TT):
                act.dma_start(xres[:, t, :], x[t * P:(t + 1) * P, :]).then_inc(x_loaded[t], 16)
            act.wait_ge(vec_loaded, 16)
            nc.scalar.activation(silu_c[:, 0, :], vec[:, 32:40], ACT.Exp, scale=-1.0).then_inc(silu_exp, 1)
            act.wait_ge(lam_dots, 1)
            nc.scalar.activation(lam[:, 2:4], lam[:, 0:2], ACT.Exp).then_inc(lam_exps, 1)
            for t in range(TT):
                act.wait_ge(x_loaded[t], 16)
                nc.scalar.activation(work[:, t, :], xres[:, t, :], ACT.Square,
                                     accum_out=sumsq[:, 0, t:t + 1]).then_inc(sumsq_done, 1)
            act.wait_ge(smalls_loaded, 5 * 16)
            nc.scalar.activation(wfl_hi[:, :, :], wfl[:, :, :], ACT.Copy).then_inc(wfl_hi_done, 1)

            def affine_ht(base, which):
                for k in range(KD):
                    act.wait_ge(turned, base + k + 1)
                    if k >= 2 or base:
                        act.wait_ge(ht_lo_done, base + k - 1 if k >= 2 else base)
                    shift = shift_cols[:, which, k:k + 1]
                    act.activation(probs[:, (k % 2) * T:(k % 2 + 1) * T], ps[:, k % 2, :], ACT.Identity, bias=shift,
                                   scale=scale1[:, which, k:k + 1]).then_inc(ht_f32, 1)
                    act.wait_ge(ht_f32, which * KD + k + 1)
                    act.activation(ht_hi[:, k, :], probs[:, (k % 2) * T:(k % 2 + 1) * T], ACT.Copy).then_inc(ht_hi_done, 1)

            act.wait_ge(mod_ready, 1)
            affine_ht(0, 0)
            for n in range(SLOTS):
                split_hi(n, RAW_V[n], 0)
            act.wait_ge(forget_abs, 1)
            nc.scalar.activation(forget[:, 2, :], forget[:, 1, :], ACT.Exp).then_inc(forget_ln, 1)
            act.wait_ge(forget_ln, 1)
            nc.scalar.activation(forget[:, 1, :], forget[:, 2, :], ACT.Ln, bias=1.0).then_inc(forget_ln, 1)
            for n in range(SLOTS):
                split_hi(n, RAW_V[n] + 1, 1)
            act.wait_ge(unit_done[3], 1)
            for t in range(2):
                act.activation(v_sb[:, t, 0:512], ps[:, t, :], ACT.Copy).then_inc(v_ready, 1)
            for s in range(2):
                split_hi(s, RAW_QK[s], SPLIT_QK[s])
            act.wait_ge(unit_done[3], 2)
            for t in range(2):
                act.activation(v_sb[:, t, 512:1024], ps[:, 4 + t, :], ACT.Copy).then_inc(v_ready, 1)

            def evacuate_qk(u):
                act.wait_ge(unit_done[0], u + (SPLIT_QK[0] + 1))
                act.activation(q_t[:, :], ps[:, 5, :], ACT.Copy, scale=0.125).then_inc(qk_ready, 1)
                act.wait_ge(unit_done[1], u + (SPLIT_QK[1] + 1))
                act.activation(k_t[:, :], ps[:, 6, :], ACT.Copy).then_inc(qk_ready, 1)

            evacuate_qk(0)

            def attention(u, fox, last, jobs_before):
                if not last:
                    for s in range(2):
                        split_hi(s, u + (RAW_QK[s] + 1), u + (SPLIT_QK[s] + 1))
                for b, held in enumerate(SCORE_BANKS):
                    act.wait_ge(max_done, u * NB + (b + 1))
                    for i, m in held:
                        at, w, c = SCORE_AT[i, m], (i + 1) * P, 2 * i + m
                        last_exp = act.activation(probs[:, at:at + w], ps[:, b, at % 512:at % 512 + w], ACT.Exp,
                                                  bias=negmax[:, c:c + 1], accum_out=psums[:, c:c + 1])
                    last_exp.then_inc(exp_done, 1)
                if not last:
                    evacuate_qk(u + 1)
                jobs = [(i, m) for i, _ in BLOCKS for m in range(1 + fox)]
                for n, (i, m) in enumerate(jobs):
                    act.wait_ge(probs_turned, jobs_before + (n + 1))
                    if n >= 2:
                        act.wait_ge(pv_done, jobs_before + (n - 1))
                    w = (i + 1) * P
                    act.activation(probs_t[:, n % 2, 0:w], ps[:, 5 + n % 2, 0:w], ACT.Copy).then_inc(probs_t_ready, 1)
                if not fox:
                    act.wait_ge(pv_done, jobs_before + 4)
                    act.wait_ge(heads_out, u * 4 + CREDIT)
                    for i in range(TT):
                        act.activation(squares[:, i, :], ps[:, 7, i * P:(i + 1) * P], ACT.Square,
                                       accum_out=sumsq[:, 1, i:i + 1]).then_inc(sumsq_done, 1)

            with act.Fori(0, N_DIFF) as u:
                attention(u, False, False, u * 4)
            with act.Fori(0, 3) as p:
                attention(p + N_DIFF, True, False, p * 8 + 16)
            attention(7, True, True, 16 + 24)

            for s in range(SLOTS):
                split_hi(s, RAW_WO[s], SPLIT_WO[s])
            for k in range(KD):
                act.wait_ge(turned, KD + k + 1)
                act.activation(ht_hi[:, k, :], ps[:, k % 2, :], ACT.Copy).then_inc(ht_hi_done, 1)
            for s in range(SLOTS):
                split_hi(s, RAW_WO[s] + 1, SPLIT_WO[s] + 1)
            act.wait_ge(unit_done[3], SPLIT_WO[3] + 1)
            for t in range(2):
                act.activation(work[:, t, 0:512], ps[:, t, :], ACT.Copy).then_inc(y_ready, 1)
            act.wait_ge(y_ready, TT)
            for t in range(TT):
                act.activation(v_sb[:, t, 0:512], ps[:, t, :], ACT.Square, accum_out=sumsq[:, 2, t:t + 1]).then_inc(sumsq_done, 1)
            for t in range(LEAD):
                split_hi_main(t, 0)
            act.wait_ge(unit_done[3], SPLIT_WO[3] + 2)
            for t in range(TT):
                act.activation(v_sb[:, t, 512:1024], ps[:, 4 + t, :], ACT.Square,
                               accum_out=sumsq[:, 5, t:t + 1]).then_inc(sumsq_done, 1)
            for t in range(TT):
                act.wait_ge(x1_ready, t + 1)
                act.activation(v_sb[:, t, :], xres[:, t, :], ACT.Square,
                               accum_out=sumsq[:, 3, t:t + 1]).then_inc(sumsq_done, 1)
            act.wait_ge(mod_ready, 2)
            affine_ht(2 * KD, 1)

            def gelu(parity, uses, chunk):
                act.wait_ge(act_stored[parity], uses * 16 + CREDIT)
                act.activation(aout[:, parity, :], ps[:, parity, :], ACT.Gelu_apprx_tanh).then_inc(gelu_done[parity], 1)
                act.wait_ge(gelu_done[parity], uses + (CREDIT + 1))
                act.dma_start(act_dram[bass.ds(chunk, 1), :, :].rearrange("o p t -> (o p) t") if not isinstance(chunk, int)
                              else act_dram[chunk], aout[:, parity, :]).then_inc(act_stored[parity], 16)

            def unit_end(t, turn):
                s = t % SLOTS
                act.wait_ge(unit_done[s], turn + (SPLIT_MAIN[s] + t // SLOTS + 1))

            with act.Fori(0, PEER_HEADS) as h:
                for t in range(8):
                    split_hi_main(t + LEAD, h * 2)
                    unit_end(t, h * 2)
                    if t < 2:
                        act.wait_ge(key_scores, h * 2 + CREDIT)
                        act.activation(query[:, t, :], ps[:, 4 + t, :], ACT.Copy).then_inc(query_ready, 1)
                    else:
                        gelu(t % 2, h * 3 + (t - 2) // 2, h * A1_PER_HEAD + (t - 2))
            act.wait_ge(gate_shifted, 1)
            act.activation(picked[:, 2], picked[:, 2], ACT.Exp).then_inc(gate_exp, 1)

            def gates_out(t, r):
                half, par = t // 8, t % 2
                act.wait_ge(gate_mm[par], r * 8 + (t // 2 + 1 + CREDIT))
                if t % 8 == 0:
                    act.wait_ge(gates_stored[half], r * 16 + CREDIT)
                at = (t % 8) * TOK
                act.activation(gates[:, half, :, at:at + TOK],
                               ps[:, 2 + 2 * par:4 + 2 * par, :].rearrange("p a (q j) -> p j (a q)", j=P),
                               ACT.Copy).then_inc(gates_staged[par], 1)
                if t % 8 == 7:
                    for b in range(2):
                        act.wait_ge(gates_staged[b], r * 8 + (4 * (half + 1) + CREDIT))
                    act.dma_start(gate_dram[bass.ds(r * 2 + half, 1), :, :, :].rearrange("o i j t -> (o i) j t"),
                                  gates[:, half, :, :]).then_inc(gates_stored[half], 16)

            with act.Fori(0, A2 // 16) as r:
                for t in range(16):
                    split_hi_main(t + LEAD + M_A2, r * 4)
                    unit_end(t + M_A2, r * 4)
                    gelu(t % 2, r * 8 + (A1 + t) // 2, r * 16 + (A1 + t))
                    if t:
                        gates_out(t - 1, r)
                gates_out(15, r)

            def split_w_hi(n, buffer, e, turn, tile):
                act.wait_ge(w_f32, n + 1)
                if e == 0:
                    unit_end(tile, turn)
                act.activation(w_hi[buffer][:, e, :], w_tmp[:, e % 2, :], ACT.Copy).then_inc(w_hi_done, 1)

            for t in range(A3):
                split_hi_main(t + LEAD + M_A3, 0)
                unit_end(t + M_A3, 0)
                gelu(t % 2, (A1 + A2 + t) // 2, A1 + A2 + t)
                if t >= A3 - GROUP:
                    e = t - (A3 - GROUP)
                    split_w_hi(e, 0, e, 0, M_A2 - 1)

            def second_sweep(g2, last):
                for half in range(2):
                    for dc in range(KD):
                        t = half * 8 + dc
                        final_half = last and half == 1
                        if not (final_half and dc + LEAD >= KD):
                            split_hi_main(t + LEAD + M_V, g2 * 4)
                        if not final_half:
                            split_w_hi(g2 * 16 + (GROUP + t), 1 - half, dc, g2 * 4, M_V + half * 8 - 1)

            with act.Fori(0, GROUPS // 2 - 1) as g2:
                second_sweep(g2, False)
            second_sweep(GROUPS // 2 - 1, True)

            for t in range(TT):
                act.wait_ge(turned, 3 * KD + t + 1)
                act.activation(raw[:, t, :], ps[:, 2 * t:2 * t + 2, :].rearrange("p a n -> p (a n)"), ACT.Square,
                               accum_out=sumsq[:, 4, t:t + 1]).then_inc(sumsq_done, 1)
            for t in range(TT):
                act.wait_ge(x1_ready, TT + t + 1)
                act.dma_start(out[t * P:(t + 1) * P, :], xres[:, t, :]).then_inc(out_stored, 16)
            act.wait_ge(out_stored, 16 * TT)

        @block.vector
        def _(dve):
            steps = Steps(dve, dve_steps)
            V = nc.vector

            def split_lo(slot, split_use):
                dve.wait_ge(hi_done[slot], split_use + 1)
                V.tensor_tensor(lo[:, slot, :], raw[:, slot, :], hi[:, slot, :].bitcast(F32),
                                ALU.subtract).then_inc(lo_done[slot], 1)

            def split_lo_main(t, turn):
                s = t % SLOTS
                split_lo(s, turn + (SPLIT_MAIN[s] + t // SLOTS))

            def mean_square(norm, n, width):
                dve.wait_ge(sumsq_done, n)
                V.tensor_scalar(meansq[:, norm, :], sumsq[:, norm, :], 1.0 / width, EPS, ALU.mult, ALU.add).then_inc(meansq_ready, 1)

            for s in (heads_out, *level1_done, *acc_added, *ada_read):
                dve.sem_inc(s, CREDIT)
            dve.wait_ge(silu_exp, 1)
            steps.after(V.tensor_scalar(silu_c[:, 1, :], silu_c[:, 0, :], 1.0, None, ALU.add))
            steps.after(V.reciprocal(silu_c[:, 2, :], silu_c[:, 1, :]))
            steps.after(V.tensor_tensor(silu_c[:, 0, :], silu_c[:, 2, :], vec[:, 32:40], ALU.mult))

            def ada1(o):
                for k in range(KD):
                    n = o * KD + k
                    slot, use = n % SLOTS, n // SLOTS
                    dve.wait_ge(raw_full[slot], use * 16 + 16)
                    if k == 0:
                        done = V.tensor_scalar(ada1_acc[:, o, :], raw[:, slot, :], silu_c[:, 0, k:k + 1], None, ALU.mult)
                    else:
                        dve.wait_ge(ada_read[(n - 1) % SLOTS], CREDIT + (n - 1) // SLOTS + 1)
                        done = V.scalar_tensor_tensor(ada1_acc[:, o, :], raw[:, slot, :], silu_c[:, 0, k:k + 1],
                                                      ada1_acc[:, o, :], ALU.mult, ALU.add)
                    done.then_inc(ada_read[slot], 1)

            ada1(0)
            dve.wait_ge(smalls_loaded, 5 * 16)
            for m in range(2):
                steps.count(V.tensor_tensor(lam_prod[:, m, :], row[:, 128 + 128 * m:192 + 128 * m],
                                            row[:, 192 + 128 * m:256 + 128 * m], ALU.mult))
            steps.wait()
            V.tensor_reduce(lam[:, 0:2], lam_prod[:, :, :], X_AXIS, ALU.add).then_inc(lam_dots, 1)
            dve.wait_ge(bias_mm, 2)
            steps.after(V.tensor_copy(bias_row[:, 0:512], ps[0:N_DIFF, 2, :]))
            V.tensor_copy(bias_row[:, 512:BIAS_LEN], ps[0:N_DIFF, 3, 0:BIAS_LEN - 512]).then_inc(bias_row_ready, 1)
            mean_square(0, 4, D)
            dve.wait_ge(wfl_hi_done, 1)
            V.tensor_tensor(wfl_lo[:, :, :], wfl[:, :, :], wfl_hi[:, :, :].bitcast(F32), ALU.subtract).then_inc(wfl_lo_done, 1)
            ada1(1)

            def normalise(n, norm):
                dve.wait_ge(rstd_ready, n)
                for t in range(TT):
                    V.tensor_scalar(work[:, t, :], xres[:, t, :], rstd[:, norm, t:t + 1], None, ALU.mult).then_inc(xn_ready, 1)

            normalise(1, 0)
            dve.wait_ge(lam_exps, 1)
            steps.after(V.tensor_tensor(lam[:, 4:5], lam[:, 3:4], lam[:, 2:3], ALU.subtract))
            steps.after(V.tensor_scalar(lam[:, 5:6], lam[:, 4:5], -LAMBDA_INIT, None, ALU.add))
            steps.count(V.tensor_scalar(gsub[:, :], row[:, 0:P], 1.0 - LAMBDA_INIT, None, ALU.mult))
            dve.wait_ge(mod_mm, 1)
            steps.count(V.tensor_tensor(shift_cols[:, 0, :], ps[:, 7, 0:8], vec[:, 0:8], ALU.add))
            steps.after(V.tensor_tensor(scale1[:, 1, :], ps[:, 7, 8:16], vec[:, 8:16], ALU.add))
            V.scalar_tensor_tensor(scale1[:, 0, :], scale1[:, 1, :], 1.0, vec[:, 16:24], ALU.add, ALU.mult).then_inc(mod_ready, 1)

            def ht_remainder(base, source):
                for k in range(KD):
                    dve.wait_ge(ht_hi_done, base + k + 1)
                    V.tensor_tensor(ht_lo[:, k, :], source(k), ht_hi[:, k, :].bitcast(F32), ALU.subtract).then_inc(ht_lo_done, 1)

            ht_remainder(0, lambda k: probs[:, (k % 2) * T:(k % 2 + 1) * T])
            for n in range(SLOTS):
                split_lo(n, 0)
            dve.wait_ge(forget_mm, 1)
            steps.after(V.tensor_scalar(forget[:, 0, :], ps[0:8, 6, :], forget_b[:, 0:1], None, ALU.add))
            steps.after(V.tensor_scalar(forget[:, 2, :], forget[:, 0, :], -1.0, None, ALU.mult))
            V.tensor_tensor(forget[:, 1, :], forget[:, 0, :], forget[:, 2, :], ALU.min).then_inc(forget_abs, 1)
            dve.wait_ge(forget_ln, 2)
            steps.after(V.scalar_tensor_tensor(forget[:, 2, :], forget[:, 0, :], 0.0, forget[:, 1, :], ALU.min, ALU.subtract))
            steps.after(V.memset(forget[:, 0, :], 1.0))
            steps.after(V.tensor_tensor_scan(forget[:, 1, :], forget[:, 0, :], forget[:, 2, :], 0.0, ALU.mult, ALU.add))
            V.tensor_scalar(forget[:, 2, :], forget[:, 1, :], -1.0, None, ALU.mult).then_inc(cum_ready, 1)
            for n in range(SLOTS):
                split_lo(n, 1)
            dve.wait_ge(unit_done[3], 1)
            for t in range(2, TT):
                V.tensor_copy(v_sb[:, t, 0:512], ps[:, t, :]).then_inc(v_ready, 1)
            for s in range(2):
                split_lo(s, SPLIT_QK[s])
            dve.wait_ge(unit_done[3], 2)
            for t in range(2, TT):
                V.tensor_copy(v_sb[:, t, 512:1024], ps[:, 4 + t, :]).then_inc(v_ready, 1)

            def ada2(u, i):
                s = 2 + i % 2
                dve.wait_ge(raw_full[s], u * 32 + 16 * (RAW_ADA2 + i // 2 + 1))
                dve.wait_ge(ada_read[s], u * 2 + (CREDIT + ADA_V + i // 2))
                V.scalar_tensor_tensor(ada_acc[:, i, :], raw[:, s, :], silu_c[:, 0, u:u + 1] if isinstance(u, int) else silu_c[:, 0, bass.ds(u, 1)],
                                       ada_acc[:, i, :], ALU.mult, ALU.add).then_inc(ada_read[s], 1)

            dve.wait_ge(ada_bias_loaded, 16)

            def attention(u, fox, last):
                if not last:
                    for s in range(2):
                        split_lo(s, u + (SPLIT_QK[s] + 1))
                for b, held in enumerate(SCORE_BANKS):
                    dve.wait_ge(scores_done, u * NB + (b + 1))
                    if b == NB - 1:
                        V.tensor_reduce(negmax[:, 2:4], ps[:, b, :].rearrange("p (m k) -> p m k", m=2), X_AXIS, ALU.max,
                                        negate=True).then_inc(max_done, 1)
                        continue
                    for i, m in held:
                        at, w, c = SCORE_AT[i, m] % 512, (i + 1) * P, 2 * i + m
                        last_max = V.tensor_reduce(negmax[:, c:c + 1], ps[:, b, at:at + w], X_AXIS, ALU.max, negate=True)
                    last_max.then_inc(max_done, 1)
                for i in range(2):
                    ada2(u, i)
                for i, banks in BLOCKS:
                    w, c = (i + 1) * P, 2 * i
                    p0 = probs[:, SCORE_AT[i, 0]:SCORE_AT[i, 0] + w]
                    p1 = probs[:, SCORE_AT[i, 1]:SCORE_AT[i, 1] + w]
                    dve.wait_ge(exp_done, u * NB + (banks + CREDIT))
                    steps.after(V.reciprocal(rsums[:, c:c + 2], psums[:, c:c + 2]))
                    if fox:
                        V.tensor_scalar(p0, p0, rsums[:, c:c + 1], None, ALU.mult).then_inc(probs_ready, 1)
                        V.tensor_scalar(p1, p1, rsums[:, c + 1:c + 2], None, ALU.mult).then_inc(probs_ready, 1)
                    else:
                        steps.after(V.tensor_tensor(lrsums[:, i:i + 1], rsums[:, c + 1:c + 2], lam[:, 5:6], ALU.mult))
                        steps.after(V.tensor_scalar(p1, p1, lrsums[:, i:i + 1], None, ALU.mult))
                        V.scalar_tensor_tensor(p0, p0, rsums[:, c:c + 1], p1, ALU.mult, ALU.add).then_inc(probs_ready, 1)
                for i in range(2, ADA2_PER_UNIT):
                    ada2(u, i)

            with dve.Fori(0, N_DIFF) as u:
                steps.enter(u, 4 * 3)
                attention(u, False, False)
                mean_square(1, u * 4 + 8, P)
                dve.wait_ge(rstd_ready, u + 2)
                for i in range(TT):
                    V.scalar_tensor_tensor(work[:, i, bass.ds(u * P, P)], ps[:, 7, i * P:(i + 1) * P], rstd[:, 1, i:i + 1],
                                           gsub[:, :], ALU.mult, ALU.mult).then_inc(heads_out, 1)
                steps.leave(N_DIFF)

            def fox_out(u, jobs):
                dve.wait_ge(pv_done, jobs)
                for i in range(TT):
                    V.tensor_copy(work[:, i, bass.ds(u * P, P)], ps[:, 7, i * P:(i + 1) * P]).then_inc(heads_out, 1)

            with dve.Fori(0, 3) as p:
                steps.enter(p, 4)
                attention(p + N_DIFF, True, False)
                fox_out(p + N_DIFF, p * 8 + 24)
                steps.leave(3)
            attention(7, True, True)
            fox_out(7, 48)

            for s in range(SLOTS):
                split_lo(s, SPLIT_WO[s])
            ht_remainder(KD, lambda k: ps[:, k % 2, :])
            dve.wait_ge(gains_loaded, 32)
            for n, gg in enumerate((gg1, gg2)):
                dve.wait_ge(spread, n + 1)
                V.tensor_tensor(gg[:, :], gg[:, :], ps[:, 4 + 2 * n:6 + 2 * n, :].rearrange("p a n -> p (a n)"),
                                ALU.mult).then_inc(gg_ready, 1)
            for s in range(SLOTS):
                split_lo(s, SPLIT_WO[s] + 1)
            dve.wait_ge(unit_done[3], SPLIT_WO[3] + 1)
            for t in range(2, TT):
                V.tensor_copy(work[:, t, 0:512], ps[:, t, :]).then_inc(y_ready, 1)
            for t in range(LEAD):
                split_lo_main(t, 0)
            dve.wait_ge(sumsq_done, 28)
            steps.after(V.tensor_tensor(sumsq[:, 2, :], sumsq[:, 2, :], sumsq[:, 5, :], ALU.add))
            mean_square(2, 28, D)
            dve.wait_ge(rstd_ready, 6)
            dve.wait_ge(gg_ready, 2)
            dve.wait_ge(y_ready, TT)
            for t in range(TT):
                steps.count(V.scalar_tensor_tensor(work[:, t, 0:512], work[:, t, 0:512], rstd[:, 2, t:t + 1],
                                                   gg1[:, 0:512], ALU.mult, ALU.mult))
                steps.after(V.scalar_tensor_tensor(work[:, t, 512:1024], ps[:, 4 + t, :], rstd[:, 2, t:t + 1],
                                                   gg1[:, 512:1024], ALU.mult, ALU.mult))
                V.tensor_tensor(xres[:, t, :], xres[:, t, :], work[:, t, :], ALU.add).then_inc(x1_ready, 1)
            dve.wait_ge(mod_mm, 2)
            steps.count(V.tensor_copy(shift_cols[:, 1, :], ps[:, 2, 0:8]))
            V.scalar_tensor_tensor(scale1[:, 1, :], ps[:, 2, 8:16], 1.0, vec[:, 24:32], ALU.add, ALU.mult).then_inc(mod_ready, 1)
            mean_square(3, 32, D)
            normalise(7, 3)
            ht_remainder(2 * KD, lambda k: probs[:, (k % 2) * T:(k % 2 + 1) * T])

            def apart():
                steps.count(V.memset(spare[0:1, 0:1], 0.0))

            def level1(p, h):
                s = lambda t: ps[:, 6 + p, t * P:(t + 1) * P]
                dve.wait_ge(key_scores, h * 2 + (p + 1 + CREDIT))
                apart()
                for t in range(TT):
                    steps.count(V.max(top_v[:, p, t, 0:8], s(t)))
                steps.wait()
                apart()
                for t in range(TT):
                    steps.count(V.match_replace(left[:, t, :], top_v[:, p, t, 0:8], s(t), REMOVED))
                for t in range(TT):
                    steps.count(V.max_index(top_i[:, p, t, 0:8], top_v[:, p, t, 0:8], s(t)))
                steps.wait()
                apart()
                for t in range(TT):
                    steps.count(V.max(top_v[:, p, t, 8:16], left[:, t, :]))
                steps.wait()
                apart()
                for t in range(TT):
                    steps.count(V.max_index(top_i[:, p, t, 8:16], top_v[:, p, t, 8:16], left[:, t, :]))
                steps.wait()
                V.tensor_copy(top_f[:, p], top_i[:, p]).then_inc(level1_done[p], 1)

            def level2_first():
                b = top_v[:, 1].unsqueeze(2).to_broadcast([P, TT, TOPK, TOPK])
                steps.count(V.tensor_tensor(cand[:, :, :, :], top_v[:, 0].unsqueeze(3).to_broadcast([P, TT, TOPK, TOPK]), b, ALU.add))
                steps.wait()
                apart()
                for t in range(TT):
                    steps.count(V.max(best[:, t, 0:8], cand[:, t].rearrange("p a b -> p (a b)")))
                steps.wait()
                apart()
                for t in range(TT):
                    steps.count(V.match_replace(cand_left[:, t].rearrange("p a b -> p (a b)"), best[:, t, 0:8],
                                                cand[:, t].rearrange("p a b -> p (a b)"), REMOVED))
                steps.wait()

            def level2_second():
                steps.wait()
                apart()
                for t in range(TT):
                    steps.count(V.max(best[:, t, 8:16], cand_left[:, t].rearrange("p a b -> p (a b)")))
                for t in range(TT):
                    steps.count(V.max_index(pos[:, 0, t, 0:8], best[:, t, 0:8], cand[:, t].rearrange("p a b -> p (a b)")))
                steps.wait()
                apart()
                for t in range(TT):
                    steps.count(V.max_index(pos[:, 0, t, 8:16], best[:, t, 8:16], cand_left[:, t].rearrange("p a b -> p (a b)")))
                steps.wait()

            def decode(p, h):
                if p == 0:
                    steps.count(V.tensor_scalar(pos[:, 1], pos[:, 0], 4, None, ALU.logical_shift_right))
                    steps.count(V.tensor_scalar(pos[:, 2], pos[:, 0], 15, None, ALU.bitwise_and))
                    steps.wait()
                    steps.count(V.tensor_copy(pos_f[:, :], pos[:, 1:3]))
                    steps.count(V.tensor_copy(picked[:, 2, :, bass.ds(h, 1), :].rearrange("p t o k -> p t (o k)"), best[:, :, :]))
                    steps.wait()
                four = [P, TT, TOPK, TOPK]
                steps.after(V.tensor_tensor(match[:, 0].rearrange("p t k a -> p (t k) a"),
                                            pos_f[:, p].rearrange("p t k -> p (t k)").unsqueeze(2).to_broadcast([P, TT * TOPK, TOPK]),
                                            iota[:, 0:TOPK].unsqueeze(1).to_broadcast([P, TT * TOPK, TOPK]), ALU.is_equal))
                steps.after(V.tensor_tensor(match[:, 1], match[:, 0], top_f[:, p].unsqueeze(2).to_broadcast(four), ALU.mult))
                steps.after(V.tensor_reduce(picked[:, p, :, bass.ds(h, 1), :].rearrange("p t o k -> p t (o k)"), match[:, 1],
                                            X_AXIS, ALU.add))

            with dve.Fori(0, PEER_HEADS) as h:
                steps.enter(h, 2 * 24 + 11 + 14 + 4 + 6)
                for t in range(8):
                    split_lo_main(t + LEAD, h * 2)
                    if t in (2, 3):
                        level1(t - 2, h)
                    elif t == 4:
                        level2_first()
                    elif t == 5:
                        level2_second()
                    elif t >= 6:
                        decode(t - 6, h)
                steps.leave(PEER_HEADS)
            flat = [P, TT * PEER_HEADS, TOPK]
            gate = picked[:, 2].rearrange("p t h k -> p (t h) k")
            total = gate_sum[:, 0].rearrange("p t h -> p (t h)")
            inverse = gate_sum[:, 1].rearrange("p t h -> p (t h)")
            steps.after(V.tensor_copy(total, gate[:, :, 0:1].rearrange("p a o -> p (a o)")))
            V.tensor_tensor(gate, gate, total.unsqueeze(2).to_broadcast(flat), ALU.subtract).then_inc(gate_shifted, 1)
            dve.wait_ge(gate_exp, 1)
            steps.after(V.tensor_reduce(total, gate, X_AXIS, ALU.add))
            steps.after(V.reciprocal(inverse, total))
            V.tensor_tensor(gate, gate, inverse.unsqueeze(2).to_broadcast(flat), ALU.mult).then_inc(picks_ready, 1)
            dve.wait_ge(picks_turned, 3)
            for n in range(3):
                steps.count(V.tensor_copy(pick_t[:, n, :], ps[:, 4 + n, :]))
            steps.wait()
            V.memset(lam[:, 6:7], 0.0).then_inc(ids_ready, 1)

            with dve.Fori(0, A2 // 16) as r:
                for t in range(16):
                    split_lo_main(t + LEAD + M_A2, r * 4)
                    par = t % 2
                    dve.wait_ge(gate_mm[par], r * 8 + (t // 2 + CREDIT))
                    for q in range(TOK):
                        col = bass.ds(r * (16 * TOK) + (t * TOK + q), 1)
                        V.tensor_scalar(onehot_i[:, par, q, :], iota[:, :], pick_t[:, 0, col], None, ALU.is_equal)
                        last = V.tensor_scalar(gated_j[:, par, q, :], iota[:, :], pick_t[:, 1, col],
                                               pick_t[:, 2, col], ALU.is_equal, ALU.mult)
                    last.then_inc(onehots_ready[par], 1)

            def w_chunk(e, turn, chunk):
                slot, four = chunk % SLOTS, chunk // SLOTS
                dve.wait_ge(act_in[slot], turn * 64 + 16 * (four + 1))
                dve.wait_ge(gate_in[four % 2], turn * 32 + 16 * (four // 2 + 1))
                V.tensor_tensor(w_tmp[:, e % 2, :].rearrange("p (b t) -> p b t", t=TB),
                                a_in[:, slot, :].rearrange("p (b t) -> p b t", t=TB),
                                g_in[:, four % 2, :, slot, :], ALU.mult).then_inc(w_f32, 1)

            def w_rest(n, buffer, e):
                dve.wait_ge(w_hi_done, n + 1)
                V.tensor_tensor(w_lo[buffer][:, e, :], w_tmp[:, e % 2, :], w_hi[buffer][:, e, :].bitcast(F32),
                                ALU.subtract).then_inc(w_ready, 1)

            for t in range(A3):
                split_lo_main(t + LEAD + M_A3, 0)
                if t >= A3 - GROUP:
                    e = t - (A3 - GROUP)
                    if e >= 2:
                        dve.wait_ge(w_ready, e - 1)
                    w_chunk(e, 0, e)
                    w_rest(e, 0, e)

            dve.wait_ge(acc_clear, 1)

            def second_sweep(g2, last):
                for half in range(2):
                    final_half = last and half == 1
                    for dc in range(KD):
                        t = half * 8 + dc
                        if not (final_half and dc + LEAD >= KD):
                            split_lo_main(t + LEAD + M_V, g2 * 4)
                        n = g2 * 16 + (GROUP + t)
                        if not final_half:
                            dve.wait_ge(w_ready, n - 1)
                            w_chunk(dc, g2, GROUP + t)
                        s = dc % SLOTS
                        dve.wait_ge(unit_done[s], g2 * 4 + (SPLIT_MAIN[s] + (M_V + t) // SLOTS + 1))
                        dve.wait_ge(acc_added[s], g2 * 4 + (t // SLOTS + CREDIT))
                        V.tensor_tensor(acc[:, dc, :], acc[:, dc, :], ps[:, s, :], ALU.add).then_inc(acc_added[s], 1)
                        if not final_half:
                            w_rest(n, 1 - half, dc)

            with dve.Fori(0, GROUPS // 2 - 1) as g2:
                second_sweep(g2, False)
            second_sweep(GROUPS // 2 - 1, True)

            mean_square(4, 36, D)
            dve.wait_ge(rstd_ready, 8)
            for t in range(TT):
                steps.count(V.scalar_tensor_tensor(raw[:, t, :], ps[:, 2 * t:2 * t + 2, :].rearrange("p a n -> p (a n)"),
                                                   rstd[:, 4, t:t + 1], gg2[:, :], ALU.mult, ALU.mult))
                steps.wait()
                V.tensor_tensor(xres[:, t, :], xres[:, t, :], raw[:, t, :], ALU.add).then_inc(x1_ready, 1)

        @block.tensor
        def _(pe):
            mm = nc.tensor.matmul

            def three(dst, w_hi_ap, w_lo_ap, r_hi, r_lo, start, stop):
                mm(dst, w_hi_ap, r_hi, start=start, stop=False)
                mm(dst, w_hi_ap, r_lo, start=False, stop=False)
                return mm(dst, w_lo_ap, r_hi, start=False, stop=stop)

            def unit(slot, split_use, bank, r_hi, r_lo):
                pe.wait_ge(lo_done[slot], split_use + 1)
                for k in range(KD):
                    at = slice(k * P, (k + 1) * P)
                    last = three(ps[:, bank, :], hi[:, slot, at], lo[:, slot, at], r_hi[:, k, :], r_lo[:, k, :],
                                 k == 0, k == KD - 1)
                last.then_inc(unit_done[slot], 1)

            def row_unit(slot, split_use, first_bank, quarter):
                pe.wait_ge(lo_done[slot], split_use + 1)
                for k2 in range(2):
                    k, at = 2 * quarter + k2, slice(k2 * 512, k2 * 512 + 512)
                    for t in range(TT):
                        cols = slice(t * P, (t + 1) * P)
                        last = three(ps[:, first_bank + t, :], ht_hi[:, k, cols], ht_lo[:, k, cols],
                                     hi[:, slot, at], lo[:, slot, at], k == 0, k == KD - 1)
                last.then_inc(unit_done[slot], 1)

            def turn_work(base, source):
                for k in range(KD):
                    if k >= 2:
                        pe.wait_ge(ht_lo_done, base + k - 1)
                    for t in range(TT):
                        last = nc.tensor.transpose(ps[:, k % 2, t * P:(t + 1) * P], work[:, t, k * P:(k + 1) * P], ident[:, :])
                    last.then_inc(turned, 1)

            def mod_columns(acc, bank, col):
                for k in range(KD):
                    last = mm(ps[:, bank, col + k:col + k + 1], acc[:, k * P:(k + 1) * P], ones[:, 0:1], start=True, stop=True)
                return last

            for s in (key_scores, *gate_mm):
                pe.sem_inc(s, CREDIT)
            pe.wait_ge(smalls_loaded, 5 * 16)
            pe.wait_ge(relb_loaded, 16)
            mm(ps[0:N_DIFF, 2, :], relb[:, :], table_sb[:, 0:512], start=True, stop=True).then_inc(bias_mm, 1)
            mm(ps[0:N_DIFF, 3, 0:BIAS_LEN - 512], relb[:, :], table_sb[:, 512:BIAS_LEN], start=True, stop=True).then_inc(bias_mm, 1)
            pe.wait_ge(consts_ready, 6)
            for o in range(2):
                pe.wait_ge(ada_read[SLOTS - 1], CREDIT + 2 * (o + 1))
                last = mod_columns(ada1_acc[:, o, :], 7, o * KD)
            last.then_inc(mod_mm, 1)
            pe.wait_ge(xn_ready, TT)
            turn_work(0, work)
            pe.wait_ge(ht_lo_done, KD)
            pe.wait_ge(wfl_lo_done, 1)
            for k in range(KD):
                last = three(ps[0:8, 6, :], wfl_hi[:, k, :], wfl_lo[:, k, :], ht_hi[:, k, :], ht_lo[:, k, :], k == 0, k == KD - 1)
            last.then_inc(forget_mm, 1)
            pe.wait_ge(hankel_loaded, 16)
            for n in range(2 * SLOTS):
                if n == SLOTS:
                    pe.wait_ge(forget_abs, 1)
                    pe.wait_ge(mod_ready, 1)
                row_unit(n % SLOTS, n // SLOTS, 4 * (n // SLOTS), n % SLOTS)

            def project(u):
                for s in range(2):
                    unit(s, u + SPLIT_QK[s], 5 + s, ht_hi, ht_lo)

            pe.wait_ge(v_ready, 2 * TT)
            project(0)

            def attention(u, fox, last, jobs_before):
                pe.wait_ge(qk_ready, u * 2 + 2)
                pe.wait_ge(exp_done, u * NB + CREDIT)
                if fox:
                    pe.wait_ge(aug_loaded, (u - (N_DIFF - 1)) * 32)
                for b, held in enumerate(SCORE_BANKS):
                    for i, m in held:
                        at, w = SCORE_AT[i, m] % 512, (i + 1) * P
                        dst = ps[:, b, at:at + w]
                        half = slice(64 * m, 64 * m + 64)
                        if (i, m) == (1, 1):
                            pe.wait_ge(other_rows, u + 1)
                        mm(dst, q_t[half, i * P:(i + 1) * P], k_t[half, 0:w], start=True, stop=False)
                        if fox:
                            mm(dst, aug_q[:, m, i * P:(i + 1) * P], aug_k[:, m, 0:w], start=False, stop=False)
                            done = mm(dst[:, i * P:w], ident_bf[:, :], causal[:, :], start=False, stop=True)
                        else:
                            done = mm(dst, flip[:, :], hankel[:, bass.ds(u, 1), (3 - i) * P:T].rearrange("p o k -> p (o k)"),
                                      start=False, stop=True)
                        if (i, m) == (1, 0):
                            done.then_inc(other_rows, 1)
                    done.then_inc(scores_done, 1)
                pe.wait_ge(probs_t_ready, jobs_before + CREDIT)
                if not last:
                    project(u + 1)
                    pe.wait_ge(qk_ready, u * 2 + 4)
                pe.wait_ge(heads_out, u * 4 + CREDIT)
                jobs = [(i, m) for i, _ in BLOCKS for m in range(1 + fox)]

                def turn_probs(n):
                    pe.wait_ge(probs_ready, jobs_before + (n + 1))
                    if n >= 2:
                        pe.wait_ge(probs_t_ready, jobs_before + (n - 1 + CREDIT))
                    i, m = jobs[n]
                    at = SCORE_AT[i, m]
                    for kb in range(i + 1):
                        done = nc.tensor.transpose(ps[:, 5 + n % 2, kb * P:(kb + 1) * P],
                                                   probs[:, at + kb * P:at + (kb + 1) * P], ident[:, :])
                    done.then_inc(probs_turned, 1)

                def times_v(n):
                    pe.wait_ge(probs_t_ready, jobs_before + (n + 1 + CREDIT))
                    i, m = jobs[n]
                    width = 64 if fox else P
                    for kb in range(i + 1):
                        cols = bass.ds(u * P + m * 64, width) if not isinstance(u, int) else slice(u * P + m * 64, u * P + m * 64 + width)
                        done = mm(ps[:, 7, i * P + m * 64:i * P + m * 64 + width], probs_t[:, n % 2, kb * P:(kb + 1) * P],
                                  v_sb[:, kb, cols], start=(kb == 0), stop=(kb == i))
                    done.then_inc(pv_done, 1)

                turn_probs(0)
                for n in range(1, len(jobs)):
                    turn_probs(n)
                    times_v(n - 1)
                times_v(len(jobs) - 1)

            with pe.Fori(0, N_DIFF) as u:
                attention(u, False, False, u * 4)
            with pe.Fori(0, 3) as p:
                attention(p + N_DIFF, True, False, p * 8 + 16)
            attention(7, True, True, 40)

            def spread_gate(n, i):
                for half in range(2):
                    last = mm(ps[:, 4 + 2 * n + half, :], ones[:, :], ada_acc[:, i, half * 512:half * 512 + 512], start=True, stop=True)
                last.then_inc(spread, 1)

            pe.wait_ge(exp_done, HEAD_UNITS * NB + CREDIT)
            for s in range(2, SLOTS):
                pe.wait_ge(ada_read[s], CREDIT + ADA_END[s])
            spread_gate(0, 0)
            pe.wait_ge(heads_out, HEAD_UNITS * TT + CREDIT)
            turn_work(KD, work)
            spread_gate(1, 3)
            pe.wait_ge(ht_lo_done, 2 * KD)
            for n in range(SLOTS):
                row_unit(n, SPLIT_WO[n], 0, n)
            pe.wait_ge(gg_ready, 2)
            for n in range(SLOTS):
                row_unit(n, SPLIT_WO[n] + 1, 4, n)
            pe.wait_ge(y_ready, TT)
            pe.wait_ge(sumsq_done, 24)
            mod_columns(ada_acc[:, 1, :], 2, 0)
            mod_columns(ada_acc[:, 2, :], 2, KD).then_inc(mod_mm, 1)
            pe.wait_ge(xn_ready, 2 * TT)
            turn_work(2 * KD, work)
            pe.wait_ge(ht_lo_done, 3 * KD)

            def main_unit(t, turn, bank, r_hi, r_lo):
                s = t % SLOTS
                unit(s, turn + (SPLIT_MAIN[s] + t // SLOTS), bank, r_hi, r_lo)

            def key_products(p, h):
                pe.wait_ge(query_ready, h * 2 + (p + 1 + CREDIT))
                pe.wait_ge(level1_done[p], h + CREDIT)
                for t in range(TT):
                    last = mm(ps[:, 6 + p, t * P:(t + 1) * P], query[:, p, t * P:(t + 1) * P], keys_sb[:, p, :],
                              start=True, stop=True)
                last.then_inc(key_scores, 1)

            with pe.Fori(0, PEER_HEADS) as h:
                for t in range(8):
                    if t < 2:
                        pe.wait_ge(query_ready, h * 2 + (t + CREDIT))
                        main_unit(t, h * 2, 4 + t, ht_hi, ht_lo)
                        if t == 1:
                            key_products(0, h)
                    else:
                        pe.wait_ge(gelu_done[t % 2], h * 3 + ((t - 2) // 2 + CREDIT))
                        main_unit(t, h * 2, t % 2, ht_hi, ht_lo)
                        if t == 2:
                            key_products(1, h)
            pe.wait_ge(picks_ready, 1)
            for n in range(3):
                for t in range(TT):
                    last = nc.tensor.transpose(ps[:, 4 + n, t * P:(t + 1) * P], picked[:, n, t].rearrange("p h k -> p (h k)"), ident[:, :])
                last.then_inc(picks_turned, 1)
            pe.wait_ge(ids_ready, 1)
            with pe.Fori(0, A2 // 16) as r:
                for t in range(16):
                    par = t % 2
                    pe.wait_ge(gelu_done[par], r * 8 + ((A1 + t) // 2 + CREDIT))
                    main_unit(t + M_A2, r * 4, par, ht_hi, ht_lo)
                    pe.wait_ge(onehots_ready[par], r * 8 + (t // 2 + 1))
                    pe.wait_ge(gates_staged[par], r * 8 + (t // 2 + CREDIT))
                    for q in range(TOK):
                        last = mm(ps[:, 2 + 2 * par + q // 4, (q % 4) * P:(q % 4 + 1) * P], onehot_i[:, par, q, :],
                                  gated_j[:, par, q, :], start=True, stop=True)
                    last.then_inc(gate_mm[par], 1)
            for t in range(A3):
                pe.wait_ge(gelu_done[t % 2], (A1 + A2 + t) // 2 + CREDIT)
                main_unit(t + M_A3, 0, t % 2, ht_hi, ht_lo)

            def second_sweep(g2):
                for half in range(2):
                    for dc in range(KD):
                        t, s = half * 8 + dc, dc % SLOTS
                        pe.wait_ge(acc_added[s], g2 * 4 + (t // SLOTS + CREDIT))
                        pe.wait_ge(lo_done[s], g2 * 4 + (SPLIT_MAIN[s] + (M_V + t) // SLOTS + 1))
                        for e in range(GROUP):
                            if dc == 0:
                                pe.wait_ge(w_ready, g2 * 16 + (half * 8 + e + 1))
                            at = slice(e * P, (e + 1) * P)
                            last = three(ps[:, s, :], hi[:, s, at], lo[:, s, at], w_hi[half][:, e, :], w_lo[half][:, e, :],
                                         e == 0, e == GROUP - 1)
                        last.then_inc(unit_done[s], 1)

            for b in range(2):
                pe.wait_ge(gelu_done[b], CHUNKS // 2 + CREDIT)
            with pe.Fori(0, GROUPS // 2 - 1) as g2:
                second_sweep(g2)
            second_sweep(GROUPS // 2 - 1)
            for s in range(SLOTS):
                pe.wait_ge(acc_added[s], CHUNKS // SLOTS + CREDIT)
            for t in range(TT):
                for k in range(KD):
                    last = nc.tensor.transpose(ps[:, 2 * t + k // 4, (k % 4) * P:(k % 4 + 1) * P], acc[:, k, t * P:(t + 1) * P], ident[:, :])
                last.then_inc(turned, 1)


def kernel(**inputs):
    import numpy as _np
    import concourse.bacc as _bacc
    from concourse import mybir as _mybir
    from concourse.bass_utils import run_bass_kernel_spmd as _run

    a = {k: _np.asarray(v) for k, v in inputs.items()}

    def tiles(w):
        return w.reshape(KD, P, -1, P).transpose(2, 1, 0, 3).reshape(-1, P, D)

    def row_tiles(w):
        return w.reshape(4, 2, P, -1, 512).transpose(3, 0, 2, 1, 4).reshape(-1, P, D)

    def columns(v):
        return v.reshape(-1, P).T

    w_in = a["w_in"][0]
    qk = _np.concatenate([w_in[:, at + (u % 4) * P:at + (u % 4) * P + P] for u in range(HEAD_UNITS)
                          for at in ((0, 512) if u < 4 else (1536, 2048))], axis=1)
    sent = {
        "x": a["x"][0],
        "vecs": _np.concatenate([columns(a["b_ada"][0, :2 * D]), columns(a["g_pre_mix"][0]), columns(a["g_pre_ffn"][0]),
                                 columns(a["c"][0])], axis=1),
        "g_post": _np.concatenate([a["g_post_mix"], a["g_post_ffn"]]),
        "b_ada": a["b_ada"][:, 2 * D:],
        "rows": _np.concatenate([a["g_subln"][0], a["lam_q1"][0], a["lam_k1"][0], a["lam_q2"][0], a["lam_k2"][0]])[None],
        "b_f": a["b_f"].reshape(8, 1),
        "rel_bias": a["rel_bias"],
        "table": bucket_table(),
        "w_fl": w_in[:, 3072:].reshape(KD, P, 8).transpose(1, 0, 2),
        "keys": a["sub_keys"][0].transpose(2, 0, 1),
        "w_ada": a["w_ada"][0].reshape(KD, P, 6, D).transpose(2, 0, 1, 3).reshape(6 * KD, P, D),
        "w_v": _np.concatenate([row_tiles(w_in[:, 1024:1536]), row_tiles(w_in[:, 2560:3072])]),
        "w_qk": tiles(qk),
        "w_o": row_tiles(a["w_o"][0]),
        "w_pq": tiles(a["w_pq"][0]),
        "peer_u": a["peer_u"][0].reshape(P, CHUNKS, KD, P).transpose(1, 3, 2, 0).reshape(CHUNKS, P, D),
        "peer_v": a["peer_v"][0].reshape(P, GROUPS, GROUP, KD, P).transpose(1, 3, 0, 2, 4).reshape(CHUNKS, P, D),
    }
    nc = _bacc.Bacc("TRN2", target_bir_lowering=False, num_devices=1)
    arrays, args = {}, {}
    for name, array in sent.items():
        arrays[f"in_{name}"] = array = _np.ascontiguousarray(array)
        args[name] = nc.dram_tensor(f"in_{name}", array.shape, _mybir.dt.from_np(array.dtype), kind="ExternalInput").ap()
    args["out"] = nc.dram_tensor("out_0", (T, D), _mybir.dt.float32, kind="ExternalOutput").ap()
    build_layer(nc, **args)
    r = _run(nc, [arrays], core_ids=[0])
    return _np.asarray(r.results[0]["out_0"]).reshape(1, T, D)
```

```python
import math
from contextlib import ExitStack

import numpy as np

import concourse.bass as bass
from concourse import mybir

P = 128
T = 512
D = 1024
TT = T // P
KD = D // P
SLOTS = 4
LEAD = 3
HEAD_UNITS = 8
N_DIFF = 4
N_BUCKETS = 32
MAX_DISTANCE = 128
BIAS_LEN = 640
PEER_HEADS = 8
TOPK = 16
CHUNKS = 128
EPS = 1e-6
LAMBDA_INIT = 0.8 - 0.6 * math.exp(0.0)
MASKED = -1e30
REMOVED = -3e38

A1_PER_HEAD = 6
A1 = PEER_HEADS * A1_PER_HEAD
A1_END = 2
A2 = 64
A3 = CHUNKS - A1 - A1_END - A2
M_U = PEER_HEADS * 8
M_A2 = M_U + A1_END
M_A3 = M_A2 + A2
M_V = M_A3 + A3
FIRST_A2 = A1 + A1_END
FIRST_A3 = FIRST_A2 + A2
GROUP = 8
GROUPS = CHUNKS // GROUP
TOK = 8
TB = 64

ADA1_TILES = 16
ADA2_PER_UNIT = 4
RAW_V = [4, 4, 4, 4]
RAW_QK = [6, 6]
RAW_ADA2 = 6
RAW_WO = [14, 14, 22, 22]
RAW_MAIN = [16, 16, 24, 24]
SPLIT_QK = [2, 2]
SPLIT_WO = [10, 10, 2, 2]
SPLIT_MAIN = [12, 12, 4, 4]
ADA_V = 4
ADA_END = [4, 4, 20, 20]

CREDIT = 1

SCORE_BANKS = [[(3, 0)], [(3, 1)], [(2, 0), (0, 0)], [(2, 1), (0, 1)], [(1, 0), (1, 1)]]
SCORE_AT = {(3, 0): 0, (3, 1): 512, (2, 0): 1024, (0, 0): 1408, (2, 1): 1536, (0, 1): 1920, (1, 0): 2048, (1, 1): 2304}
BLOCKS = [(3, 2), (2, 4), (0, 4), (1, 5)]
NB = len(SCORE_BANKS)
TURNS_AHEAD = 3


class Steps:

    def __init__(self, engine, sem):
        self.engine, self.sem, self.turns, self.n = engine, sem, 0, 0

    def after(self, ins):
        self.count(ins)
        self.wait()

    def count(self, ins):
        self.n += 1
        ins.then_inc(self.sem, 1)

    def wait(self):
        self.engine.wait_ge(self.sem, self.turns + self.n)

    def enter(self, turn, steps_per_turn):
        self.first, self.per_turn = self.n, steps_per_turn
        self.turns = turn * steps_per_turn

    def leave(self, turns):
        assert self.n - self.first == self.per_turn, (self.n - self.first, self.per_turn)
        self.turns, self.n = 0, self.first + turns * self.per_turn


def bucket_table():
    table = np.zeros((N_BUCKETS + 1, BIAS_LEN), np.float32)
    exact = N_BUCKETS // 2
    for m in range(BIAS_LEN):
        dist = T - 1 - m
        if dist < 0:
            table[N_BUCKETS, m] = MASKED
        elif dist < exact:
            table[dist, m] = 1.0
        else:
            large = exact + int(math.log(dist / exact) / math.log(MAX_DISTANCE / exact) * (N_BUCKETS - exact))
            table[min(large, N_BUCKETS - 1), m] = 1.0
    return table


def build_layer(nc, x, vecs, rows, g_post, b_ada, b_f, rel_bias, table, w_fl, keys, w_ada, w_v, w_qk, w_o, w_pq, peer_u, peer_v, out):
    F32, F32R, BF16, U32 = mybir.dt.float32, mybir.dt.float32r, mybir.dt.bfloat16, mybir.dt.uint32
    ACT = mybir.ActivationFunctionType
    ALU = mybir.AluOpType
    X_AXIS = mybir.AxisListType.X

    bias_dram = nc.dram_tensor("bias_by_distance", (N_DIFF, BIAS_LEN), F32, kind="Internal").ap()
    cum_dram = nc.dram_tensor("cumulative_forget_parts", (8, 2, T), F32R, kind="Internal").ap()
    act_dram = nc.dram_tensor("expert_activations", (CHUNKS, P, T), F32, kind="Internal").ap()
    gate_dram = nc.dram_tensor("expert_gates", (T // TB, P, P, TB), F32, kind="Internal").ap()

    with ExitStack() as ctx:
        def sb(name, shape, dt, scope=ctx):
            return scope.enter_context(nc.sbuf_tensor(name, shape, dt))

        raw = sb("raw", [P, SLOTS, D], F32)
        hi = sb("hi", [P, SLOTS, D], F32R)
        lo = sb("lo", [P, SLOTS, D], F32R)
        xres = sb("xres", [P, TT, D], F32)
        ident = sb("ident", [P, P], F32)
        ones = sb("ones", [P, P], F32)
        ident_bf = sb("ident_bf", [P, P], BF16)
        causal = sb("causal", [P, P], BF16)
        iota = sb("iota", [P, P], F32)
        keys_sb = sb("keys_sb", [P, 2, P], F32)
        vec = sb("vec", [P, 40], F32)
        row = sb("row", [P, 384], F32)
        gsub = sb("gsub", [P, P], F32)
        silu_c = sb("silu_c", [P, 3, KD], F32)
        shift_cols = sb("shift_cols", [P, 2, KD], F32)
        scale1 = sb("scale1", [P, 2, KD], F32)
        forget_b = sb("forget_b", [8, 1], F32)
        relb = sb("relb", [N_BUCKETS + 1, N_DIFF], F32)
        lam = sb("lam", [P, 8], F32)
        spare = sb("spare", [1, 1], F32)
        lam_prod = sb("lam_prod", [P, 2, 64], F32)
        sumsq = sb("sumsq", [P, 6, TT], F32)
        meansq = sb("meansq", [P, 5, TT], F32)
        rstd = sb("rstd", [P, 5, TT], F32)
        minus_half = sb("minus_half", [P, TT], F32)
        negmax = sb("negmax", [P, 8], F32)
        psums = sb("psums", [P, 8], F32)
        rsums = sb("rsums", [P, 8], F32)
        lrsums = sb("lrsums", [P, 4], F32)
        gg2 = sb("gg2", [P, D], F32)
        with ExitStack() as s:
            aout = sb("aout", [P, 2, T], F32, s)
            pick_t = sb("pick_t", [P, 3, T], F32, s)
        ada_acc = sb("ada_acc", [P, ADA2_PER_UNIT, D], F32)

        with ExitStack() as s:
            ht_hi = sb("ht_hi", [P, KD, T], F32R, s)
            ht_lo = sb("ht_lo", [P, KD, T], F32R, s)
        w_odd_hi = sb("w_odd_hi", [P, GROUP, T], F32R)
        w_odd_lo = sb("w_odd_lo", [P, GROUP, T], F32R)
        with ExitStack() as s:
            work = sb("work", [P, TT, D], F32, s)
        with ExitStack() as s:
            onehot_i = sb("onehot_i", [P, 2, TOK, P], F32, s)
            gated_j = sb("gated_j", [P, 2, TOK, P], F32, s)
        acc = sb("acc", [P, KD, T], F32)
        with ExitStack() as s:
            v_sb = sb("v_sb", [P, TT, D], F32, s)
            probs = sb("probs", [P, 5 * T], F32, s)
            hankel_hi = sb("hankel_hi", [P, N_DIFF, T], F32R, s)
            hankel_lo = sb("hankel_lo", [P, N_DIFF, T], F32R, s)
            flip_r = sb("flip_r", [P, P], F32R, s)
            probs_t = sb("probs_t", [P, TURNS_AHEAD + 1, T], F32, s)
            q_t = sb("q_t", [P, T], F32, s)
            k_t = sb("k_t", [P, T], F32, s)
            aug_q = sb("aug_q", [4, 2, T], F32R, s)
            aug_k = sb("aug_k", [4, 2, T], F32R, s)
            gg1 = sb("gg1", [P, D], F32, s)
            squares = sb("squares", [P, TT, P], F32, s)
            wfl = sb("wfl", [P, KD, 8], F32, s)
            wfl_hi = sb("wfl_hi", [P, KD, 8], F32R, s)
            wfl_lo = sb("wfl_lo", [P, KD, 8], F32R, s)
            flip = squares[:, 0, :]
            cum_parts = probs_t[0:8, 0:2, :]
            forget = probs[0:8, 0:3 * T].rearrange("p (a t) -> p a t", t=T)
            table_sb = v_sb[0:N_BUCKETS + 1, 0, 0:BIAS_LEN]
            bias_row = v_sb[0:N_DIFF, 1, 0:BIAS_LEN]
            ada1_acc = v_sb[:, 2:4, :]
            hankel = v_sb[:, 2:4, :].rearrange("p a (b t) -> p (a b) t", t=T)
        with ExitStack() as s:
            query = sb("query", [P, 2, T], F32, s)
            top_v = sb("top_v", [P, 2, TT, TOPK], F32, s)
            top_i = sb("top_i", [P, 2, TT, TOPK], U32, s)
            top_f = sb("top_f", [P, 2, TT, TOPK], F32, s)
            left = sb("left", [P, TT, P], F32, s)
            cand = sb("cand", [P, TT, TOPK, TOPK], F32, s)
            cand_left = sb("cand_left", [P, TT, TOPK, TOPK], F32, s)
            best = sb("best", [P, TT, TOPK], F32, s)
            pos = sb("pos", [P, 3, TT, TOPK], U32, s)
            pos_f = sb("pos_f", [P, 2, TT, TOPK], F32, s)
            match = sb("match", [P, 2, TT, TOPK, TOPK], F32, s)
            picked = sb("picked", [P, 3, TT, PEER_HEADS, TOPK], F32, s)
            gate_sum = sb("gate_sum", [P, 2, TT, PEER_HEADS], F32, s)
        with ExitStack() as s:
            gates = sb("gates", [P, 2, P, TB], F32, s)
        w_even_hi = sb("w_even_hi", [P, GROUP, T], F32R)
        w_even_lo = sb("w_even_lo", [P, GROUP, T], F32R)
        a_in = sb("a_in", [P, SLOTS, T], F32)
        g_in = sb("g_in", [P, 2, T // TB, SLOTS, TB], F32)
        w_tmp = sb("w_tmp", [P, 2, T], F32)
        w_hi, w_lo = [w_even_hi, w_odd_hi], [w_even_lo, w_odd_lo]

        ps = ctx.enter_context(nc.psum_tensor("ps", [P, 8, 512], F32))

        def sem(name):
            return ctx.enter_context(nc.semaphore(name))

        vec_loaded = sem("vec_loaded")
        smalls_loaded = sem("smalls_loaded")
        row_loaded = sem("row_loaded")
        keys_loaded = sem("keys_loaded")
        relb_loaded = sem("relb_loaded")
        x_loaded = [sem(f"x_loaded{t}") for t in range(TT)]
        raw_full = [sem(f"raw_full{s}") for s in range(SLOTS)]
        ada_read = [sem(f"ada_read{s}") for s in range(SLOTS)]
        hi_done = [sem(f"hi_done{s}") for s in range(SLOTS)]
        lo_done = [sem(f"lo_done{s}") for s in range(SLOTS)]
        unit_done = [sem(f"unit_done{s}") for s in range(SLOTS)]
        consts_ready = sem("consts_ready")
        pool_steps = sem("pool_steps")
        act_steps = sem("act_steps")
        dve_steps = sem("dve_steps")
        silu_exp = sem("silu_exp")
        lam_dots = sem("lam_dots")
        lam_exps = sem("lam_exps")
        ada_acc_clear = sem("ada_acc_clear")
        ada_bias_loaded = sem("ada_bias_loaded")
        mod_mm = sem("mod_mm")
        gains_loaded = sem("gains_loaded")
        bias_mm = sem("bias_mm")
        bias_row_ready = sem("bias_row_ready")
        bias_stored = sem("bias_stored")
        hankel_loaded = sem("hankel_loaded")
        hankel_hi_done = sem("hankel_hi_done")
        mod_ready = sem("mod_ready")
        sumsq_done = sem("sumsq_done")
        meansq_ready = sem("meansq_ready")
        rstd_ready = sem("rstd_ready")
        xn_ready = sem("xn_ready")
        turned = sem("turned")
        ht_f32 = [sem(f"ht_f32_{e}") for e in ("even", "odd")]
        ht_hi_done = sem("ht_hi_done")
        ht_lo_done = sem("ht_lo_done")
        wfl_hi_done = sem("wfl_hi_done")
        wfl_lo_done = sem("wfl_lo_done")
        forget_mm = sem("forget_mm")
        forget_abs = sem("forget_abs")
        forget_ln = sem("forget_ln")
        cum_ready = sem("cum_ready")
        cum_hi_done = sem("cum_hi_done")
        cum_lo_done = sem("cum_lo_done")
        cum_stored = sem("cum_stored")
        aug_loaded = sem("aug_loaded")
        v_ready = sem("v_ready")
        qk_ready = sem("qk_ready")
        scores_done = sem("scores_done")
        other_rows = sem("other_rows")
        max_done = sem("max_done")
        exp_done = sem("exp_done")
        probs_ready = sem("probs_ready")
        probs_turned = sem("probs_turned")
        probs_t_ready = sem("probs_t_ready")
        pv_done = sem("pv_done")
        heads_out = sem("heads_out")
        spread = sem("spread")
        gg_ready = sem("gg_ready")
        y_ready = sem("y_ready")
        x1_ready = sem("x1_ready")
        query_ready = sem("query_ready")
        key_scores = sem("key_scores")
        level1_done = [sem(f"level1_done{p}") for p in range(2)]
        gate_shifted = sem("gate_shifted")
        gate_exp = sem("gate_exp")
        picks_ready = sem("picks_ready")
        picks_turned = sem("picks_turned")
        gelu_done = [sem(f"gelu_done{b}") for b in range(2)]
        act_stored = [sem(f"act_stored{b}") for b in range(2)]
        onehots_ready = [sem(f"onehots_ready{b}") for b in range(2)]
        gate_mm = [sem(f"gate_mm{b}") for b in range(2)]
        gates_staged = [sem(f"gates_staged{b}") for b in range(2)]
        gates_stored = [sem(f"gates_stored{b}") for b in range(2)]
        act_in = [sem(f"act_in{s}") for s in range(SLOTS)]
        gate_in = [sem(f"gate_in{b}") for b in range(2)]
        acc_clear = sem("acc_clear")
        w_f32 = sem("w_f32")
        w_hi_done = sem("w_hi_done")
        w_ready = sem("w_ready")
        acc_added = [sem(f"acc_added{s}") for s in range(SLOTS)]
        out_stored = sem("out_stored")

        block = ctx.enter_context(nc.Block())

        @block.sync
        def _(sp):
            def load(slot, tile, ada_uses, split_uses):
                if ada_uses is not None:
                    sp.wait_ge(ada_read[slot], CREDIT + ada_uses)
                if split_uses is not None:
                    sp.wait_ge(hi_done[slot], split_uses)
                    sp.wait_ge(lo_done[slot], split_uses)
                sp.dma_start(raw[:, slot, :], tile).then_inc(raw_full[slot], 16)

            def tile_of(dram, n):
                return dram[n] if isinstance(n, int) else dram[bass.ds(n, 1), :, :].rearrange("o p n -> (o p) n")

            sp.dma_start(vec[:, :], vecs).then_inc(vec_loaded, 16)
            for s in range(SLOTS):
                load(s, w_ada[s], None, None)
            with sp.Fori(0, ADA1_TILES // SLOTS - 1) as j:
                for s in range(SLOTS):
                    load(s, tile_of(w_ada, (j + 1) * SLOTS + s), j + 1, None)
            for n in range(2 * SLOTS):
                load(n % SLOTS, w_v[n], ADA_V, n // SLOTS if n >= SLOTS else None)

            def load_qk(u):
                for s in range(2):
                    load(s, tile_of(w_qk, u * 2 + s), None, u + SPLIT_QK[s])

            def load_ada2(u):
                for i in range(ADA2_PER_UNIT):
                    s = 2 + i % 2
                    load(s, tile_of(w_ada, u + (ADA1_TILES + i * KD)), u * 2 + (ADA_V + i // 2), SPLIT_QK[0])

            load_qk(0)
            load_qk(1)
            with sp.Fori(0, HEAD_UNITS - 2) as u:
                load_ada2(u)
                load_qk(u + 2)
            with sp.Fori(HEAD_UNITS - 2, HEAD_UNITS) as u:
                load_ada2(u)
            for n in range(2 * SLOTS):
                s = n % SLOTS
                load(s, w_o[n], ADA_END[s], SPLIT_WO[s] + n // SLOTS)
            with sp.Fori(0, PEER_HEADS) as h:
                for t in range(8):
                    s = t % SLOTS
                    tile = tile_of(w_pq, h * 2 + t) if t < 2 else tile_of(peer_u, h * A1_PER_HEAD + (t - 2))
                    load(s, tile, None, h * 2 + (SPLIT_MAIN[s] + t // SLOTS))

            def load_u(j):
                for s in range(SLOTS):
                    load(s, tile_of(peer_u, j * SLOTS + (A1 + s)), None, j + (SPLIT_MAIN[s] + M_U // SLOTS))

            with sp.Fori(0, (CHUNKS - A1) // SLOTS - 1) as j:
                load_u(j)

            def load_act(n, slot, multiplied):
                if multiplied is not None:
                    sp.wait_ge(w_f32, multiplied)
                chunk = slice(n, n + 1) if isinstance(n, int) else bass.ds(n, 1)
                sp.dma_start(a_in[:, slot, :], act_dram[chunk, :, :].rearrange("o p t -> (o p) t")).then_inc(act_in[slot], 16)

            def load_gates(q, buffer, multiplied):
                if multiplied is not None:
                    sp.wait_ge(w_f32, multiplied)
                four = slice(q * SLOTS, q * SLOTS + SLOTS) if isinstance(q, int) else bass.ds(q * SLOTS, SLOTS)
                sp.dma_start(g_in[:, buffer, :, :, :].rearrange("i b j t -> i b (j t)"),
                             gate_dram[:, :, four, :].rearrange("b i j t -> i b (j t)")).then_inc(gate_in[buffer], 16)

            for b in range(2):
                sp.wait_ge(gates_stored[b], CREDIT + 16 * (T // TB // 2))
                sp.wait_ge(act_stored[b], CREDIT + 16 * GROUP // 2)
            load_gates(0, 0, None)
            for n in range(SLOTS):
                load_act(n, n, None)
            load_gates(1, 1, None)
            load_u((CHUNKS - A1) // SLOTS - 1)

            def load_v(j, with_act, with_gates):
                for parity in range(2):
                    for s in range(SLOTS):
                        load(s, tile_of(peer_v, (j * 2 + parity) * SLOTS + s), None, (j * 2 + parity) + (SPLIT_MAIN[s] + M_V // SLOTS))
                        if with_act[parity]:
                            load_act((j * 2 + parity) * SLOTS + (SLOTS + s), s, (j * 2 + parity) * SLOTS + (s + 1))
                    if with_gates[parity]:
                        load_gates((j * 2 + parity) + 2, parity, (j * 2 + parity) * SLOTS + SLOTS)

            both, one, none = (True, True), (True, False), (False, False)
            last_chunks = (A1 + A1_END + A2) // GROUP - 1
            with sp.Fori(0, last_chunks) as j:
                load_v(j, both, both)
            for b in range(2):
                sp.wait_ge(act_stored[b], CREDIT + 16 * CHUNKS // 2)
            with sp.Fori(last_chunks, GROUPS - 1) as j:
                load_v(j, both, both)
            load_v(GROUPS - 1, one, none)

        @block.gpsimd
        def _(pool):
            steps = Steps(pool, pool_steps)
            nc.gpsimd.memset(ident[:, :], 0.0).then_inc(pool_steps, 1)
            nc.gpsimd.memset(flip, 0.0).then_inc(pool_steps, 1)
            nc.gpsimd.memset(causal[:, :], 0.0).then_inc(pool_steps, 1)
            nc.gpsimd.memset(ident_bf[:, :], 0.0).then_inc(pool_steps, 1)
            nc.gpsimd.memset(ones[:, :], 1.0).then_inc(consts_ready, 1)
            nc.gpsimd.memset(aug_q[:, :, :].bitcast(F32), -1.0).then_inc(pool_steps, 1)
            nc.gpsimd.memset(aug_k[:, :, :].bitcast(F32), 1.0).then_inc(pool_steps, 1)
            nc.gpsimd.memset(relb[:, :], 1.0).then_inc(pool_steps, 1)
            nc.gpsimd.memset(minus_half[:, :], -0.5).then_inc(pool_steps, 1)
            steps.n = 8
            steps.wait()
            pool.dma_start(relb[0:N_BUCKETS, :], rel_bias).then_inc(relb_loaded, 16)
            for m in (ident, ident_bf):
                nc.gpsimd.affine_select(out=m[:, :], in_=m[:, :], compare_op=ALU.not_equal, fill=1.0, base=0,
                                        pattern=[[-1, P]], channel_multiplier=1).then_inc(consts_ready, 1)
            nc.gpsimd.affine_select(out=flip, in_=flip, compare_op=ALU.not_equal, fill=1.0,
                                    base=-(P - 1), pattern=[[1, P]], channel_multiplier=1).then_inc(consts_ready, 1)
            nc.gpsimd.affine_select(out=causal[:, :], in_=causal[:, :], compare_op=ALU.is_ge, fill=MASKED, base=0,
                                    pattern=[[-1, P]], channel_multiplier=1).then_inc(consts_ready, 1)
            nc.gpsimd.iota(iota[:, :], pattern=[[1, P]], base=0, channel_multiplier=0,
                           allow_small_or_imprecise_dtypes=True).then_inc(consts_ready, 1)
            nc.gpsimd.memset(ada_acc[:, :, :], 0.0).then_inc(ada_acc_clear, 1)
            pool.wait_ge(ada_acc_clear, 1)
            pool.dma_start(ada_acc[0:1, :, :], b_ada.rearrange("o (i n) -> o i n", n=D)).then_inc(ada_bias_loaded, 16)

            def root(n, norm):
                pool.wait_ge(meansq_ready, n)
                nc.gpsimd.tensor_tensor(rstd[:, norm, :], meansq[:, norm, :], minus_half[:, :],
                                        ALU.pow).then_inc(rstd_ready, 1)

            pool.wait_ge(bias_row_ready, 1)
            pool.dma_start(bias_dram, bias_row).then_inc(bias_stored, 16)
            root(1, 0)
            pool.wait_ge(bias_stored, 16)
            pool.wait_ge(mod_ready, 1)
            pool.dma_start(hankel,
                           bass.AP(bias_dram.tensor, 0, [[1, P], [BIAS_LEN, N_DIFF], [1, T]])).then_inc(hankel_loaded, 16)
            for n, gg in enumerate((gg1, gg2)):
                pool.dma_start(gg[:, :], bass.AP(g_post.tensor, n * D, [[0, P], [1, D]])).then_inc(gains_loaded, 16)
            pool.wait_ge(cum_lo_done, 1)
            pool.dma_start(cum_dram, cum_parts.bitcast(F32R)).then_inc(cum_stored, 16)
            pool.wait_ge(cum_stored, 16)

            def load_aug(pair, scores_before):
                if scores_before is not None:
                    pool.wait_ge(scores_done, scores_before)
                    pool.wait_ge(aug_loaded, pair * 32)
                first = pair * 2
                at = slice(0, 2) if isinstance(pair, int) else bass.ds(first, 2)
                pool.dma_start(aug_q[0:2, :, :], cum_dram[at, :, :].rearrange("h p t -> p h t")).then_inc(aug_loaded, 16)
                pool.dma_start(aug_k[2:4, :, :], cum_dram[at, :, :].rearrange("h p t -> p h t")).then_inc(aug_loaded, 16)

            load_aug(0, None)
            with pool.Fori(0, N_DIFF) as u:
                root(u + 2, 1)
            with pool.Fori(0, 3) as p:
                load_aug(p + 1, p * NB + (N_DIFF + 1) * NB)
            root(6, 2)
            root(7, 3)

            for b in range(2):
                pool.wait_ge(gate_mm[b], CREDIT + A2 // 2)
            nc.gpsimd.memset(acc[:, :, :], 0.0).then_inc(acc_clear, 1)
            root(8, 4)

        @block.scalar
        def _(act):
            steps = Steps(act, act_steps)

            def split_hi(slot, raw_use, split_use):
                act.wait_ge(raw_full[slot], raw_use * 16 + 16)
                act.wait_ge(unit_done[slot], split_use)
                nc.scalar.activation(hi[:, slot, :], raw[:, slot, :], ACT.Copy).then_inc(hi_done[slot], 1)

            def split_hi_main(t, turn):
                s, k = t % SLOTS, t // SLOTS
                split_hi(s, turn + (RAW_MAIN[s] + k), turn + (SPLIT_MAIN[s] + k))

            for s in (exp_done, probs_t_ready, query_ready, *gelu_done, *gates_staged, *act_stored, *gates_stored):
                act.sem_inc(s, CREDIT)
            act.dma_start(table_sb, table).then_inc(smalls_loaded, 16)
            act.dma_start(forget_b[:, :], b_f).then_inc(smalls_loaded, 16)
            act.dma_start(wfl[:, :, :], w_fl).then_inc(smalls_loaded, 16)
            for t in range(TT):
                act.dma_start(xres[:, t, :], x[t * P:(t + 1) * P, :]).then_inc(x_loaded[t], 16)
            act.wait_ge(vec_loaded, 16)
            nc.scalar.activation(silu_c[:, 0, :], vec[:, 32:40], ACT.Exp, scale=-1.0).then_inc(silu_exp, 1)
            for t in range(TT):
                act.wait_ge(x_loaded[t], 16)
                nc.scalar.activation(work[:, t, :], xres[:, t, :], ACT.Square,
                                     accum_out=sumsq[:, 0, t:t + 1]).then_inc(sumsq_done, 1)
            act.wait_ge(smalls_loaded, 3 * 16)
            nc.scalar.activation(wfl_hi[:, :, :], wfl[:, :, :], ACT.Copy).then_inc(wfl_hi_done, 1)

            def affine_ht(base, which):
                for k in range(KD):
                    if k % 2 == 0:
                        act.wait_ge(turned, base + k + 1)
                        if k >= 4 or base:
                            act.wait_ge(ht_lo_done, base + max(k - 3, 0))
                        act.activation(probs[:, (k % 4) * T:(k % 4 + 1) * T], ps[:, k % 4, :], ACT.Identity,
                                       bias=shift_cols[:, which, k:k + 1], scale=scale1[:, which, k:k + 1]).then_inc(ht_f32[0], 1)
                    act.wait_ge(ht_f32[k % 2], which * (KD // 2) + k // 2 + 1)
                    act.activation(ht_hi[:, k, :], probs[:, (k % 4) * T:(k % 4 + 1) * T], ACT.Copy).then_inc(ht_hi_done, 1)

            split_hi(0, RAW_V[0], 0)
            act.dma_start(row[:, :], bass.AP(rows.tensor, 0, [[0, P], [1, 384]])).then_inc(row_loaded, 16)
            act.dma_start(keys_sb[:, :, :], keys).then_inc(keys_loaded, 16)
            act.wait_ge(mod_ready, 1)
            affine_ht(0, 0)
            for n in range(1, SLOTS):
                split_hi(n, RAW_V[n], 0)
            act.activation(flip_r[:, :], flip, ACT.Copy).then_inc(hankel_hi_done, 1)
            act.wait_ge(hankel_loaded, 16)
            act.activation(hankel_hi[:, :, :], hankel, ACT.Copy).then_inc(hankel_hi_done, 1)
            act.wait_ge(forget_abs, 1)
            nc.scalar.activation(forget[:, 2, :], forget[:, 1, :], ACT.Exp).then_inc(forget_ln, 1)
            act.wait_ge(forget_ln, 1)
            nc.scalar.activation(forget[:, 1, :], forget[:, 2, :], ACT.Ln, bias=1.0).then_inc(forget_ln, 1)
            for n in range(SLOTS):
                split_hi(n, RAW_V[n] + 1, 1)
            act.wait_ge(lam_dots, 1)
            nc.scalar.activation(lam[:, 2:4], lam[:, 0:2], ACT.Exp).then_inc(lam_exps, 1)
            act.wait_ge(cum_ready, 1)
            act.activation(cum_parts[:, 0, :].bitcast(F32R), forget[:, 1, :], ACT.Copy).then_inc(cum_hi_done, 1)
            act.wait_ge(unit_done[3], 1)
            for t in range(2):
                act.activation(v_sb[:, t, 0:512], ps[:, t, :], ACT.Copy).then_inc(v_ready, 1)
            for s in range(2):
                split_hi(s, RAW_QK[s], SPLIT_QK[s])
            act.wait_ge(unit_done[3], 2)
            for t in range(2):
                act.activation(v_sb[:, t, 512:1024], ps[:, 4 + t, :], ACT.Copy).then_inc(v_ready, 1)

            def evacuate_qk(u):
                act.wait_ge(unit_done[0], u + (SPLIT_QK[0] + 1))
                act.activation(q_t[:, :], ps[:, 5, :], ACT.Copy, scale=0.125).then_inc(qk_ready, 1)
                act.wait_ge(unit_done[1], u + (SPLIT_QK[1] + 1))
                act.activation(k_t[:, :], ps[:, 6, :], ACT.Copy).then_inc(qk_ready, 1)

            evacuate_qk(0)
            act.wait_ge(cum_stored, 16)

            def attention(u, fox, last, jobs_before):
                if not last:
                    for s in range(2):
                        split_hi(s, u + (RAW_QK[s] + 1), u + (SPLIT_QK[s] + 1))
                for b, held in enumerate(SCORE_BANKS):
                    act.wait_ge(max_done, u * NB + (b + 1))
                    for i, m in held:
                        at, w, c = SCORE_AT[i, m], (i + 1) * P, 2 * i + m
                        last_exp = act.activation(probs[:, at:at + w], ps[:, b, at % 512:at % 512 + w], ACT.Exp,
                                                  bias=negmax[:, c:c + 1], accum_out=psums[:, c:c + 1])
                    last_exp.then_inc(exp_done, 1)
                if not last:
                    evacuate_qk(u + 1)
                jobs = [(i, m) for i, _ in BLOCKS for m in range(1 + fox)]
                for n, (i, m) in enumerate(jobs):
                    act.wait_ge(probs_turned, jobs_before + (n + 1))
                    b = n % (TURNS_AHEAD + 1)
                    if n > TURNS_AHEAD:
                        act.wait_ge(pv_done, jobs_before + (n - TURNS_AHEAD))
                    w = (i + 1) * P
                    act.activation(probs_t[:, b, 0:w], ps[:, b, 0:w], ACT.Copy).then_inc(probs_t_ready, 1)
                if not fox:
                    act.wait_ge(pv_done, jobs_before + 4)
                    act.wait_ge(heads_out, u * 4 + CREDIT)
                    for i in range(TT):
                        act.activation(squares[:, i, :], ps[:, 7, i * P:(i + 1) * P], ACT.Square,
                                       accum_out=sumsq[:, 1, i:i + 1]).then_inc(sumsq_done, 1)

            with act.Fori(0, N_DIFF) as u:
                attention(u, False, False, u * 4)
            with act.Fori(0, 3) as p:
                attention(p + N_DIFF, True, False, p * 8 + 16)
            attention(7, True, True, 16 + 24)

            for s in range(SLOTS):
                split_hi(s, RAW_WO[s], SPLIT_WO[s])
            for k in range(KD):
                act.wait_ge(turned, KD + k + 1)
                act.activation(ht_hi[:, k, :], ps[:, k % 4, :], ACT.Copy).then_inc(ht_hi_done, 1)
            for s in range(SLOTS):
                split_hi(s, RAW_WO[s] + 1, SPLIT_WO[s] + 1)
            act.wait_ge(unit_done[3], SPLIT_WO[3] + 1)
            for t in range(TT):
                act.activation(v_sb[:, t, 0:512], ps[:, t, :], ACT.Square, accum_out=sumsq[:, 2, t:t + 1]).then_inc(sumsq_done, 1)
            for t in range(LEAD):
                split_hi_main(t, 0)
            act.wait_ge(unit_done[3], SPLIT_WO[3] + 2)
            for t in range(TT):
                act.activation(v_sb[:, t, 512:1024], ps[:, 4 + t, :], ACT.Square,
                               accum_out=sumsq[:, 5, t:t + 1]).then_inc(sumsq_done, 1)
            for t in range(TT):
                act.wait_ge(x1_ready, t + 1)
                act.activation(v_sb[:, t, :], xres[:, t, :], ACT.Square,
                               accum_out=sumsq[:, 3, t:t + 1]).then_inc(sumsq_done, 1)
            act.wait_ge(mod_ready, 2)
            affine_ht(2 * KD, 1)

            def gelu(parity, uses, chunk):
                act.wait_ge(act_stored[parity], uses * 16 + CREDIT)
                act.activation(aout[:, parity, :], ps[:, parity, :], ACT.Gelu_apprx_tanh).then_inc(gelu_done[parity], 1)
                act.wait_ge(gelu_done[parity], uses + (CREDIT + 1))
                act.dma_start(act_dram[bass.ds(chunk, 1), :, :].rearrange("o p t -> (o p) t") if not isinstance(chunk, int)
                              else act_dram[chunk], aout[:, parity, :]).then_inc(act_stored[parity], 16)

            def unit_end(t, turn):
                s = t % SLOTS
                act.wait_ge(unit_done[s], turn + (SPLIT_MAIN[s] + t // SLOTS + 1))

            with act.Fori(0, PEER_HEADS) as h:
                for t in range(8):
                    split_hi_main(t + LEAD, h * 2)
                    unit_end(t, h * 2)
                    if t < 2:
                        act.wait_ge(key_scores, h * 2 + CREDIT)
                        act.activation(query[:, t, :], ps[:, 4 + t, :], ACT.Copy).then_inc(query_ready, 1)
                    else:
                        gelu(t % 2, h * 3 + (t - 2) // 2, h * A1_PER_HEAD + (t - 2))
            for t in range(A1_END):
                split_hi_main(t + LEAD + M_U, 0)
                if t == 0:
                    act.wait_ge(gate_shifted, 1)
                    act.activation(picked[:, 2], picked[:, 2], ACT.Exp).then_inc(gate_exp, 1)
                unit_end(t + M_U, 0)
                gelu(t % 2, (A1 + t) // 2, A1 + t)

            def gates_out(t, r):
                half, par = t // 8, t % 2
                act.wait_ge(gate_mm[par], r * 8 + (t // 2 + 1 + CREDIT))
                if t % 8 == 0:
                    act.wait_ge(gates_stored[half], r * 16 + CREDIT)
                at = (t % 8) * TOK
                act.activation(gates[:, half, :, at:at + TOK],
                               ps[:, 2 + 2 * par:4 + 2 * par, :].rearrange("p a (q j) -> p j (a q)", j=P),
                               ACT.Copy).then_inc(gates_staged[par], 1)
                if t % 8 == 7:
                    for b in range(2):
                        act.wait_ge(gates_staged[b], r * 8 + (4 * (half + 1) + CREDIT))
                    act.dma_start(gate_dram[bass.ds(r * 2 + half, 1), :, :, :].rearrange("o i j t -> (o i) j t"),
                                  gates[:, half, :, :]).then_inc(gates_stored[half], 16)

            with act.Fori(0, A2 // 16) as r:
                for t in range(16):
                    split_hi_main(t + LEAD + M_A2, r * 4)
                    unit_end(t + M_A2, r * 4)
                    gelu(t % 2, r * 8 + (FIRST_A2 + t) // 2, r * 16 + (FIRST_A2 + t))
                    if t:
                        gates_out(t - 1, r)
                gates_out(15, r)

            def split_w_hi(n, buffer, e, turn, tile):
                act.wait_ge(w_f32, n + 1)
                if e == 0:
                    unit_end(tile, turn)
                act.activation(w_hi[buffer][:, e, :], w_tmp[:, e % 2, :], ACT.Copy).then_inc(w_hi_done, 1)

            for t in range(A3):
                split_hi_main(t + LEAD + M_A3, 0)
                unit_end(t + M_A3, 0)
                gelu(t % 2, (FIRST_A3 + t) // 2, FIRST_A3 + t)
                if t >= A3 - GROUP:
                    e = t - (A3 - GROUP)
                    split_w_hi(e, 0, e, 0, M_A2 - 1)

            def second_sweep(g2, last):
                for half in range(2):
                    for dc in range(KD):
                        t = half * 8 + dc
                        final_half = last and half == 1
                        if not (final_half and dc + LEAD >= KD):
                            split_hi_main(t + LEAD + M_V, g2 * 4)
                        if not final_half:
                            split_w_hi(g2 * 16 + (GROUP + t), 1 - half, dc, g2 * 4, M_V + half * 8 - 1)

            with act.Fori(0, GROUPS // 2 - 1) as g2:
                second_sweep(g2, False)
            second_sweep(GROUPS // 2 - 1, True)

            for t in range(TT):
                act.wait_ge(turned, 3 * KD + t + 1)
                act.activation(g_in[:, t // 2, (t % 2) * 4:(t % 2) * 4 + 4].rearrange("p b s t -> p (b s t)"),
                               ps[:, 2 * t:2 * t + 2, :].rearrange("p a n -> p (a n)"), ACT.Square,
                               accum_out=sumsq[:, 4, t:t + 1]).then_inc(sumsq_done, 1)
            for t in range(TT):
                act.wait_ge(x1_ready, TT + t + 1)
                act.dma_start(out[t * P:(t + 1) * P, :], xres[:, t, :]).then_inc(out_stored, 16)
            act.wait_ge(out_stored, 16 * TT)

        @block.vector
        def _(dve):
            steps = Steps(dve, dve_steps)
            V = nc.vector

            def split_lo(slot, split_use):
                dve.wait_ge(hi_done[slot], split_use + 1)
                V.tensor_tensor(lo[:, slot, :], raw[:, slot, :], hi[:, slot, :].bitcast(F32),
                                ALU.subtract).then_inc(lo_done[slot], 1)

            def split_lo_main(t, turn):
                s = t % SLOTS
                split_lo(s, turn + (SPLIT_MAIN[s] + t // SLOTS))

            def mean_square(norm, n, width):
                dve.wait_ge(sumsq_done, n)
                V.tensor_scalar(meansq[:, norm, :], sumsq[:, norm, :], 1.0 / width, EPS, ALU.mult, ALU.add).then_inc(meansq_ready, 1)

            for s in (heads_out, *level1_done, *acc_added, *ada_read):
                dve.sem_inc(s, CREDIT)
            dve.wait_ge(silu_exp, 1)
            steps.after(V.tensor_scalar(silu_c[:, 1, :], silu_c[:, 0, :], 1.0, None, ALU.add))
            steps.after(V.reciprocal(silu_c[:, 2, :], silu_c[:, 1, :]))
            steps.after(V.tensor_tensor(silu_c[:, 0, :], silu_c[:, 2, :], vec[:, 32:40], ALU.mult))

            def ada1(o, first, end):
                for k in range(first, end):
                    n = o * KD + k
                    slot, use = n % SLOTS, n // SLOTS
                    dve.wait_ge(raw_full[slot], use * 16 + 16)
                    if k == 0:
                        done = V.tensor_scalar(ada1_acc[:, o, :], raw[:, slot, :], silu_c[:, 0, k:k + 1], None, ALU.mult)
                    else:
                        dve.wait_ge(ada_read[(n - 1) % SLOTS], CREDIT + (n - 1) // SLOTS + 1)
                        done = V.scalar_tensor_tensor(ada1_acc[:, o, :], raw[:, slot, :], silu_c[:, 0, k:k + 1],
                                                      ada1_acc[:, o, :], ALU.mult, ALU.add)
                    done.then_inc(ada_read[slot], 1)

            ada1(0, 0, KD)
            dve.wait_ge(smalls_loaded, 3 * 16)
            dve.wait_ge(bias_mm, 2)
            steps.after(V.tensor_copy(bias_row[:, 0:512], ps[0:N_DIFF, 2, :]))
            V.tensor_copy(bias_row[:, 512:BIAS_LEN], ps[0:N_DIFF, 3, 0:BIAS_LEN - 512]).then_inc(bias_row_ready, 1)
            mean_square(0, 4, D)
            dve.wait_ge(wfl_hi_done, 1)
            V.tensor_tensor(wfl_lo[:, :, :], wfl[:, :, :], wfl_hi[:, :, :].bitcast(F32), ALU.subtract).then_inc(wfl_lo_done, 1)
            ada1(1, 0, KD // 2)

            def normalise(n, norm):
                dve.wait_ge(rstd_ready, n)
                for t in range(TT):
                    V.tensor_scalar(work[:, t, :], xres[:, t, :], rstd[:, norm, t:t + 1], None, ALU.mult).then_inc(xn_ready, 1)

            normalise(1, 0)
            ada1(1, KD // 2, KD)
            dve.wait_ge(mod_mm, 1)
            steps.count(V.tensor_tensor(shift_cols[:, 0, :], ps[:, 7, 0:8], vec[:, 0:8], ALU.add))
            steps.after(V.tensor_tensor(scale1[:, 1, :], ps[:, 7, 8:16], vec[:, 8:16], ALU.add))
            V.scalar_tensor_tensor(scale1[:, 0, :], scale1[:, 1, :], 1.0, vec[:, 16:24], ALU.add, ALU.mult).then_inc(mod_ready, 1)

            def affine_remainder(base, which):
                for k in range(KD):
                    odd = k + 1
                    if odd < KD and odd % 2:
                        dve.wait_ge(turned, base + odd + 1)
                        if odd >= 4 or base:
                            dve.wait_ge(ht_lo_done, base + max(odd - 3, 0))
                        V.tensor_scalar(probs[:, (odd % 4) * T:(odd % 4 + 1) * T], ps[:, odd % 4, :], scale1[:, which, odd:odd + 1],
                                        shift_cols[:, which, odd:odd + 1], ALU.mult, ALU.add).then_inc(ht_f32[1], 1)
                    dve.wait_ge(ht_hi_done, base + k + 1)
                    V.tensor_tensor(ht_lo[:, k, :], probs[:, (k % 4) * T:(k % 4 + 1) * T], ht_hi[:, k, :].bitcast(F32),
                                    ALU.subtract).then_inc(ht_lo_done, 1)

            def ht_remainder(base, source):
                for k in range(KD):
                    dve.wait_ge(ht_hi_done, base + k + 1)
                    V.tensor_tensor(ht_lo[:, k, :], source(k), ht_hi[:, k, :].bitcast(F32), ALU.subtract).then_inc(ht_lo_done, 1)

            split_lo(0, 0)
            dve.wait_ge(mod_ready, 1)
            affine_remainder(0, 0)
            for n in range(1, SLOTS):
                split_lo(n, 0)
            dve.wait_ge(forget_mm, 1)
            steps.after(V.tensor_scalar(forget[:, 0, :], ps[0:8, 6, :], forget_b[:, 0:1], None, ALU.add))
            steps.after(V.tensor_scalar(forget[:, 2, :], forget[:, 0, :], -1.0, None, ALU.mult))
            V.tensor_tensor(forget[:, 1, :], forget[:, 0, :], forget[:, 2, :], ALU.min).then_inc(forget_abs, 1)
            dve.wait_ge(forget_ln, 2)
            steps.after(V.scalar_tensor_tensor(forget[:, 2, :], forget[:, 0, :], 0.0, forget[:, 1, :], ALU.min, ALU.subtract))
            steps.after(V.memset(forget[:, 0, :], 1.0))
            V.tensor_tensor_scan(forget[:, 1, :], forget[:, 0, :], forget[:, 2, :], 0.0, ALU.mult, ALU.add).then_inc(cum_ready, 1)
            dve.wait_ge(row_loaded, 16)
            for m in range(2):
                steps.count(V.tensor_tensor(lam_prod[:, m, :], row[:, 128 + 128 * m:192 + 128 * m],
                                            row[:, 192 + 128 * m:256 + 128 * m], ALU.mult))
            steps.wait()
            V.tensor_reduce(lam[:, 0:2], lam_prod[:, :, :], X_AXIS, ALU.add).then_inc(lam_dots, 1)
            dve.wait_ge(hankel_hi_done, 2)
            steps.after(V.tensor_tensor(hankel_lo[:, :, :], hankel, hankel_hi[:, :, :].bitcast(F32), ALU.subtract))
            for n in range(SLOTS):
                split_lo(n, 1)
            dve.wait_ge(lam_exps, 1)
            steps.after(V.tensor_tensor(lam[:, 4:5], lam[:, 3:4], lam[:, 2:3], ALU.subtract))
            steps.after(V.tensor_scalar(lam[:, 5:6], lam[:, 4:5], -LAMBDA_INIT, None, ALU.add))
            steps.count(V.tensor_scalar(gsub[:, :], row[:, 0:P], 1.0 - LAMBDA_INIT, None, ALU.mult))
            dve.wait_ge(cum_hi_done, 1)
            V.tensor_tensor(cum_parts[:, 1, :].bitcast(F32R), forget[:, 1, :], cum_parts[:, 0, :], ALU.subtract).then_inc(cum_lo_done, 1)
            dve.wait_ge(unit_done[3], 1)
            for t in range(2, TT):
                V.tensor_copy(v_sb[:, t, 0:512], ps[:, t, :]).then_inc(v_ready, 1)
            for s in range(2):
                split_lo(s, SPLIT_QK[s])
            dve.wait_ge(unit_done[3], 2)
            for t in range(2, TT):
                V.tensor_copy(v_sb[:, t, 512:1024], ps[:, 4 + t, :]).then_inc(v_ready, 1)

            def ada2(u, i):
                s = 2 + i % 2
                dve.wait_ge(raw_full[s], u * 32 + 16 * (RAW_ADA2 + i // 2 + 1))
                dve.wait_ge(ada_read[s], u * 2 + (CREDIT + ADA_V + i // 2))
                V.scalar_tensor_tensor(ada_acc[:, i, :], raw[:, s, :], silu_c[:, 0, u:u + 1] if isinstance(u, int) else silu_c[:, 0, bass.ds(u, 1)],
                                       ada_acc[:, i, :], ALU.mult, ALU.add).then_inc(ada_read[s], 1)

            dve.wait_ge(ada_bias_loaded, 16)

            def attention(u, fox, last):
                if not last:
                    for s in range(2):
                        split_lo(s, u + (SPLIT_QK[s] + 1))
                for b, held in enumerate(SCORE_BANKS):
                    dve.wait_ge(scores_done, u * NB + (b + 1))
                    if b == NB - 1:
                        V.tensor_reduce(negmax[:, 2:4], ps[:, b, :].rearrange("p (m k) -> p m k", m=2), X_AXIS, ALU.max,
                                        negate=True).then_inc(max_done, 1)
                        continue
                    for i, m in held:
                        at, w, c = SCORE_AT[i, m] % 512, (i + 1) * P, 2 * i + m
                        last_max = V.tensor_reduce(negmax[:, c:c + 1], ps[:, b, at:at + w], X_AXIS, ALU.max, negate=True)
                    last_max.then_inc(max_done, 1)
                for i in range(2):
                    ada2(u, i)
                for i, banks in BLOCKS:
                    w, c = (i + 1) * P, 2 * i
                    p0 = probs[:, SCORE_AT[i, 0]:SCORE_AT[i, 0] + w]
                    p1 = probs[:, SCORE_AT[i, 1]:SCORE_AT[i, 1] + w]
                    dve.wait_ge(exp_done, u * NB + (banks + CREDIT))
                    steps.after(V.reciprocal(rsums[:, c:c + 2], psums[:, c:c + 2]))
                    if fox:
                        V.tensor_scalar(p0, p0, rsums[:, c:c + 1], None, ALU.mult).then_inc(probs_ready, 1)
                        V.tensor_scalar(p1, p1, rsums[:, c + 1:c + 2], None, ALU.mult).then_inc(probs_ready, 1)
                    else:
                        steps.after(V.tensor_tensor(lrsums[:, i:i + 1], rsums[:, c + 1:c + 2], lam[:, 5:6], ALU.mult))
                        steps.after(V.tensor_scalar(p1, p1, lrsums[:, i:i + 1], None, ALU.mult))
                        V.scalar_tensor_tensor(p0, p0, rsums[:, c:c + 1], p1, ALU.mult, ALU.add).then_inc(probs_ready, 1)
                for i in range(2, ADA2_PER_UNIT):
                    ada2(u, i)

            with dve.Fori(0, N_DIFF) as u:
                steps.enter(u, 4 * 3)
                attention(u, False, False)
                mean_square(1, u * 4 + 8, P)
                dve.wait_ge(rstd_ready, u + 2)
                for i in range(TT):
                    V.scalar_tensor_tensor(work[:, i, bass.ds(u * P, P)], ps[:, 7, i * P:(i + 1) * P], rstd[:, 1, i:i + 1],
                                           gsub[:, :], ALU.mult, ALU.mult).then_inc(heads_out, 1)
                steps.leave(N_DIFF)

            def fox_out(u, jobs):
                dve.wait_ge(pv_done, jobs)
                for i in range(TT):
                    V.tensor_copy(work[:, i, bass.ds(u * P, P)], ps[:, 7, i * P:(i + 1) * P]).then_inc(heads_out, 1)

            with dve.Fori(0, 3) as p:
                steps.enter(p, 4)
                attention(p + N_DIFF, True, False)
                fox_out(p + N_DIFF, p * 8 + 24)
                steps.leave(3)
            attention(7, True, True)
            fox_out(7, 48)

            for s in range(SLOTS):
                split_lo(s, SPLIT_WO[s])
            ht_remainder(KD, lambda k: ps[:, k % 4, :])
            dve.wait_ge(gains_loaded, 32)
            for n, gg in enumerate((gg1, gg2)):
                dve.wait_ge(spread, n + 1)
                V.tensor_tensor(gg[:, :], gg[:, :], ps[:, 4 + 2 * n:6 + 2 * n, :].rearrange("p a n -> p (a n)"),
                                ALU.mult).then_inc(gg_ready, 1)
            for s in range(SLOTS):
                split_lo(s, SPLIT_WO[s] + 1)
            dve.wait_ge(gg_ready, 2)

            def gain_columns(half, t):
                dve.wait_ge(sumsq_done, 20 + 4 * half + t + 1)
                V.tensor_tensor(work[:, t, half * 512:half * 512 + 512], ps[:, 4 * half + t, :],
                                gg1[:, half * 512:half * 512 + 512], ALU.mult).then_inc(y_ready, 1)

            for t in range(TT):
                gain_columns(0, t)
            for t in range(LEAD):
                split_lo_main(t, 0)
            for t in range(TT - 1):
                gain_columns(1, t)
            dve.wait_ge(sumsq_done, 28)
            steps.after(V.tensor_tensor(sumsq[:, 2, :], sumsq[:, 2, :], sumsq[:, 5, :], ALU.add))
            mean_square(2, 28, D)
            gain_columns(1, TT - 1)
            dve.wait_ge(rstd_ready, 6)
            dve.wait_ge(y_ready, 2 * TT)
            for t in range(TT):
                V.scalar_tensor_tensor(xres[:, t, :], work[:, t, :], rstd[:, 2, t:t + 1], xres[:, t, :],
                                       ALU.mult, ALU.add).then_inc(x1_ready, 1)
            dve.wait_ge(mod_mm, 2)
            steps.count(V.tensor_copy(shift_cols[:, 1, :], ps[:, 2, 0:8]))
            V.scalar_tensor_tensor(scale1[:, 1, :], ps[:, 2, 8:16], 1.0, vec[:, 24:32], ALU.add, ALU.mult).then_inc(mod_ready, 1)
            mean_square(3, 32, D)
            normalise(7, 3)
            dve.wait_ge(mod_ready, 2)
            affine_remainder(2 * KD, 1)

            def apart():
                steps.count(V.memset(spare[0:1, 0:1], 0.0))

            def level1(p, h):
                s = lambda t: ps[:, 6 + p, t * P:(t + 1) * P]
                dve.wait_ge(key_scores, h * 2 + (p + 1 + CREDIT))
                apart()
                for t in range(TT):
                    steps.count(V.max(top_v[:, p, t, 0:8], s(t)))
                steps.wait()
                apart()
                for t in range(TT):
                    steps.count(V.match_replace(left[:, t, :], top_v[:, p, t, 0:8], s(t), REMOVED))
                for t in range(TT):
                    steps.count(V.max_index(top_i[:, p, t, 0:8], top_v[:, p, t, 0:8], s(t)))
                steps.wait()
                apart()
                for t in range(TT):
                    steps.count(V.max(top_v[:, p, t, 8:16], left[:, t, :]))
                steps.wait()
                apart()
                for t in range(TT):
                    steps.count(V.max_index(top_i[:, p, t, 8:16], top_v[:, p, t, 8:16], left[:, t, :]))
                steps.wait()
                V.tensor_copy(top_f[:, p], top_i[:, p]).then_inc(level1_done[p], 1)

            def level2_first():
                b = top_v[:, 1].unsqueeze(2).to_broadcast([P, TT, TOPK, TOPK])
                steps.count(V.tensor_tensor(cand[:, :, :, :], top_v[:, 0].unsqueeze(3).to_broadcast([P, TT, TOPK, TOPK]), b, ALU.add))
                steps.wait()
                apart()
                for t in range(TT):
                    steps.count(V.max(best[:, t, 0:8], cand[:, t].rearrange("p a b -> p (a b)")))
                steps.wait()
                apart()
                for t in range(TT):
                    steps.count(V.match_replace(cand_left[:, t].rearrange("p a b -> p (a b)"), best[:, t, 0:8],
                                                cand[:, t].rearrange("p a b -> p (a b)"), REMOVED))
                steps.wait()

            def level2_second():
                steps.wait()
                apart()
                for t in range(TT):
                    steps.count(V.max(best[:, t, 8:16], cand_left[:, t].rearrange("p a b -> p (a b)")))
                for t in range(TT):
                    steps.count(V.max_index(pos[:, 0, t, 0:8], best[:, t, 0:8], cand[:, t].rearrange("p a b -> p (a b)")))
                steps.wait()
                apart()
                for t in range(TT):
                    steps.count(V.max_index(pos[:, 0, t, 8:16], best[:, t, 8:16], cand_left[:, t].rearrange("p a b -> p (a b)")))
                steps.wait()

            def decode(p, h):
                if p == 0:
                    steps.count(V.tensor_scalar(pos[:, 1], pos[:, 0], 4, None, ALU.logical_shift_right))
                    steps.count(V.tensor_scalar(pos[:, 2], pos[:, 0], 15, None, ALU.bitwise_and))
                    steps.wait()
                    steps.count(V.tensor_copy(pos_f[:, :], pos[:, 1:3]))
                    steps.count(V.tensor_copy(picked[:, 2, :, bass.ds(h, 1), :].rearrange("p t o k -> p t (o k)"), best[:, :, :]))
                    steps.wait()
                four = [P, TT, TOPK, TOPK]
                steps.after(V.tensor_tensor(match[:, 0].rearrange("p t k a -> p (t k) a"),
                                            pos_f[:, p].rearrange("p t k -> p (t k)").unsqueeze(2).to_broadcast([P, TT * TOPK, TOPK]),
                                            iota[:, 0:TOPK].unsqueeze(1).to_broadcast([P, TT * TOPK, TOPK]), ALU.is_equal))
                steps.after(V.tensor_tensor(match[:, 1], match[:, 0], top_f[:, p].unsqueeze(2).to_broadcast(four), ALU.mult))
                steps.after(V.tensor_reduce(picked[:, p, :, bass.ds(h, 1), :].rearrange("p t o k -> p t (o k)"), match[:, 1],
                                            X_AXIS, ALU.add))

            with dve.Fori(0, PEER_HEADS) as h:
                steps.enter(h, 2 * 24 + 11 + 14 + 4 + 6)
                for t in range(8):
                    split_lo_main(t + LEAD, h * 2)
                    if t in (2, 3):
                        level1(t - 2, h)
                    elif t == 4:
                        level2_first()
                    elif t == 5:
                        level2_second()
                    elif t >= 6:
                        decode(t - 6, h)
                steps.leave(PEER_HEADS)
            split_lo_main(LEAD + M_U, 0)
            flat = [P, TT * PEER_HEADS, TOPK]
            gate = picked[:, 2].rearrange("p t h k -> p (t h) k")
            total = gate_sum[:, 0].rearrange("p t h -> p (t h)")
            inverse = gate_sum[:, 1].rearrange("p t h -> p (t h)")
            steps.after(V.tensor_copy(total, gate[:, :, 0:1].rearrange("p a o -> p (a o)")))
            V.tensor_tensor(gate, gate, total.unsqueeze(2).to_broadcast(flat), ALU.subtract).then_inc(gate_shifted, 1)
            dve.wait_ge(gate_exp, 1)
            steps.after(V.tensor_reduce(total, gate, X_AXIS, ALU.add))
            steps.after(V.reciprocal(inverse, total))
            V.tensor_tensor(gate, gate, inverse.unsqueeze(2).to_broadcast(flat), ALU.mult).then_inc(picks_ready, 1)
            split_lo_main(LEAD + M_U + 1, 0)
            dve.wait_ge(picks_turned, 3)
            for n in range(3):
                steps.count(V.tensor_copy(pick_t[:, n, :], ps[:, 4 + n, :]))
            steps.wait()

            with dve.Fori(0, A2 // 16) as r:
                for t in range(16):
                    par = t % 2
                    dve.wait_ge(gate_mm[par], r * 8 + (t // 2 + CREDIT))
                    for q in range(TOK):
                        col = bass.ds(r * (16 * TOK) + (t * TOK + q), 1)
                        V.tensor_scalar(onehot_i[:, par, q, :], iota[:, :], pick_t[:, 0, col], None, ALU.is_equal)
                        last = V.tensor_scalar(gated_j[:, par, q, :], iota[:, :], pick_t[:, 1, col],
                                               pick_t[:, 2, col], ALU.is_equal, ALU.mult)
                    last.then_inc(onehots_ready[par], 1)
                    split_lo_main(t + LEAD + M_A2, r * 4)

            def w_chunk(e, turn, chunk):
                slot, four = chunk % SLOTS, chunk // SLOTS
                dve.wait_ge(act_in[slot], turn * 64 + 16 * (four + 1))
                dve.wait_ge(gate_in[four % 2], turn * 32 + 16 * (four // 2 + 1))
                V.tensor_tensor(w_tmp[:, e % 2, :].rearrange("p (b t) -> p b t", t=TB),
                                a_in[:, slot, :].rearrange("p (b t) -> p b t", t=TB),
                                g_in[:, four % 2, :, slot, :], ALU.mult).then_inc(w_f32, 1)

            def w_rest(n, buffer, e):
                dve.wait_ge(w_hi_done, n + 1)
                V.tensor_tensor(w_lo[buffer][:, e, :], w_tmp[:, e % 2, :], w_hi[buffer][:, e, :].bitcast(F32),
                                ALU.subtract).then_inc(w_ready, 1)

            for t in range(A3):
                split_lo_main(t + LEAD + M_A3, 0)
                if t >= A3 - GROUP:
                    e = t - (A3 - GROUP)
                    if e >= 2:
                        dve.wait_ge(w_ready, e - 1)
                    w_chunk(e, 0, e)
                    w_rest(e, 0, e)

            dve.wait_ge(acc_clear, 1)

            def second_sweep(g2, last):
                for half in range(2):
                    final_half = last and half == 1
                    for dc in range(KD):
                        t = half * 8 + dc
                        if not (final_half and dc + LEAD >= KD):
                            split_lo_main(t + LEAD + M_V, g2 * 4)
                        n = g2 * 16 + (GROUP + t)
                        if not final_half:
                            dve.wait_ge(w_ready, n - 1)
                            w_chunk(dc, g2, GROUP + t)
                        s = dc % SLOTS
                        dve.wait_ge(unit_done[s], g2 * 4 + (SPLIT_MAIN[s] + (M_V + t) // SLOTS + 1))
                        dve.wait_ge(acc_added[s], g2 * 4 + (t // SLOTS + CREDIT))
                        V.tensor_tensor(acc[:, dc, :], acc[:, dc, :], ps[:, s, :], ALU.add).then_inc(acc_added[s], 1)
                        if not final_half:
                            w_rest(n, 1 - half, dc)

            with dve.Fori(0, GROUPS // 2 - 1) as g2:
                second_sweep(g2, False)
            second_sweep(GROUPS // 2 - 1, True)

            def gain_rows(t):
                dve.wait_ge(sumsq_done, 32 + t + 1)
                steps.count(V.tensor_tensor(raw[:, t, :], ps[:, 2 * t:2 * t + 2, :].rearrange("p a n -> p (a n)"), gg2[:, :], ALU.mult))

            for t in range(TT - 1):
                gain_rows(t)
            mean_square(4, 36, D)
            gain_rows(TT - 1)
            dve.wait_ge(rstd_ready, 8)
            steps.wait()
            for t in range(TT):
                V.scalar_tensor_tensor(xres[:, t, :], raw[:, t, :], rstd[:, 4, t:t + 1], xres[:, t, :],
                                       ALU.mult, ALU.add).then_inc(x1_ready, 1)

        @block.tensor
        def _(pe):
            mm = nc.tensor.matmul

            def three(dst, w_hi_ap, w_lo_ap, r_hi, r_lo, start, stop):
                mm(dst, w_hi_ap, r_hi, start=start, stop=False)
                mm(dst, w_hi_ap, r_lo, start=False, stop=False)
                return mm(dst, w_lo_ap, r_hi, start=False, stop=stop)

            def unit(slot, split_use, bank, r_hi, r_lo, chunks_ready=None):
                pe.wait_ge(lo_done[slot], split_use + 1)
                for k in range(KD):
                    if chunks_ready is not None:
                        pe.wait_ge(ht_lo_done, chunks_ready + k + 1)
                    at = slice(k * P, (k + 1) * P)
                    last = three(ps[:, bank, :], hi[:, slot, at], lo[:, slot, at], r_hi[:, k, :], r_lo[:, k, :],
                                 k == 0, k == KD - 1)
                last.then_inc(unit_done[slot], 1)

            def row_unit(slot, split_use, first_bank, quarter):
                pe.wait_ge(lo_done[slot], split_use + 1)
                for k2 in range(2):
                    k, at = 2 * quarter + k2, slice(k2 * 512, k2 * 512 + 512)
                    for t in range(TT):
                        cols = slice(t * P, (t + 1) * P)
                        last = three(ps[:, first_bank + t, :], ht_hi[:, k, cols], ht_lo[:, k, cols],
                                     hi[:, slot, at], lo[:, slot, at], k == 0, k == KD - 1)
                last.then_inc(unit_done[slot], 1)

            def turn_work(base, which, first, end):
                for k in range(first, end):
                    if k >= 4 and which is not None:
                        pe.wait_ge(ht_f32[k % 2], which * (KD // 2) + (k - 4) // 2 + 1)
                    elif k >= 4:
                        pe.wait_ge(ht_lo_done, base + k - 3)
                    for t in range(TT):
                        last = nc.tensor.transpose(ps[:, k % 4, t * P:(t + 1) * P], work[:, t, k * P:(k + 1) * P], ident[:, :])
                    last.then_inc(turned, 1)

            def mod_columns(acc, bank, col):
                for k in range(KD):
                    last = mm(ps[:, bank, col + k:col + k + 1], acc[:, k * P:(k + 1) * P], ones[:, 0:1], start=True, stop=True)
                return last

            for s in (key_scores, *gate_mm):
                pe.sem_inc(s, CREDIT)
            pe.wait_ge(smalls_loaded, 3 * 16)
            pe.wait_ge(relb_loaded, 16)
            mm(ps[0:N_DIFF, 2, :], relb[:, :], table_sb[:, 0:512], start=True, stop=True).then_inc(bias_mm, 1)
            mm(ps[0:N_DIFF, 3, 0:BIAS_LEN - 512], relb[:, :], table_sb[:, 512:BIAS_LEN], start=True, stop=True).then_inc(bias_mm, 1)
            pe.wait_ge(consts_ready, 6)
            pe.wait_ge(ada_read[SLOTS - 1], CREDIT + 2)
            mod_columns(ada1_acc[:, 0, :], 7, 0)
            pe.wait_ge(bias_row_ready, 1)
            pe.wait_ge(xn_ready, TT)
            turn_work(0, 0, 0, 4)
            pe.wait_ge(ada_read[SLOTS - 1], CREDIT + 4)
            mod_columns(ada1_acc[:, 1, :], 7, KD).then_inc(mod_mm, 1)
            turn_work(0, 0, 4, KD)
            pe.wait_ge(wfl_lo_done, 1)
            for k in range(KD):
                pe.wait_ge(ht_lo_done, k + 1)
                last = three(ps[0:8, 6, :], wfl_hi[:, k, :], wfl_lo[:, k, :], ht_hi[:, k, :], ht_lo[:, k, :], k == 0, k == KD - 1)
            last.then_inc(forget_mm, 1)
            pe.wait_ge(hankel_loaded, 16)
            for n in range(2 * SLOTS):
                if n == SLOTS:
                    pe.wait_ge(forget_abs, 1)
                    pe.wait_ge(mod_ready, 1)
                row_unit(n % SLOTS, n // SLOTS, 4 * (n // SLOTS), n % SLOTS)

            def project(u):
                for s in range(2):
                    unit(s, u + SPLIT_QK[s], 5 + s, ht_hi, ht_lo)

            pe.wait_ge(v_ready, 2 * TT)
            project(0)

            def attention(u, fox, last, jobs_before):
                pe.wait_ge(qk_ready, u * 2 + 2)
                pe.wait_ge(exp_done, u * NB + CREDIT)
                if fox:
                    pe.wait_ge(aug_loaded, (u - (N_DIFF - 1)) * 32)
                for b, held in enumerate(SCORE_BANKS):
                    for i, m in held:
                        at, w = SCORE_AT[i, m] % 512, (i + 1) * P
                        dst = ps[:, b, at:at + w]
                        half = slice(64 * m, 64 * m + 64)
                        if (i, m) == (1, 1):
                            pe.wait_ge(other_rows, u + 1)
                        mm(dst, q_t[half, i * P:(i + 1) * P], k_t[half, 0:w], start=True, stop=False)
                        if fox:
                            mm(dst, aug_q[:, m, i * P:(i + 1) * P], aug_k[:, m, 0:w], start=False, stop=False)
                            done = mm(dst[:, i * P:w], ident_bf[:, :], causal[:, :], start=False, stop=True)
                        else:
                            for part in (hankel_hi, hankel_lo):
                                done = mm(dst, flip_r[:, :], part[:, bass.ds(u, 1), (3 - i) * P:T].rearrange("p o k -> p (o k)"),
                                          start=False, stop=(part is hankel_lo))
                        if (i, m) == (1, 0):
                            done.then_inc(other_rows, 1)
                    done.then_inc(scores_done, 1)
                if not last:
                    project(u + 1)
                pe.wait_ge(heads_out, u * 4 + CREDIT)
                jobs = [(i, m) for i, _ in BLOCKS for m in range(1 + fox)]

                def turn_probs(n):
                    pe.wait_ge(probs_ready, jobs_before + (n + 1))
                    if n > TURNS_AHEAD:
                        pe.wait_ge(probs_t_ready, jobs_before + (n - TURNS_AHEAD + CREDIT))
                    i, m = jobs[n]
                    at = SCORE_AT[i, m]
                    for kb in range(i + 1):
                        done = nc.tensor.transpose(ps[:, n % (TURNS_AHEAD + 1), kb * P:(kb + 1) * P],
                                                   probs[:, at + kb * P:at + (kb + 1) * P], ident[:, :])
                    done.then_inc(probs_turned, 1)

                def times_v(n):
                    pe.wait_ge(probs_t_ready, jobs_before + (n + 1 + CREDIT))
                    i, m = jobs[n]
                    width = 64 if fox else P
                    for kb in range(i + 1):
                        cols = bass.ds(u * P + m * 64, width) if not isinstance(u, int) else slice(u * P + m * 64, u * P + m * 64 + width)
                        done = mm(ps[:, 7, i * P + m * 64:i * P + m * 64 + width], probs_t[:, n % (TURNS_AHEAD + 1), kb * P:(kb + 1) * P],
                                  v_sb[:, kb, cols], start=(kb == 0), stop=(kb == i))
                    done.then_inc(pv_done, 1)

                for n in range(len(jobs) + TURNS_AHEAD):
                    if n >= TURNS_AHEAD:
                        times_v(n - TURNS_AHEAD)
                    if n < len(jobs):
                        turn_probs(n)

            with pe.Fori(0, N_DIFF) as u:
                attention(u, False, False, u * 4)
            with pe.Fori(0, 3) as p:
                attention(p + N_DIFF, True, False, p * 8 + 16)
            attention(7, True, True, 40)

            def spread_gate(n, i):
                for half in range(2):
                    last = mm(ps[:, 4 + 2 * n + half, :], ones[:, :], ada_acc[:, i, half * 512:half * 512 + 512], start=True, stop=True)
                last.then_inc(spread, 1)

            pe.wait_ge(exp_done, HEAD_UNITS * NB + CREDIT)
            for s in range(2, SLOTS):
                pe.wait_ge(ada_read[s], CREDIT + ADA_END[s])
            spread_gate(0, 0)
            pe.wait_ge(heads_out, HEAD_UNITS * TT + CREDIT)
            turn_work(KD, None, 0, KD)
            spread_gate(1, 3)
            pe.wait_ge(ht_lo_done, 2 * KD)
            for n in range(SLOTS):
                row_unit(n, SPLIT_WO[n], 0, n)
            pe.wait_ge(gg_ready, 2)
            for n in range(SLOTS):
                row_unit(n, SPLIT_WO[n] + 1, 4, n)
            pe.wait_ge(y_ready, TT)
            mod_columns(ada_acc[:, 1, :], 2, 0)
            mod_columns(ada_acc[:, 2, :], 2, KD).then_inc(mod_mm, 1)
            pe.wait_ge(xn_ready, 2 * TT)
            pe.wait_ge(mod_ready, 2)
            turn_work(2 * KD, 1, 0, KD)

            pe.wait_ge(keys_loaded, 16)

            def main_unit(t, turn, bank, r_hi, r_lo, chunks_ready=None):
                s = t % SLOTS
                unit(s, turn + (SPLIT_MAIN[s] + t // SLOTS), bank, r_hi, r_lo, chunks_ready)

            def key_products(p, h):
                pe.wait_ge(query_ready, h * 2 + (p + 1 + CREDIT))
                pe.wait_ge(level1_done[p], h + CREDIT)
                for t in range(TT):
                    last = mm(ps[:, 6 + p, t * P:(t + 1) * P], query[:, p, t * P:(t + 1) * P], keys_sb[:, p, :],
                              start=True, stop=True)
                last.then_inc(key_scores, 1)

            with pe.Fori(0, PEER_HEADS) as h:
                for t in range(8):
                    if t < 2:
                        pe.wait_ge(query_ready, h * 2 + CREDIT)
                        main_unit(t, h * 2, 4 + t, ht_hi, ht_lo, 2 * KD if t == 0 else None)
                        if t == 1:
                            key_products(0, h)
                    else:
                        pe.wait_ge(gelu_done[t % 2], h * 3 + ((t - 2) // 2 + CREDIT))
                        main_unit(t, h * 2, t % 2, ht_hi, ht_lo)
                        if t == 2:
                            key_products(1, h)
            for t in range(A1_END):
                pe.wait_ge(gelu_done[t % 2], (A1 + t) // 2 + CREDIT)
                main_unit(t + M_U, 0, t % 2, ht_hi, ht_lo)
            pe.wait_ge(picks_ready, 1)
            for n in range(3):
                for t in range(TT):
                    last = nc.tensor.transpose(ps[:, 4 + n, t * P:(t + 1) * P], picked[:, n, t].rearrange("p h k -> p (h k)"), ident[:, :])
                last.then_inc(picks_turned, 1)
            with pe.Fori(0, A2 // 16) as r:
                for t in range(16):
                    par = t % 2
                    pe.wait_ge(gelu_done[par], r * 8 + ((FIRST_A2 + t) // 2 + CREDIT))
                    main_unit(t + M_A2, r * 4, par, ht_hi, ht_lo)
                    pe.wait_ge(onehots_ready[par], r * 8 + (t // 2 + 1))
                    pe.wait_ge(gates_staged[par], r * 8 + (t // 2 + CREDIT))
                    for q in range(TOK):
                        last = mm(ps[:, 2 + 2 * par + q // 4, (q % 4) * P:(q % 4 + 1) * P], onehot_i[:, par, q, :],
                                  gated_j[:, par, q, :], start=True, stop=True)
                    last.then_inc(gate_mm[par], 1)
            for t in range(A3):
                pe.wait_ge(gelu_done[t % 2], (FIRST_A3 + t) // 2 + CREDIT)
                main_unit(t + M_A3, 0, t % 2, ht_hi, ht_lo)

            def second_sweep(g2):
                for half in range(2):
                    for dc in range(KD):
                        t, s = half * 8 + dc, dc % SLOTS
                        pe.wait_ge(acc_added[s], g2 * 4 + (t // SLOTS + CREDIT))
                        pe.wait_ge(lo_done[s], g2 * 4 + (SPLIT_MAIN[s] + (M_V + t) // SLOTS + 1))
                        for e in range(GROUP):
                            if dc == 0:
                                pe.wait_ge(w_ready, g2 * 16 + (half * 8 + e + 1))
                            at = slice(e * P, (e + 1) * P)
                            last = three(ps[:, s, :], hi[:, s, at], lo[:, s, at], w_hi[half][:, e, :], w_lo[half][:, e, :],
                                         e == 0, e == GROUP - 1)
                        last.then_inc(unit_done[s], 1)

            for b in range(2):
                pe.wait_ge(gelu_done[b], CHUNKS // 2 + CREDIT)
            with pe.Fori(0, GROUPS // 2 - 1) as g2:
                second_sweep(g2)
            second_sweep(GROUPS // 2 - 1)
            for s in range(SLOTS):
                pe.wait_ge(acc_added[s], CHUNKS // SLOTS + CREDIT)
            for t in range(TT):
                for k in range(KD):
                    last = nc.tensor.transpose(ps[:, 2 * t + k // 4, (k % 4) * P:(k % 4 + 1) * P], acc[:, k, t * P:(t + 1) * P], ident[:, :])
                last.then_inc(turned, 1)


def kernel(**inputs):
    import numpy as _np
    import concourse.bacc as _bacc
    from concourse import mybir as _mybir
    from concourse.bass_utils import run_bass_kernel_spmd as _run

    a = {k: _np.asarray(v) for k, v in inputs.items()}

    def tiles(w):
        return w.reshape(KD, P, -1, P).transpose(2, 1, 0, 3).reshape(-1, P, D)

    def row_tiles(w):
        return w.reshape(4, 2, P, -1, 512).transpose(3, 0, 2, 1, 4).reshape(-1, P, D)

    def columns(v):
        return v.reshape(-1, P).T

    w_in = a["w_in"][0]
    qk = _np.concatenate([w_in[:, at + (u % 4) * P:at + (u % 4) * P + P] for u in range(HEAD_UNITS)
                          for at in ((0, 512) if u < 4 else (1536, 2048))], axis=1)
    sent = {
        "x": a["x"][0],
        "vecs": _np.concatenate([columns(a["b_ada"][0, :2 * D]), columns(a["g_pre_mix"][0]), columns(a["g_pre_ffn"][0]),
                                 columns(a["c"][0])], axis=1),
        "g_post": _np.concatenate([a["g_post_mix"], a["g_post_ffn"]]),
        "b_ada": a["b_ada"][:, 2 * D:],
        "rows": _np.concatenate([a["g_subln"][0], a["lam_q1"][0], a["lam_k1"][0], a["lam_q2"][0], a["lam_k2"][0]])[None],
        "b_f": a["b_f"].reshape(8, 1),
        "rel_bias": a["rel_bias"],
        "table": bucket_table(),
        "w_fl": w_in[:, 3072:].reshape(KD, P, 8).transpose(1, 0, 2),
        "keys": a["sub_keys"][0].transpose(2, 0, 1),
        "w_ada": a["w_ada"][0].reshape(KD, P, 6, D).transpose(2, 0, 1, 3).reshape(6 * KD, P, D),
        "w_v": _np.concatenate([row_tiles(w_in[:, 1024:1536]), row_tiles(w_in[:, 2560:3072])]),
        "w_qk": tiles(qk),
        "w_o": row_tiles(a["w_o"][0]),
        "w_pq": tiles(a["w_pq"][0]),
        "peer_u": a["peer_u"][0].reshape(P, CHUNKS, KD, P).transpose(1, 3, 2, 0).reshape(CHUNKS, P, D),
        "peer_v": a["peer_v"][0].reshape(P, GROUPS, GROUP, KD, P).transpose(1, 3, 0, 2, 4).reshape(CHUNKS, P, D),
    }
    nc = _bacc.Bacc("TRN2", target_bir_lowering=False, num_devices=1)
    arrays, args = {}, {}
    for name, array in sent.items():
        arrays[f"in_{name}"] = array = _np.ascontiguousarray(array)
        args[name] = nc.dram_tensor(f"in_{name}", array.shape, _mybir.dt.from_np(array.dtype), kind="ExternalInput").ap()
    args["out"] = nc.dram_tensor("out_0", (T, D), _mybir.dt.float32, kind="ExternalOutput").ap()
    build_layer(nc, **args)
    r = _run(nc, [arrays], core_ids=[0])
    return _np.asarray(r.results[0]["out_0"]).reshape(1, T, D)
```
